# Optimizing a Trainium2 kernel written in Bass

```python
import math
import jax, jax.numpy as jnp
from jax import lax
import numpy as np

D_MODEL = 2048
BATCH = 1
SEQ = 256
DEPTH = 1

BRANCH_WIDTH = 1024
N_BRANCH = 3
GLA_HEADS = 4
GLA_DK = 128
GLA_DV = 256
GLA_RANK = 16
GLA_TAU = 16.0
GLA_CHUNK = 64
SWA_Q_HEADS = 16
SWA_KV_HEADS = 2
SWA_HEAD_DIM = 64
SWA_WINDOW = 128
MOBA_HEADS = 8
MOBA_HEAD_DIM = 128
MOBA_BLOCK = 256
MOBA_TOPK = 3
MOBA_Q_CHUNK = 16
DEEPNORM_ALPHA = (2 * DEPTH) ** 0.25
DEEPNORM_BETA = (8 * DEPTH) ** -0.25
LN_EPS = 1e-5
RMS_EPS = 1e-6

IN_SPLITS = (
    GLA_HEADS * GLA_DK, GLA_HEADS * GLA_DK, GLA_HEADS * GLA_DV, GLA_RANK, BRANCH_WIDTH,
    SWA_Q_HEADS * SWA_HEAD_DIM, SWA_KV_HEADS * SWA_HEAD_DIM, SWA_KV_HEADS * SWA_HEAD_DIM, BRANCH_WIDTH,
    MOBA_HEADS * MOBA_HEAD_DIM, MOBA_HEADS * MOBA_HEAD_DIM, MOBA_HEADS * MOBA_HEAD_DIM, BRANCH_WIDTH,
    N_BRANCH * D_MODEL,
)
VALUE_SEGMENTS = (2, 7, 11)
D_IN = sum(IN_SPLITS)


def _layer_norm(h, g, b):
    h32 = h.astype(jnp.float32)
    mu = h32.mean(-1, keepdims=True)
    var = jnp.square(h32 - mu).mean(-1, keepdims=True)
    return ((h32 - mu) * lax.rsqrt(var + LN_EPS) * g.astype(jnp.float32) + b.astype(jnp.float32)).astype(h.dtype)

def _gla_branch(q, k, v, g, norm_g):
    B, S, H, dk = q.shape
    dv = v.shape[-1]
    nc = S // GLA_CHUNK

    def to_chunks(t):
        t = t.astype(jnp.float32).reshape(B, nc, GLA_CHUNK, H, t.shape[-1])
        return t.transpose(1, 0, 3, 2, 4)

    qc, kc, vc, gc = to_chunks(q * (dk ** -0.5)), to_chunks(k), to_chunks(v), to_chunks(g)
    causal = jnp.tril(jnp.ones((GLA_CHUNK, GLA_CHUNK), dtype=bool))

    def step(state, inp):
        qi, ki, vi, gi = inp
        b = jnp.cumsum(gi, axis=2)
        b_last = b[:, :, -1:, :]
        o_inter = jnp.einsum('bhcd,bhde->bhce', qi * jnp.exp(b), state)
        diff = b[:, :, :, None, :] - b[:, :, None, :, :]
        decay = jnp.exp(jnp.where(causal[None, None, :, :, None], diff, -jnp.inf))
        attn = jnp.einsum('bhid,bhjd,bhijd->bhij', qi, ki, decay)
        o = o_inter + jnp.einsum('bhij,bhje->bhie', attn, vi)
        new_state = (jnp.exp(b_last[:, :, 0, :])[..., None] * state
                     + jnp.einsum('bhcd,bhce->bhde', ki * jnp.exp(b_last - b), vi))
        return new_state, o

    state0 = jnp.zeros((B, H, dk, dv), jnp.float32)
    _, o = lax.scan(step, state0, (qc, kc, vc, gc))
    o = o.transpose(1, 0, 3, 2, 4).reshape(B, S, H, dv)
    o = o * lax.rsqrt(jnp.mean(jnp.square(o), axis=-1, keepdims=True) + RMS_EPS) * norm_g.astype(jnp.float32)
    return o.reshape(B, S, H * dv).astype(v.dtype)

def _swa_branch(q, k, v, sinks):
    B, S, Hq, hd = q.shape
    Hkv = k.shape[2]
    G = Hq // Hkv
    W = SWA_WINDOW
    nb = S // W
    qb = q.reshape(B, nb, W, Hkv, G, hd)
    kb = k.reshape(B, nb, W, Hkv, hd)
    vb = v.reshape(B, nb, W, Hkv, hd)
    shift = lambda t: jnp.concatenate([jnp.zeros_like(t[:, :1]), t[:, :-1]], axis=1)
    kk = jnp.concatenate([shift(kb), kb], axis=2)
    vv = jnp.concatenate([shift(vb), vb], axis=2)
    s = jnp.einsum('bnqhgd,bnkhd->bnhgqk', qb, kk).astype(jnp.float32) * (hd ** -0.5)
    qpos = jnp.arange(W)[:, None] + W
    kpos = jnp.arange(2 * W)[None, :]
    rel = qpos - kpos
    band = (rel >= 0) & (rel < W)
    mask = band[None] & ((jnp.arange(nb) > 0)[:, None, None] | (kpos >= W)[None])
    s = jnp.where(mask[None, :, None, None], s, -jnp.inf)
    sink = jnp.broadcast_to(sinks.astype(jnp.float32).reshape(1, 1, Hkv, G, 1, 1), s.shape[:-1] + (1,))
    p = jax.nn.softmax(jnp.concatenate([s, sink], axis=-1), axis=-1)[..., :-1]
    o = jnp.einsum('bnhgqk,bnkhd->bnqhgd', p.astype(v.dtype), vv)
    return o.reshape(B, S, Hq * hd)

def _moba_branch(q, k, v):
    B, S, H, hd = q.shape
    BLK = MOBA_BLOCK
    QC = MOBA_Q_CHUNK
    nblk = -(-S // BLK)
    Sp = nblk * BLK
    padw = ((0, 0), (0, Sp - S), (0, 0), (0, 0))
    q, k, v = [jnp.pad(t, padw).transpose(0, 2, 1, 3) for t in (q, k, v)]
    kb = k.reshape(B, H, nblk, BLK, hd)
    vb = v.reshape(B, H, nblk, BLK, hd)
    kmean = kb.astype(jnp.float32).mean(axis=3)
    gate = jnp.einsum('bhsd,bhnd->bhsn', q.astype(jnp.float32), kmean)
    qblk = jnp.arange(Sp) // BLK
    past = jnp.arange(nblk)[None, :] < qblk[:, None]
    gate = jnp.where(past, gate, -jnp.inf)
    topk = min(MOBA_TOPK, nblk)
    _, idx = lax.top_k(gate, topk)
    valid = idx < qblk[:, None]
    nc = Sp // QC
    scale = hd ** -0.5

    def chunks(t):
        return jnp.moveaxis(t.reshape((B, H, nc, QC) + t.shape[3:]), 2, 0)

    bi = jnp.arange(B)[:, None, None, None]
    hi = jnp.arange(H)[None, :, None, None]

    def one_chunk(inp):
        qc, idxc, validc, c = inp
        kg = kb[bi, hi, idxc]
        vg = vb[bi, hi, idxc]
        s_sel = jnp.einsum('bhqd,bhqkjd->bhqkj', qc, kg).astype(jnp.float32) * scale
        s_sel = jnp.where(validc[..., None], s_sel, -jnp.inf).reshape(B, H, QC, topk * BLK)
        own = (c * QC) // BLK
        ko = lax.dynamic_index_in_dim(kb, own, axis=2, keepdims=False)
        vo = lax.dynamic_index_in_dim(vb, own, axis=2, keepdims=False)
        s_own = jnp.einsum('bhqd,bhjd->bhqj', qc, ko).astype(jnp.float32) * scale
        qpos = c * QC + jnp.arange(QC)
        kpos = own * BLK + jnp.arange(BLK)
        s_own = jnp.where(kpos[None, :] <= qpos[:, None], s_own, -jnp.inf)
        p = jax.nn.softmax(jnp.concatenate([s_sel, s_own], axis=-1), axis=-1).astype(v.dtype)
        p_sel = p[..., :topk * BLK].reshape(B, H, QC, topk, BLK)
        p_own = p[..., topk * BLK:]
        return (jnp.einsum('bhqkj,bhqkjd->bhqd', p_sel, vg)
                + jnp.einsum('bhqj,bhjd->bhqd', p_own, vo))

    o = lax.map(one_chunk, (chunks(q), chunks(idx), chunks(valid), jnp.arange(nc)))
    o = o.transpose(1, 0, 3, 2, 4).reshape(B, Sp, H * hd)
    return o[:, :S]

def _hybrid_layer(x, w_in, gla_w_up, gla_b, gla_norm_g, swa_sinks, b_merge, w_branch, w_o, ln_g, ln_b):
    B, S, D = x.shape
    proj = x @ w_in
    split_idx = np.cumsum(IN_SPLITS)[:-1].tolist()
    (aq, ak, av, alr, agate, bq, bk, bv, bgate, cq, ck, cv, cgate, mgate) = jnp.split(proj, split_idx, axis=-1)
    g = jax.nn.log_sigmoid((alr @ gla_w_up + gla_b).astype(jnp.float32)) / GLA_TAU
    ya = _gla_branch(aq.reshape(B, S, GLA_HEADS, GLA_DK), ak.reshape(B, S, GLA_HEADS, GLA_DK),
                     av.reshape(B, S, GLA_HEADS, GLA_DV), g.reshape(B, S, GLA_HEADS, GLA_DK), gla_norm_g)
    ya = ya * jax.nn.silu(agate)
    yb = _swa_branch(bq.reshape(B, S, SWA_Q_HEADS, SWA_HEAD_DIM), bk.reshape(B, S, SWA_KV_HEADS, SWA_HEAD_DIM),
                     bv.reshape(B, S, SWA_KV_HEADS, SWA_HEAD_DIM), swa_sinks)
    yb = yb * jax.nn.silu(bgate)
    yc = _moba_branch(cq.reshape(B, S, MOBA_HEADS, MOBA_HEAD_DIM), ck.reshape(B, S, MOBA_HEADS, MOBA_HEAD_DIM),
                      cv.reshape(B, S, MOBA_HEADS, MOBA_HEAD_DIM))
    yc = yc * jax.nn.silu(cgate)
    ys = jnp.stack([ya.astype(x.dtype), yb.astype(x.dtype), yc.astype(x.dtype)], axis=2)
    up = jnp.einsum('bsnw,nwd->bsnd', ys, w_branch)
    gates = jax.nn.sigmoid(mgate.reshape(B, S, N_BRANCH, D) + b_merge)
    merged = jnp.sum(gates * up, axis=2)
    out = merged @ w_o
    return _layer_norm(DEEPNORM_ALPHA * x + out, ln_g, ln_b)

def first_inputs(seed: int = 0) -> dict:
    key = jax.random.key(seed)
    ks = jax.random.split(key, 12)
    L, D = DEPTH, D_MODEL
    col_scale = np.concatenate([np.full((n,), DEEPNORM_BETA if i in VALUE_SEGMENTS else 1.0, np.float32)
                                for i, n in enumerate(IN_SPLITS)])
    x = jax.random.normal(ks[0], (BATCH, SEQ, D), jnp.float32)
    w_in = jax.random.normal(ks[1], (L, D, D_IN), jnp.float32) * (D ** -0.5) * jnp.asarray(col_scale)
    gla_w_up = jax.random.normal(ks[2], (L, GLA_RANK, GLA_HEADS * GLA_DK), jnp.float32) * (GLA_RANK ** -0.5)
    gla_b = 0.1 * jax.random.normal(ks[3], (L, GLA_HEADS * GLA_DK), jnp.float32)
    gla_norm_g = 1.0 + 0.02 * jax.random.normal(ks[4], (L, GLA_DV), jnp.float32)
    swa_sinks = 0.5 * jax.random.normal(ks[5], (L, SWA_Q_HEADS), jnp.float32)
    b_merge = 0.02 * jax.random.normal(ks[6], (L, N_BRANCH, D), jnp.float32)
    w_branch = jax.random.normal(ks[7], (L, N_BRANCH, BRANCH_WIDTH, D), jnp.float32) * (BRANCH_WIDTH ** -0.5) * DEEPNORM_BETA
    w_o = jax.random.normal(ks[8], (L, D, D), jnp.float32) * (D ** -0.5) * DEEPNORM_BETA
    ln_g = 1.0 + 0.02 * jax.random.normal(ks[9], (L, D), jnp.float32)
    ln_b = 0.02 * jax.random.normal(ks[10], (L, D), jnp.float32)
    return {"x": x, "w_in": w_in, "gla_w_up": gla_w_up, "gla_b": gla_b, "gla_norm_g": gla_norm_g,
            "swa_sinks": swa_sinks, "b_merge": b_merge, "w_branch": w_branch, "w_o": w_o,
            "ln_g": ln_g, "ln_b": ln_b}

def first_block(x, w_in, gla_w_up, gla_b, gla_norm_g, swa_sinks, b_merge, w_branch, w_o, ln_g, ln_b):
    for l in range(DEPTH):
        x = _hybrid_layer(x, w_in[l], gla_w_up[l], gla_b[l], gla_norm_g[l], swa_sinks[l], b_merge[l],
                          w_branch[l], w_o[l], ln_g[l], ln_b[l])
    return x


_first_inputs = first_inputs


def first_inputs(seed=0):
    import zlib

    import numpy as np

    out = dict(_first_inputs(seed))
    spreads = {}
    factors = {'gla_w_up': 5.984,
     'gla_b': 8.0,
     'gla_norm_g': 8.0,
     'swa_sinks': 8.0,
     'b_merge': 8.0,
     'ln_g': 2.79,
     'ln_b': 2.86}
    for name, (base, spread) in spreads.items():
        noise = np.random.default_rng([zlib.crc32(name.encode()), seed]).standard_normal(out[name].shape)
        drawn = base * np.exp(spread * noise) if base else spread * noise
        out[name] = __import__('jax').numpy.asarray(drawn.astype(out[name].dtype))
    for name, factor in factors.items():
        out[name] = (out[name] * factor).astype(out[name].dtype)
    return out


_narrow_inputs = first_inputs


def first_inputs(seed=0):

    out = dict(_narrow_inputs(seed))
    wider = {'gla_norm_g': 5.38, 'swa_sinks': 12.0, 'ln_g': 3.13, 'ln_b': 3.14}
    for name, times in wider.items():
        mean = out[name].mean()
        out[name] = (mean + times * (out[name] - mean)).astype(out[name].dtype)
    return out


MIX_WIDTH = D_MODEL
CONV_CH = MIX_WIDTH // 2
CONV_GROUPS = 8
CONV_WIDTH = 31
GDN_HEADS = 8
HEAD_DIM = (MIX_WIDTH - CONV_CH) // GDN_HEADS
GDN_WIDTH = GDN_HEADS * HEAD_DIM
SHORT_CONV = 4
CHUNK = 64
D_FF = ((8 * D_MODEL // 3 + 255) // 256) * 256
IN_COLS = 2 * CONV_CH + 4 * GDN_WIDTH + 2 * GDN_HEADS
L2_EPS = 1e-6


def layer_norm(x, g, b):
    xf = x.astype(jnp.float32)
    mu = jnp.mean(xf, -1, keepdims=True)
    var = jnp.mean(jnp.square(xf - mu), -1, keepdims=True)
    y = (xf - mu) * lax.rsqrt(var + LN_EPS) * g.astype(jnp.float32) + b.astype(jnp.float32)
    return y.astype(x.dtype)

def rms_norm(x, g):
    xf = x.astype(jnp.float32)
    return xf * lax.rsqrt(jnp.mean(xf * xf, -1, keepdims=True) + RMS_EPS) * g.astype(jnp.float32)

def l2norm(x):
    xf = x.astype(jnp.float32)
    return xf * lax.rsqrt(jnp.sum(xf * xf, -1, keepdims=True) + L2_EPS)

def causal_depthwise_conv(x, w):
    k_len, ch = w.shape
    return lax.conv_general_dilated(
        x, w.astype(x.dtype)[:, None, :], window_strides=(1,),
        padding=[(k_len - 1, 0)], dimension_numbers=('NWC', 'WIO', 'NWC'),
        feature_group_count=ch)

def conformer_conv_group(u_val, u_gate, dw_w, dw_b, ln_g, ln_b):
    h = u_val * jax.nn.sigmoid(u_gate)
    h = causal_depthwise_conv(h, dw_w) + dw_b.astype(h.dtype)
    h = layer_norm(h, ln_g, ln_b)
    return jax.nn.silu(h)

def chunk_gated_delta_rule(q, k, v, g, beta):
    bsz, seq, nh, dk = q.shape
    dv = v.shape[-1]
    n_chunks = seq // CHUNK
    q = q * (dk ** -0.5)

    def chunks(t):
        return t.reshape(bsz, n_chunks, CHUNK, nh, -1).transpose(0, 3, 1, 2, 4)

    q, k, v = chunks(q), chunks(k), chunks(v)
    beta = beta.reshape(bsz, n_chunks, CHUNK, nh).transpose(0, 3, 1, 2)
    g = jnp.cumsum(g.reshape(bsz, n_chunks, CHUNK, nh).transpose(0, 3, 1, 2), axis=-1)

    idx = jnp.arange(CHUNK)
    causal = idx[:, None] >= idx[None, :]
    strict = idx[:, None] > idx[None, :]
    decay = jnp.exp(jnp.where(causal, g[..., :, None] - g[..., None, :], -jnp.inf))

    k_beta = k * beta[..., None]
    v_beta = v * beta[..., None]
    L = jnp.einsum('bhnid,bhnjd->bhnij', k_beta, k) * jnp.where(strict, decay, 0.0)
    lhs = jnp.eye(CHUNK, dtype=jnp.float32) + L
    rhs = jnp.concatenate([v_beta, k_beta * jnp.exp(g)[..., None]], axis=-1)
    sol = lax.linalg.triangular_solve(lhs, rhs, left_side=True, lower=True, unit_diagonal=True)
    u_c = sol[..., :dv]
    w_c = sol[..., dv:]

    intra = jnp.einsum('bhnid,bhnjd->bhnij', q, k) * decay
    q_dec = q * jnp.exp(g)[..., None]
    g_last = g[..., -1]
    k_dec = k * jnp.exp(g_last[..., None] - g)[..., None]

    def step(state, xs):
        u_i, w_i, qd_i, kd_i, a_i, gl_i = xs
        v_new = u_i - jnp.einsum('bhcd,bhde->bhce', w_i, state)
        o_i = (jnp.einsum('bhcd,bhde->bhce', qd_i, state)
               + jnp.einsum('bhij,bhje->bhie', a_i, v_new))
        state = state * jnp.exp(gl_i)[..., None, None] + jnp.einsum('bhcd,bhce->bhde', kd_i, v_new)
        return state, o_i

    xs = tuple(jnp.moveaxis(t, 2, 0) for t in (u_c, w_c, q_dec, k_dec, intra, g_last))
    state0 = jnp.zeros((bsz, nh, dk, dv), jnp.float32)
    _, o = lax.scan(step, state0, xs)
    return o.transpose(1, 0, 3, 2, 4).reshape(bsz, seq, nh, dv)

def gated_deltanet_group(qkv, z, b_raw, a_raw, sc_w, A_log, dt_bias, norm_w):
    bsz, seq, _ = qkv.shape
    qkv = jax.nn.silu(causal_depthwise_conv(qkv, sc_w))
    q = qkv[..., :GDN_WIDTH].reshape(bsz, seq, GDN_HEADS, HEAD_DIM)
    k = qkv[..., GDN_WIDTH:2 * GDN_WIDTH].reshape(bsz, seq, GDN_HEADS, HEAD_DIM)
    v = qkv[..., 2 * GDN_WIDTH:].reshape(bsz, seq, GDN_HEADS, HEAD_DIM).astype(jnp.float32)
    q, k = l2norm(q), l2norm(k)
    beta = jax.nn.sigmoid(b_raw.astype(jnp.float32))
    g = -jnp.exp(A_log.astype(jnp.float32)) * jax.nn.softplus(
        a_raw.astype(jnp.float32) + dt_bias.astype(jnp.float32))
    o = chunk_gated_delta_rule(q, k, v, g, beta)
    zh = z.reshape(bsz, seq, GDN_HEADS, HEAD_DIM).astype(jnp.float32)
    o = rms_norm(o, norm_w) * jax.nn.silu(zh)
    return o.reshape(bsz, seq, GDN_WIDTH).astype(z.dtype)

def second_inputs(seed: int = 0) -> dict:
    key = jax.random.key(seed)
    ks = jax.random.split(key, 20)
    f32 = jnp.float32
    beta_init = (8 * DEPTH) ** -0.25
    nrm = lambda k, shape, s: jax.random.normal(k, shape, f32) * s
    dt = jnp.exp(jax.random.uniform(ks[8], (DEPTH, GDN_HEADS), f32, np.log(1e-3), np.log(1e-1)))
    return {
        "x": jax.random.normal(ks[0], (BATCH, SEQ, D_MODEL), f32),
        "w_in": nrm(ks[1], (DEPTH, D_MODEL, IN_COLS), D_MODEL ** -0.5),
        "conv_dw_w": nrm(ks[2], (DEPTH, CONV_WIDTH, CONV_CH), CONV_WIDTH ** -0.5),
        "conv_dw_b": nrm(ks[3], (DEPTH, CONV_CH), 0.01),
        "conv_ln_g": 1.0 + nrm(ks[4], (DEPTH, CONV_CH), 0.02),
        "conv_ln_b": nrm(ks[5], (DEPTH, CONV_CH), 0.01),
        "gdn_conv_w": nrm(ks[6], (DEPTH, SHORT_CONV, 3 * GDN_WIDTH), SHORT_CONV ** -0.5),
        "gdn_A_log": jnp.log(jax.random.uniform(ks[7], (DEPTH, GDN_HEADS), f32, 1.0, 16.0)),
        "gdn_dt_bias": dt + jnp.log(-jnp.expm1(-dt)),
        "gdn_norm_w": 1.0 + nrm(ks[9], (DEPTH, HEAD_DIM), 0.02),
        "w_out": nrm(ks[10], (DEPTH, MIX_WIDTH, D_MODEL), MIX_WIDTH ** -0.5 * beta_init),
        "ln1_g": 1.0 + nrm(ks[11], (DEPTH, D_MODEL), 0.02),
        "ln1_b": nrm(ks[12], (DEPTH, D_MODEL), 0.01),
        "w_gate_up": nrm(ks[13], (DEPTH, D_MODEL, 2 * D_FF), D_MODEL ** -0.5),
        "w_down": nrm(ks[14], (DEPTH, D_FF, D_MODEL), D_FF ** -0.5 * beta_init),
        "ln2_g": 1.0 + nrm(ks[15], (DEPTH, D_MODEL), 0.02),
        "ln2_b": nrm(ks[16], (DEPTH, D_MODEL), 0.01),
    }

def second_block(x, w_in, conv_dw_w, conv_dw_b, conv_ln_g, conv_ln_b, gdn_conv_w, gdn_A_log,
              gdn_dt_bias, gdn_norm_w, w_out, ln1_g, ln1_b, w_gate_up, w_down, ln2_g, ln2_b):
    alpha = (2 * DEPTH) ** 0.25
    c0 = 2 * CONV_CH
    c1 = c0 + 3 * GDN_WIDTH
    c2 = c1 + GDN_WIDTH
    c3 = c2 + GDN_HEADS
    for l in range(DEPTH):
        u = jnp.einsum('bsd,dc->bsc', x, w_in[l])
        conv_out = conformer_conv_group(u[..., :CONV_CH], u[..., CONV_CH:c0],
                                        conv_dw_w[l], conv_dw_b[l], conv_ln_g[l], conv_ln_b[l])
        gdn_out = gated_deltanet_group(u[..., c0:c1], u[..., c1:c2], u[..., c2:c3], u[..., c3:],
                                       gdn_conv_w[l], gdn_A_log[l], gdn_dt_bias[l], gdn_norm_w[l])
        mix = jnp.einsum('bsm,md->bsd', jnp.concatenate([conv_out, gdn_out], axis=-1), w_out[l])
        x = layer_norm(alpha * x + mix, ln1_g[l], ln1_b[l])
        gu = jnp.einsum('bsd,df->bsf', x, w_gate_up[l])
        hid = jax.nn.silu(gu[..., :D_FF]) * gu[..., D_FF:]
        ffn = jnp.einsum('bsf,fd->bsd', hid, w_down[l])
        x = layer_norm(alpha * x + ffn, ln2_g[l], ln2_b[l])
    return x


_first_inputs_2 = second_inputs


def second_inputs(seed=0):
    import zlib

    import numpy as np

    out = dict(_first_inputs_2(seed))
    spreads = {}
    factors = {'conv_dw_b': 8.0,
     'conv_ln_g': 8.0,
     'conv_ln_b': 8.0,
     'gdn_norm_w': 8.0,
     'ln1_g': 2.793,
     'ln1_b': 5.579,
     'ln2_g': 2.742,
     'ln2_b': 5.802}
    for name, (base, spread) in spreads.items():
        noise = np.random.default_rng([zlib.crc32(name.encode()), seed]).standard_normal(out[name].shape)
        drawn = base * np.exp(spread * noise) if base else spread * noise
        out[name] = __import__('jax').numpy.asarray(drawn.astype(out[name].dtype))
    for name, factor in factors.items():
        out[name] = (out[name] * factor).astype(out[name].dtype)
    return out


_narrow_inputs_2 = second_inputs


def second_inputs(seed=0):

    out = dict(_narrow_inputs_2(seed))
    wider = {'conv_ln_g': 3.6, 'conv_ln_b': 6.9, 'gdn_norm_w': 3.94, 'ln2_g': 3.09, 'ln2_b': 3.09}
    for name, times in wider.items():
        mean = out[name].mean()
        out[name] = (mean + times * (out[name] - mean)).astype(out[name].dtype)
    return out


D_MIX = D_MODEL
HEAD_DIM_3 = 128
A_HEADS = 6
A_WIDTH = A_HEADS * HEAD_DIM_3
IDX_HEADS = 8
IDX_DIM = 64
TOPK_MAX = 256
M_HEADS = 6
M_DH = HEAD_DIM_3
M_WIDTH = M_HEADS * M_DH
M_CHUNK = 64
CONV_W = 4
C_HEADS = 4
C_QK = 64
C_DV = 2 * C_QK
C_WIDTH = C_HEADS * C_DV
D_FF_3 = 4 * D_MODEL
Q_BLOCK = 128
ALPHA = (2.0 * DEPTH) ** 0.25
BETA = (8.0 * DEPTH) ** -0.25
EPS = 1e-5

SIZES = (A_WIDTH, A_WIDTH, A_WIDTH, IDX_HEADS * IDX_DIM, IDX_DIM, IDX_HEADS,
         M_WIDTH, M_WIDTH, M_WIDTH, M_WIDTH, M_HEADS, M_HEADS,
         C_HEADS * 2 * C_QK, C_HEADS * 2 * C_QK, C_WIDTH)
VALUE_SEGMENTS_3 = (2, 8, 14)
D_IN_3 = sum(SIZES)
SPLIT_POINTS = tuple(int(p) for p in np.cumsum(SIZES)[:-1])


def alibi_slopes(n):
    return 2.0 ** (-8.0 * jnp.arange(1, n + 1, dtype=jnp.float32) / n)

def layer_norm_3(x, g, b):
    xf = x.astype(jnp.float32)
    mu = jnp.mean(xf, axis=-1, keepdims=True)
    var = jnp.mean(jnp.square(xf - mu), axis=-1, keepdims=True)
    return ((xf - mu) * lax.rsqrt(var + EPS) * g + b).astype(x.dtype)

def head_rmsnorm(h, g):
    hf = h.astype(jnp.float32)
    return (hf * lax.rsqrt(jnp.mean(hf * hf, axis=-1, keepdims=True) + EPS) * g).astype(h.dtype)

def causal_conv(x, w):
    return lax.conv_general_dilated(x, w.astype(x.dtype), window_strides=(1,),
                                    padding=[(CONV_W - 1, 0)],
                                    dimension_numbers=('NWC', 'WIO', 'NWC'),
                                    feature_group_count=x.shape[-1])

def dsa_attention(q, k, v, q_idx, k_idx, w_idx):
    B, S, H, D = q.shape
    nb = S // Q_BLOCK
    k_sel = min(TOPK_MAX, S // 4)
    slopes = alibi_slopes(H)
    scale = D ** -0.5
    pos_k = jnp.arange(S)

    def block(args):
        qb, qib, wb, t0 = args
        pos_q = t0 + jnp.arange(Q_BLOCK)
        sc = jax.nn.relu(jnp.einsum('bqhd,bsd->bqhs', qib, k_idx).astype(jnp.float32))
        idx_score = jnp.einsum('bqhs,bqh->bqs', sc, wb.astype(jnp.float32))
        causal = pos_k[None, :] <= pos_q[:, None]
        idx_score = jnp.where(causal[None], idx_score, -jnp.inf)
        _, sel = lax.top_k(idx_score, k_sel)
        valid = sel <= pos_q[None, :, None]
        k_g = jax.vmap(lambda kk, ii: kk[ii])(k, sel)
        v_g = jax.vmap(lambda vv, ii: vv[ii])(v, sel)
        logits = jnp.einsum('bqhd,bqkhd->bhqk', qb, k_g).astype(jnp.float32) * scale
        dist = (pos_q[None, :, None] - sel).astype(jnp.float32)
        logits = logits - slopes[None, :, None, None] * dist[:, None]
        logits = jnp.where(valid[:, None], logits, -jnp.inf)
        p = jax.nn.softmax(logits, axis=-1)
        return jnp.einsum('bhqk,bqkhd->bqhd', p.astype(v.dtype), v_g)

    qs = q.reshape(B, nb, Q_BLOCK, H, D).transpose(1, 0, 2, 3, 4)
    qis = q_idx.reshape(B, nb, Q_BLOCK, IDX_HEADS, IDX_DIM).transpose(1, 0, 2, 3, 4)
    ws = w_idx.reshape(B, nb, Q_BLOCK, IDX_HEADS).transpose(1, 0, 2, 3)
    t0s = jnp.arange(nb) * Q_BLOCK
    out = lax.map(block, (qs, qis, ws, t0s))
    return out.transpose(1, 0, 2, 3, 4).reshape(B, S, H, D)

def mlstm_chunkwise(q, k, v, i_pre, f_pre):
    B, S, H, D = q.shape
    L = M_CHUNK
    nc = S // L
    f32 = jnp.float32

    def chunks(t):
        return t.astype(f32).reshape(B, nc, L, H, D).transpose(1, 0, 3, 2, 4)

    def gchunks(t):
        return t.reshape(B, nc, L, H).transpose(1, 0, 3, 2)

    log_f = gchunks(jax.nn.log_sigmoid(f_pre.astype(f32)))
    log_i = gchunks(i_pre.astype(f32))
    tril = jnp.tril(jnp.ones((L, L), dtype=bool))

    def step(carry, inp):
        C, n, m = carry
        qj, kj, vj, lfj, lij = inp
        a = jnp.cumsum(lfj, axis=-1)
        g = a[..., -1]
        d_intra = a[..., :, None] - a[..., None, :] + lij[..., None, :]
        d_intra = jnp.where(tril, d_intra, -jnp.inf)
        inter = a + m[..., None]
        m_row = jnp.maximum(inter, jnp.max(d_intra, axis=-1))
        w_intra = jnp.exp(d_intra - m_row[..., None])
        w_inter = jnp.exp(inter - m_row)
        qk = jnp.einsum('bhld,bhsd->bhls', qj, kj) * w_intra
        num = jnp.einsum('bhls,bhse->bhle', qk, vj) + w_inter[..., None] * jnp.einsum('bhld,bhde->bhle', qj, C)
        den = jnp.sum(qk, axis=-1) + w_inter * jnp.einsum('bhld,bhd->bhl', qj, n)
        h = num / jnp.maximum(jnp.abs(den), jnp.exp(-m_row))[..., None]
        decay = g[..., None] - a + lij
        m_new = jnp.maximum(g + m, jnp.max(decay, axis=-1))
        ws = jnp.exp(decay - m_new[..., None])
        wc = jnp.exp(g + m - m_new)
        C_new = wc[..., None, None] * C + jnp.einsum('bhs,bhsd,bhse->bhde', ws, kj, vj)
        n_new = wc[..., None] * n + jnp.einsum('bhs,bhsd->bhd', ws, kj)
        return (C_new, n_new, m_new), h

    init = (jnp.zeros((B, H, D, D), f32), jnp.zeros((B, H, D), f32), jnp.zeros((B, H), f32))
    _, hs = lax.scan(step, init, (chunks(q), chunks(k), chunks(v), log_f, log_i))
    return hs.transpose(1, 0, 3, 2, 4).reshape(B, S, H, D).astype(v.dtype)

def diff_attention(q, k, v, lam):
    B, S, H, _, d = q.shape
    nb = S // Q_BLOCK
    slopes = alibi_slopes(H)
    scale = d ** -0.5
    pos_k = jnp.arange(S)

    def block(args):
        qb, t0 = args
        pos_q = t0 + jnp.arange(Q_BLOCK)
        s = jnp.einsum('bqhmd,bshmd->bmhqs', qb, k).astype(jnp.float32) * scale
        dist = (pos_q[:, None] - pos_k[None, :]).astype(jnp.float32)
        s = jnp.where(dist >= 0, s - slopes[:, None, None] * dist, -jnp.inf)
        p = jax.nn.softmax(s, axis=-1)
        attn = p[:, 0] - lam * p[:, 1]
        return jnp.einsum('bhqs,bshe->bqhe', attn.astype(v.dtype), v)

    qs = q.reshape(B, nb, Q_BLOCK, H, 2, d).transpose(1, 0, 2, 3, 4, 5)
    t0s = jnp.arange(nb) * Q_BLOCK
    out = lax.map(block, (qs, t0s))
    return out.transpose(1, 0, 2, 3, 4).reshape(B, S, H, v.shape[-1])

def token_mixers(xn, layer_idx, w_in, conv_w, b_i, b_f, m_norm_g, lq1, lk1, lq2, lk2, c_norm_g):
    B, S, _ = xn.shape
    proj = jnp.einsum('bsd,de->bse', xn, w_in)
    (q_a, k_a, v_a, q_i, k_i, w_i, q_m, k_m, v_m, o_m, i_m, f_m,
     q_c, k_c, v_c) = jnp.split(proj, SPLIT_POINTS, axis=-1)

    y_a = dsa_attention(q_a.reshape(B, S, A_HEADS, HEAD_DIM_3), k_a.reshape(B, S, A_HEADS, HEAD_DIM_3),
                        v_a.reshape(B, S, A_HEADS, HEAD_DIM_3), q_i.reshape(B, S, IDX_HEADS, IDX_DIM),
                        k_i, w_i).reshape(B, S, A_WIDTH)

    qk_m = jax.nn.silu(causal_conv(jnp.concatenate([q_m, k_m], axis=-1), conv_w))
    q_m, k_m = jnp.split(qk_m, 2, axis=-1)
    h_m = mlstm_chunkwise(q_m.reshape(B, S, M_HEADS, M_DH),
                          k_m.reshape(B, S, M_HEADS, M_DH) * (M_DH ** -0.5),
                          v_m.reshape(B, S, M_HEADS, M_DH), i_m + b_i, f_m + b_f)
    y_m = jax.nn.sigmoid(o_m) * head_rmsnorm(h_m, m_norm_g.reshape(M_HEADS, M_DH)).reshape(B, S, M_WIDTH)

    lam_init = 0.8 - 0.6 * math.exp(-0.3 * layer_idx)
    lam = (jnp.exp(jnp.sum(lq1.astype(jnp.float32) * lk1)) - jnp.exp(jnp.sum(lq2.astype(jnp.float32) * lk2))
           + lam_init)
    h_c = diff_attention(q_c.reshape(B, S, C_HEADS, 2, C_QK), k_c.reshape(B, S, C_HEADS, 2, C_QK),
                         v_c.reshape(B, S, C_HEADS, C_DV), lam)
    y_c = (head_rmsnorm(h_c, c_norm_g.reshape(C_HEADS, C_DV)) * (1.0 - lam_init)).reshape(B, S, C_WIDTH)

    return jnp.concatenate([y_a, y_m, y_c], axis=-1)

def third_inputs(seed: int = 0) -> dict:
    key = jax.random.key(seed)
    ks = jax.random.split(key, 20)
    f32 = jnp.float32
    col_scale = jnp.concatenate([jnp.full((s,), BETA if i in VALUE_SEGMENTS_3 else 1.0, f32)
                                 for i, s in enumerate(SIZES)])
    x = jax.random.normal(ks[0], (BATCH, SEQ, D_MODEL), f32)
    w_in = jax.random.normal(ks[1], (DEPTH, D_MODEL, D_IN_3), f32) * (D_MODEL ** -0.5) * col_scale
    conv_m = jax.random.normal(ks[2], (DEPTH, CONV_W, 1, 2 * M_WIDTH), f32) * (CONV_W ** -0.5)
    b_i = 0.01 * jax.random.normal(ks[3], (DEPTH, M_HEADS), f32)
    b_f = jnp.linspace(3.0, 6.0, M_HEADS, dtype=f32)[None] + 0.01 * jax.random.normal(ks[4], (DEPTH, M_HEADS), f32)
    m_norm_g = 1.0 + 0.01 * jax.random.normal(ks[5], (DEPTH, M_WIDTH), f32)
    lam_q1 = 0.1 * jax.random.normal(ks[6], (DEPTH, C_QK), f32)
    lam_k1 = 0.1 * jax.random.normal(ks[7], (DEPTH, C_QK), f32)
    lam_q2 = 0.1 * jax.random.normal(ks[8], (DEPTH, C_QK), f32)
    lam_k2 = 0.1 * jax.random.normal(ks[9], (DEPTH, C_QK), f32)
    c_norm_g = 1.0 + 0.01 * jax.random.normal(ks[10], (DEPTH, C_WIDTH), f32)
    w_out = jax.random.normal(ks[11], (DEPTH, D_MIX, D_MODEL), f32) * (D_MIX ** -0.5) * BETA
    ln1_g = 1.0 + 0.01 * jax.random.normal(ks[12], (DEPTH, D_MODEL), f32)
    ln1_b = 0.01 * jax.random.normal(ks[13], (DEPTH, D_MODEL), f32)
    w_up = jax.random.normal(ks[14], (DEPTH, D_MODEL, D_FF_3), f32) * (D_MODEL ** -0.5) * BETA
    w_down = jax.random.normal(ks[15], (DEPTH, D_FF_3, D_MODEL), f32) * (D_FF_3 ** -0.5) * BETA
    ln2_g = 1.0 + 0.01 * jax.random.normal(ks[16], (DEPTH, D_MODEL), f32)
    ln2_b = 0.01 * jax.random.normal(ks[17], (DEPTH, D_MODEL), f32)
    return {"x": x, "w_in": w_in, "conv_m": conv_m, "b_i": b_i, "b_f": b_f, "m_norm_g": m_norm_g,
            "lam_q1": lam_q1, "lam_k1": lam_k1, "lam_q2": lam_q2, "lam_k2": lam_k2,
            "c_norm_g": c_norm_g, "w_out": w_out, "ln1_g": ln1_g, "ln1_b": ln1_b,
            "w_up": w_up, "w_down": w_down, "ln2_g": ln2_g, "ln2_b": ln2_b}

def third_block(x, w_in, conv_m, b_i, b_f, m_norm_g, lam_q1, lam_k1, lam_q2, lam_k2,
              c_norm_g, w_out, ln1_g, ln1_b, w_up, w_down, ln2_g, ln2_b):
    for l in range(DEPTH):
        mixed = token_mixers(x, l, w_in[l], conv_m[l], b_i[l], b_f[l], m_norm_g[l],
                             lam_q1[l], lam_k1[l], lam_q2[l], lam_k2[l], c_norm_g[l])
        x = layer_norm_3(ALPHA * x + jnp.einsum('bse,ed->bsd', mixed, w_out[l]), ln1_g[l], ln1_b[l])
        h = jnp.square(jax.nn.relu(jnp.einsum('bsd,df->bsf', x, w_up[l])))
        x = layer_norm_3(ALPHA * x + jnp.einsum('bsf,fd->bsd', h, w_down[l]), ln2_g[l], ln2_b[l])
    return x


_first_inputs_3 = third_inputs


def third_inputs(seed=0):
    import zlib

    import numpy as np

    out = dict(_first_inputs_3(seed))
    spreads = {}
    factors = {'b_i': 200.0,
     'm_norm_g': 200.0,
     'lam_q1': 64.0,
     'lam_k1': 3.964,
     'lam_q2': 2.818,
     'lam_k2': 200.0,
     'c_norm_g': 200.0,
     'ln1_g': 153.697,
     'ln1_b': 151.219,
     'ln2_g': 196.185,
     'ln2_b': 191.253}
    for name, (base, spread) in spreads.items():
        noise = np.random.default_rng([zlib.crc32(name.encode()), seed]).standard_normal(out[name].shape)
        drawn = base * np.exp(spread * noise) if base else spread * noise
        out[name] = __import__('jax').numpy.asarray(drawn.astype(out[name].dtype))
    for name, factor in factors.items():
        out[name] = (out[name] * factor).astype(out[name].dtype)
    return out


_narrow_inputs_3 = third_inputs


def third_inputs(seed=0):

    out = dict(_narrow_inputs_3(seed))
    wider = {'m_norm_g': 8.95,
     'c_norm_g': 6.88,
     'ln1_g': 5.64,
     'ln1_b': 5.65,
     'ln2_g': 6.52,
     'ln2_b': 6.52}
    for name, times in wider.items():
        mean = out[name].mean()
        out[name] = (mean + times * (out[name] - mean)).astype(out[name].dtype)
    return out


def setup_inputs(seed=0):
    out = dict(first_inputs(seed))
    for name, value in second_inputs(seed + 1).items():
        if name != "x":
            out[name + "_2"] = value
    for name, value in third_inputs(seed + 2).items():
        if name != "x":
            out[name + "_3"] = value
    return out


def reference(
    x, w_in, gla_w_up, gla_b, gla_norm_g, swa_sinks, b_merge, w_branch, w_o, ln_g, ln_b, w_in_2,
    conv_dw_w_2, conv_dw_b_2, conv_ln_g_2, conv_ln_b_2, gdn_conv_w_2, gdn_A_log_2,
    gdn_dt_bias_2, gdn_norm_w_2, w_out_2, ln1_g_2, ln1_b_2, w_gate_up_2, w_down_2, ln2_g_2,
    ln2_b_2, w_in_3, conv_m_3, b_i_3, b_f_3, m_norm_g_3, lam_q1_3, lam_k1_3, lam_q2_3, lam_k2_3,
    c_norm_g_3, w_out_3, ln1_g_3, ln1_b_3, w_up_3, w_down_3, ln2_g_3, ln2_b_3,
):
    x = first_block(
        x, w_in, gla_w_up, gla_b, gla_norm_g, swa_sinks, b_merge, w_branch, w_o, ln_g, ln_b,
    )
    x = second_block(
        x, w_in_2, conv_dw_w_2, conv_dw_b_2, conv_ln_g_2, conv_ln_b_2, gdn_conv_w_2,
        gdn_A_log_2, gdn_dt_bias_2, gdn_norm_w_2, w_out_2, ln1_g_2, ln1_b_2, w_gate_up_2,
        w_down_2, ln2_g_2, ln2_b_2,
    )
    return third_block(
        x, w_in_3, conv_m_3, b_i_3, b_f_3, m_norm_g_3, lam_q1_3, lam_k1_3, lam_q2_3, lam_k2_3,
        c_norm_g_3, w_out_3, ln1_g_3, ln1_b_3, w_up_3, w_down_3, ln2_g_3, ln2_b_3,
    )


_drawn_inputs = setup_inputs


def setup_inputs(seed=0):
    import zlib

    import numpy as np

    out = dict(_drawn_inputs(seed))
    spreads = {}
    factors = {'swa_sinks': 3.647, 'b_i_3': 6.288}
    for name, (base, spread) in spreads.items():
        noise = np.random.default_rng([zlib.crc32(name.encode()), seed]).standard_normal(out[name].shape)
        drawn = base * np.exp(spread * noise) if base else spread * noise
        out[name] = __import__('jax').numpy.asarray(drawn.astype(out[name].dtype))
    for name, factor in factors.items():
        out[name] = (out[name] * factor).astype(out[name].dtype)
    return out
```

```python
import math
from contextlib import ExitStack, contextmanager

import concourse.bass as bass
from concourse import mybir
import numpy as np

F32 = mybir.dt.float32
I32 = mybir.dt.int32
ALU = mybir.AluOpType
ACT = mybir.ActivationFunctionType
AX = mybir.AxisListType.X
ds = bass.ds

P = 128
S = 256
D = 2048
KT = D // P
CH = 8
TW = 512
RING = 4
NEG = -1.0e30
TAKEN = -3.0e38
ALPHA = 2.0 ** 0.25
LN_EPS, RMS_EPS = 1e-5, 1e-6

G_H, G_RANK, G_TAU = 4, 16, 16.0
BW = 1024
C_AQ, C_AV, C_ALR, C_AG = 0, 1024, 2048, 2064
C_BQ = C_AG + BW
C_BK = C_BQ + 1024
C_BV = C_BK + 128
C_BG = C_BV + 128
C_CQ = C_BG + BW
C_CV = C_CQ + 2048
C_CG = C_CV + 1024
C_MG = C_CG + BW
CONV_W, SHORT_W, GD_H = 31, 4, 8
D_FF2 = 5632
C_QKV2, C_Z2, C_BA2 = 2048, 5120, 6144
A_H, M_H, D_H = 6, 6, 4
C_VA = 1536
C_QI = 2304
C_KI = C_QI + 512
C_WI = C_KI + 64
C_QM = C_WI + 8
C_VM = C_QM + 1536
C_OM = C_VM + 768
C_IF = C_OM + 768
C_QC = C_IF + 12
C_VC = C_QC + 1024
TOPK = 64
D_FF3 = 8192
SHRINK = 2.0 ** -40
LARGE = 1.0e20
ROOT_MAX = math.sqrt(2.0 ** 128 / P) * SHRINK

R_DWW, R_DWB, R_CLG, R_CLB = 0, 31, 32, 33
R_SCW = 34
R_BM = R_SCW + SHORT_W * 3
R_GLAB = R_BM + 6
R_MNG, R_CNG, R_GLAG = R_GLAB + 1, R_GLAB + 2, R_GLAB + 3
R_CM = R_GLAG + 1
T_GDNW = 2
R_ALL = 64


class Count:

    def __init__(self, start):
        self.n, self.i, self.per = dict(start), None, {}

    def now(self, sem, k=0):
        v = self.n.get(sem, 0)
        self.n[sem] = v + k
        return v if self.i is None else v + self.i * self.per[sem]

    def next(self, sem, k=1):
        self.now(sem, k)
        return self.now(sem)

    @contextmanager
    def loop(self, eng, times, per):
        start = {s: self.n.get(s, 0) for s in per}
        with eng.Fori(0, times) as i:
            self.i, self.per = i, per
            yield i
        self.i, self.per = None, {}
        for s, k in per.items():
            assert self.n.get(s, 0) == start[s] + k, (s, self.n.get(s, 0) - start[s], k)
            self.n[s] = start[s] + times * k


class Section:

    def __init__(self, n, chunks, tiles, loads, used):
        self.n, self.chunks = n, chunks
        self.tiles, self.loads, self.used = tuple(tiles), tuple(loads), tuple(used)


def plan_weights():
    first = [("aqk", 2), ("av", 2), ("alr", 1), ("ag", 2), ("bq", 2), ("bkv", 1), ("bg", 2),
             ("cqk", 4), ("cv", 2), ("cg", 2), ("merge", 12), ("wo", 4)]
    second = [("cval", 2), ("cgate", 2), ("qkv", 6), ("z", 2), ("ba", 1), ("wout2", 4),
              ("gu", 2 * D_FF2 // TW), ("down2", 4)]
    third = [("qka", 3), ("va", 2), ("qi", 1), ("kwi", 1), ("qkm", 3), ("vm", 2), ("om", 2), ("if", 1),
             ("qkc", 2), ("vc", 1), ("wout3", 4), ("up3", D_FF3 // TW), ("down3", 4)]
    tiles, loads, used, plan = [0, 0], [0] * RING, [0] * RING, {}
    for name, n in first + second + third:
        chunks = {"down2": 6, "down3": 8}.get(name, 2)
        plan[name] = Section(n, chunks, tiles, loads, used)
        if name == "merge":
            tiles = [t + n for t in tiles]
            loads = [loads[0] + n, loads[1] + n, loads[2] + n, loads[3]]
        elif chunks > 2:
            tiles = [t + n // 2 for t in tiles]
            for c in range(chunks):
                loads[c % RING] += n
                used[c % RING] += n * (c < chunks - 1)
        else:
            k = ((n + 1) // 2, n // 2)
            tiles = [tiles[0] + k[0], tiles[1] + k[1]]
            per = {"bkv": 5, "kwi": 3}.get(name, 1)
            loads = [loads[s] + per * k[s // 2] for s in range(RING)]
    return plan


def tiles_of(eng, n):
    pairs = n // 2
    if pairs > 1:
        with eng.Fori(0, pairs) as i:
            for u in (0, 1):
                yield 2 * i + u, u, i
    elif pairs:
        yield 0, 0, 0
        yield 1, 1, 0
    if n % 2:
        yield n - 1, 0, pairs


def build(nc, I, out):
    plan = plan_weights()
    ctx = ExitStack()
    with ctx:
        def sb(name, shape, dt=F32):
            return ctx.enter_context(nc.sbuf_tensor(name, shape, dt))

        def sem(name):
            return ctx.enter_context(nc.semaphore(name))

        ring = sb("ring", [P, RING, CH, TW])
        xT = sb("xT", [P, KT, S])
        xtok = sb("xtok", [P, 2, D])
        ln_gb = sb("ln_gb", [P, 2, D])
        ARENA = 20480
        arena = sb("arena", [P, ARENA])
        ident = sb("ident", [P, P])
        ones = sb("ones", [P, P])
        upper = sb("upper", [P, S])
        causal = sb("causal", [P, 384])
        band = sb("band", [P, 384])
        causalT = sb("causalT", [P, 384])
        ndist = sb("ndist", [P, 384])
        levels = sb("levels", [P, 7, P])
        colp = sb("colp", [P, 8, R_ALL])
        bmc = sb("bmc", [P, 3, KT])
        small = sb("small", [P, 512])
        alrT = arena[0:G_RANK, 19456:19456 + S]
        gwu = arena[0:G_RANK, 19712:19712 + 512]
        ps = ctx.enter_context(nc.psum_tensor("ps", [P, 8, 512], F32))

        def area(at, *shape):
            n = int(np.prod(shape))
            assert at + n <= ARENA, (at, shape)
            v = arena[:, at:at + n]
            if len(shape) == 2:
                v = v.rearrange("p (a b) -> p a b", b=shape[1])
            elif len(shape) == 3:
                v = v.rearrange("p (a b c) -> p a b c", b=shape[1], c=shape[2])
            return v

        def cols(at, n):
            return small[:, at:at + n]

        eps_ln, eps_rms, one, eps_diff = cols(0, 1), cols(1, 1), cols(2, 1), cols(3, 1)
        sinks = cols(4, 16)
        lam = cols(20, 12)
        gdnA, gdndt = cols(32, 8), cols(40, 8)
        bib, bfb = cols(48, 6), cols(54, 6)
        slopes_a, slopes_c = cols(60, 6), cols(66, 4)
        stat = cols(72, 64)
        nmax, rsum, rinv, esink = cols(136, 4), cols(140, 4), cols(144, 4), cols(148, 4)
        tokc = cols(160, 128)

        w_landed = [sem(f"w_landed{s}") for s in range(RING)]
        w_used = [sem(f"w_used{s}") for s in range(RING)]
        tile_done = [sem(f"tile_done{u}") for u in range(2)]
        tile_free = [sem(f"tile_free{u}") for u in range(2)]
        x_landed, par_landed, ln_landed = sem("x_landed"), sem("par_landed"), sem("ln_landed")
        out_written = sem("out_written")
        iotas, consts = sem("iotas"), sem("consts")
        dve_order, act_order, pool_order = sem("dve_order"), sem("act_order"), sem("pool_order")
        table_ready, tableT_ready, table_zeroed = sem("table_ready"), sem("tableT_ready"), sem("table_zeroed")
        x_ready, xTp_ready, xTp_used = sem("x_ready"), sem("xTp_ready"), sem("xTp_used")
        var_ready, std_ready = sem("var_ready"), sem("std_ready")
        stage_over = sem("stage_over")
        gate_ready = sem("gate_ready")
        staged = sem("staged")
        logits_ready, logits_used = sem("logits_ready"), sem("logits_used")
        max_ready, exp_done, probs_ready = sem("max_ready"), sem("exp_done"), sem("probs_ready")
        probsT_ready, probsT_out, o_ready, o_used = sem("probsT_ready"), sem("probsT_out"), sem("o_ready"), sem("o_used")
        FREE = {logits_used: 1, o_used: 1, o_ready: 1}
        sq_ready, ss_ready, root_ready = sem("sq_ready"), sem("ss_ready"), sem("root_ready")
        mm_ready, mm_used, vec_ready, act_ready = sem("mm_ready"), sem("mm_used"), sem("vec_ready"), sem("act_ready")
        fac_ready, fac_used = sem("fac_ready"), sem("fac_used")
        lam_landed, hid_ready = sem("lam_landed"), sem("hid_ready")
        conv_ready, silu_done = sem("conv_ready"), sem("silu_done")
        lm_ready, xp_ready, xs_ready, yp_ready, inv_ready = (sem(k) for k in (
            "lm_ready", "xp_ready", "xs_ready", "yp_ready", "inv_ready"))

        y1 = area(0, 24, S)
        mergedT = area(6144, KT, S)
        sig, mtmp = area(10240, 4, S), area(11264, 4, S)
        a_qk, a_v, a_gate = area(6144, 8, S), area(8192, 2, BW), area(10240, 8, S)
        a_b, a_e = area(12288, 4, S), area(13312, 2, 4, S)
        a_qe = area(15360, 2, 4, S)
        a_ke = area(17408, 2, 4, S)
        a_sq, a_rn = area(13312, 8, S), area(15360, 4, S)
        a_at = ln_gb[:, 0, 0:4 * 384].rearrange("p (h n) -> p h n", h=4)
        s_q, s_kd, s_v, s_gate = area(6144, 8, S), area(8192, 2, S), area(10240, 2, P), area(12288, 8, S)
        m_qk, m_v, m_gate = area(6144, 16, S), area(10240, 2, BW), area(12288, 8, S)
        AT1 = 14336
        y2 = area(0, KT, S)
        c_qkv, c_z = area(4096, 24, S), area(10240, 8, S)
        HP, RP = CONV_W - 1, SHORT_W - 1
        c_h = area(12288, 8, HP + S)
        c_acc = area(14576, 8, S)
        c_raw = area(16624, 2, 4, RP + S)
        c_sq = area(12288, 8, S)
        c_mu, c_rs = area(18696, S), area(18952, S)
        l2_sq, l2_rn = xT, area(12288, 16, S)
        d_at, d_lt, d_l21 = area(12288, 8, 384), area(15360, 16, P), area(17408, 8, P)
        d_xs = area(18432, 16, P)
        d_lm = ln_gb[:, 1, :].rearrange("p (a b) -> p a b", b=P)
        d_dt = ln_gb[:, 1, 0:768].rearrange("p (a b) -> p a b", b=384)
        d_db = ln_gb[:, 1, 768:1536].rearrange("p (a b) -> p a b", b=384)
        d_vb = ln_gb[:, 0, :].rearrange("p (t n) -> p t n", t=2)
        d_t = xT[:, 0:8, :].rearrange("p a (c i) -> p (a c) i", c=2)
        d_tt = xT[:, 8:16, :].rearrange("p a (c i) -> p (a c) i", c=2)
        d_vn = area(8192, 2, 1024)
        d_sq, d_rn = xT[:, 0:8, :], xT[:, 8:16, :]
        hid = area(0, D_FF3 // P, S)
        f_sg = area(16384, 2, 4, S)
        t_ba = tokc[:, 0:32].rearrange("p (t c) -> p t c", t=2)
        t_beta = tokc[:, 32:48].rearrange("p (t c) -> p t c", t=2)
        t_x = tokc[:, 48:64].rearrange("p (t c) -> p t c", t=2)
        t_e = tokc[:, 64:80].rearrange("p (t c) -> p t c", t=2)
        t_A = tokc[:, 80:88]
        t_g = tokc[:, 88:104].rearrange("p (t c) -> p t c", t=2)
        t_gc = tokc[:, 104:120].rearrange("p (t c) -> p t c", t=2)
        scw = small[:, 288:384].rearrange("p (k c) -> p k c", k=SHORT_W)
        y3 = area(0, KT, S)
        e_qk, e_v, e_gate = area(4096, 12, S), area(7168, 2, 768), area(8704, 6, S)
        AT3 = 10240
        i_q, i_k = area(14080, 4, S), area(15104, S)
        i_sel, i_work, i_tmp = area(15360, 384), area(15744, 384), area(16128, 384)
        e_raw = area(14080, 2, 4, RP + S)
        e_bbc = area(16896, 6, S)
        e_cut, e_fits = area(16896, 4, S), area(17920, 4, S)
        e_sq, e_rn = area(AT3, 6, S), area(AT3 + 1536, 6, S)
        lam_rows = area(18944, 4, 64)
        lam_prod = area(19200, 2, 64)
        t_w = tokc[:, 0:16].rearrange("p (t c) -> p t c", t=2)
        top8 = tokc[:, 16:32].rearrange("p (t c) -> p t c", t=2)
        t_if = tokc[:, 32:56].rearrange("p (t c) -> p t c", t=2)
        t_lf = tokc[:, 56:68].rearrange("p (t c) -> p t c", t=2)
        t_ef = tokc[:, 68:80].rearrange("p (t c) -> p t c", t=2)
        t_na = tokc[:, 80:92].rearrange("p (t c) -> p t c", t=2)
        mcw = small[:, 384:432].rearrange("p (k c) -> p k c", k=SHORT_W)
        table = area(0, 1024)
        row = "(k p) c -> p k c"

        block = ctx.enter_context(nc.Block())

        class Heads:

            def __init__(self, kind, pairs, d, dv, at):
                self.kind, self.pairs, self.d, self.dv = kind, pairs, d, dv
                self.qs, self.ks = area(at, 2, S), area(at + 512, 2, S)
                self.vs = area(at + 1024, 2, 2, P)
                self.sm = area(at + 1536, 2, 384)
                self.p = area(at + 2304, 2, 384)
                self.pT = area(at + 3072, 2, 384)
                self.outs = 1 if kind == "diff" else 2
                self.halves = kind in ("swa", "diff")

            def at(self, u):
                return (64 * u, 64 * u + 64) if self.halves else (0, P)

        swa = [Heads("swa", 4, 64, 64, AT1) for _ in range(2)]
        moba = Heads("moba", 4, P, P, AT1)
        dsa = Heads("dsa", A_H // 2, P, P, AT3)
        mls = Heads("mlstm", M_H // 2, P, P, AT3)
        dif = Heads("diff", D_H, 64, P, AT3)

        @block.sync
        def _(sp):
            n = Count(FREE)

            def held(v):
                return v if isinstance(v, int) else sp.snap(v)

            def load(slot, want, src, width, landed=1):
                sp.dma_start(ring[:, slot, 0:src.shape[1], want:want + width], src).then_inc(w_landed[slot], 16)

            def tile_loads(name, w, col, width=TW, second=None):
                sec = plan[name]
                for t, u, it in tiles_of(sp, sec.n):
                    at = held(col + t * width if second is None else col + u * second + it * width)
                    sp.wait_ge(tile_done[u], sec.tiles[u] + it)
                    for c in range(2):
                        load(2 * u + c, 0, w[c * CH * P:(c + 1) * CH * P, ds(at, width)].rearrange(row, p=P), width)

            def piece_loads(name, w, pieces):
                sec = plan[name]
                sp.wait_ge(tile_done[0], sec.tiles[0])
                for c in range(2):
                    at = 0
                    for col, width in pieces:
                        load(c, at, w[c * CH * P:(c + 1) * CH * P, col:col + width].rearrange(row, p=P), width)
                        at += width

            def down_loads(name, w, kt):
                sec = plan[name]
                nch = sec.chunks
                per = [sum(1 for c in range(nch - 1) if c % RING == s) for s in range(RING)]
                last = [max(c for c in range(nch) if c % RING == s) for s in range(RING)]
                for t, u, it in tiles_of(sp, sec.n):
                    at = held(t * TW)
                    for c in range(nch):
                        s = c % RING
                        if c >= RING:
                            sp.wait_ge(w_used[s], sec.used[s] + per[s] * t + c // RING)
                        elif last[s] < nch - 1:
                            sp.wait_ge(tile_done[s // 2], sec.tiles[s // 2])
                            sp.wait_ge(w_used[s], sec.used[s] + per[s] * t)
                        elif u == 0:
                            sp.wait_ge(tile_done[s // 2], sec.tiles[s // 2])
                            sp.wait_ge(tile_done[1], sec.tiles[1] + it)
                        else:
                            sp.wait_ge(tile_done[0], sec.tiles[0] + it + 1)
                        k0, k1 = c * CH, min((c + 1) * CH, kt)
                        load(s, 0, w[k0 * P:k1 * P, ds(at, TW)].rearrange(row, p=P), TW)

            w = I["w_in"]
            tile_loads("aqk", w, C_AQ)
            tile_loads("av", w, C_AV)
            piece_loads("alr", w, [(C_ALR, G_RANK)])
            tile_loads("ag", w, C_AG)
            tile_loads("bq", w, C_BQ)
            piece_loads("bkv", w, [(C_BK, 64), (C_BK, 64), (C_BK + 64, 64), (C_BK + 64, 64), (C_BV, 128)])
            tile_loads("bg", w, C_BG)
            tile_loads("cqk", w, C_CQ)
            tile_loads("cv", w, C_CV)
            tile_loads("cg", w, C_CG)
            sec = plan["merge"]
            with sp.Fori(0, 4) as j:
                for b in range(3):
                    gate_at = held(C_MG + b * D + j * TW)
                    sp.wait_ge(tile_done[0], sec.tiles[0] + 3 * j + b)
                    for c in range(2):
                        load(c, 0, w[c * CH * P:(c + 1) * CH * P, ds(gate_at, TW)].rearrange(row, p=P), TW)
            tile_loads("wo", I["w_o"], 0)
            w = I["w_in_2"]
            tile_loads("cval", w, 0)
            tile_loads("cgate", w, 1024)
            tile_loads("qkv", w, C_QKV2)
            tile_loads("z", w, C_Z2)
            piece_loads("ba", w, [(C_BA2, 16)])
            tile_loads("wout2", I["w_out_2"], 0)
            tile_loads("gu", I["w_gate_up_2"], 0, second=D_FF2)
            down_loads("down2", I["w_down_2"], D_FF2 // P)
            w = I["w_in_3"]
            sp.wait_ge(tile_done[1], plan["qka"].tiles[1])
            tile_loads("qka", w, 0)
            tile_loads("va", w, C_VA, 384)
            tile_loads("qi", w, C_QI)
            piece_loads("kwi", w, [(C_KI, 64), (C_KI, 64), (C_WI, 8)])
            tile_loads("qkm", w, C_QM)
            tile_loads("vm", w, C_VM, 384)
            tile_loads("om", w, C_OM, 384)
            piece_loads("if", w, [(C_IF, 12)])
            tile_loads("qkc", w, C_QC)
            tile_loads("vc", w, C_VC)
            tile_loads("wout3", I["w_out_3"], 0)
            tile_loads("up3", I["w_up_3"], 0)
            down_loads("down3", I["w_down_3"], D_FF3 // P)
            sp.wait_ge(x_ready, 6)
            sp.dma_start(out.rearrange("(t p) c -> p t c", p=P), xtok[:]).then_inc(out_written, 16)
            sp.wait_ge(out_written, 16)

        posi = area(2048, P)
        posj = area(2048 + P, P)
        posx = area(2048 + 2 * P, P)
        posy = area(2048 + 3 * P, P)

        @block.gpsimd
        def _(pool):
            n = Count(FREE)
            pool.iota(posi.bitcast(I32), [[1, P]], base=0, channel_multiplier=0).then_inc(iotas, 1)
            pool.iota(posj.bitcast(I32), [[0, P]], base=0, channel_multiplier=1).then_inc(iotas, 1)

            def stage_pair(A, items):
                pool.wait_ge(o_ready, n.now(o_ready, 1))
                for dst, src in items[:-1]:
                    pool.tensor_copy(dst, src)
                pool.tensor_copy(*items[-1]).then_inc(staged, 1)

            def stage_heads(A, q, k, v, koff):
                pool.wait_ge(gate_ready, n.next(gate_ready))
                with n.loop(pool, A.pairs, {o_ready: 1}) as i:
                    items = []
                    for u in range(A.outs):
                        h = A.outs * i + u
                        items += [(A.qs[:, u], q[:, ds(h, 1), :].rearrange("p a s -> p (a s)")),
                                  (A.ks[:, u], k[:, ds(koff + h, 1), :].rearrange("p a s -> p (a s)")),
                                  (A.vs[:, u], v[:, :, ds(h * A.dv, A.dv)])]
                    stage_pair(A, items)

            def stage_swa(A, g):
                if g == 0:
                    pool.wait_ge(gate_ready, n.next(gate_ready))
                with n.loop(pool, A.pairs, {o_ready: 1}) as i:
                    stage_pair(A, [(A.qs[:, 0], s_q[:, ds(4 * g + i, 1), :].rearrange("p a s -> p (a s)"))])

            for g in range(2):
                stage_swa(swa[g], g)
            stage_heads(moba, m_qk, m_qk, m_v, 8)
            stage_heads(dsa, e_qk, e_qk, e_v, 6)
            stage_heads(mls, e_qk, e_qk, e_v, 6)
            stage_heads(dif, e_qk, e_qk, e_v, 4)

        @block.tensor
        def _(pe):
            n = Count(FREE)

            def chunk(sec, slot, it, per=1, more=0):
                pe.wait_ge(w_landed[slot], (sec.loads[slot] + it * per + more + 1) * 16)

            def tile_F(u, src, width, kt=KT, waits=lambda c: None, slots=None):
                slots = slots or (2 * u, 2 * u + 1)
                for cb in range(width // P):
                    for k in range(kt):
                        if cb == 0 and k % CH == 0:
                            waits(k // CH)
                        last = pe.matmul(ps[:, 2 * u + cb // 2, (cb % 2) * S:(cb % 2) * S + S],
                                         ring[:, slots[k // CH], k % CH, cb * P:(cb + 1) * P], src[:, k, :],
                                         start=(k == 0), stop=(k == kt - 1))
                return last

            def tile_T(u, src, width, waits):
                for k in range(KT):
                    if k % CH == 0:
                        waits(k // CH)
                    for t in range(2):
                        last = pe.matmul(ps[:, 2 * u + t, 0:width], src[:, k, t * P:(t + 1) * P],
                                         ring[:, 2 * u + k // CH, k % CH, 0:width],
                                         start=(k == 0), stop=(k == KT - 1))
                return last

            def project(name, kind, src=xT, width=TW):
                sec = plan[name]
                for t, u, it in tiles_of(pe, sec.n):
                    pe.wait_ge(tile_free[u], sec.tiles[u] + it)
                    waits = lambda c: chunk(sec, 2 * u + c, it)
                    last = (tile_F if kind == "F" else tile_T)(u, src, width, waits=waits)
                    last.then_inc(tile_done[u], 1)

            def project_pieces(name, ops, npieces, src=xT):
                sec = plan[name]
                pe.wait_ge(tile_free[0], sec.tiles[0])
                for c in range(2):
                    pe.wait_ge(w_landed[c], (sec.loads[c] + npieces) * 16)
                for kind, col, m, bank, at in ops:
                    if kind == "F":
                        for k in range(KT):
                            last = pe.matmul(ps[0:m, bank, at:at + S], ring[:, k // CH, k % CH, col:col + m],
                                             src[:, k, :], start=(k == 0), stop=(k == KT - 1))
                    else:
                        for t in range(2):
                            for k in range(KT):
                                last = pe.matmul(ps[:, bank, at + t * m:at + t * m + m], src[:, k, t * P:(t + 1) * P],
                                                 ring[:, k // CH, k % CH, col:col + m],
                                                 start=(k == 0), stop=(k == KT - 1))
                last.then_inc(tile_done[0], 1)

            def transpose_x():
                pe.wait_ge(x_ready, n.next(x_ready))
                for g in range(KT // 2):
                    pe.wait_ge(xTp_used, max(0, n.now(xTp_used, 1) - 3))
                    for k in range(2):
                        for t in range(2):
                            last = pe.transpose(ps[:, 4 + g % 4, k * S + t * P:k * S + (t + 1) * P],
                                                xtok[:, t, (2 * g + k) * P:(2 * g + k + 1) * P], ident[:])
                    last.then_inc(xTp_ready, 1)

            def attend(A, k_of, v_of, first=True, stages=True):
                with n.loop(pe, A.pairs, {staged: 1, logits_used: 2, probs_ready: A.outs, probsT_out: A.outs, o_used: 1}):
                    pe.wait_ge(staged, n.next(staged))
                    pe.wait_ge(logits_used, n.now(logits_used, 2))
                    for u in range(2):
                        a, b = A.at(u)
                        q = A.qs[a:b, 0 if A.halves else u]
                        k = k_of(u)
                        pe.matmul(ps[:, 4 + u, 0:P], q[:, 0:P], k[:, 0:P], start=True, stop=True)
                        pe.matmul(ps[:, 4 + u, P:384], q[:, P:S], k[:, 0:S], start=True, stop=True).then_inc(logits_ready, 1)
                    for u in range(A.outs):
                        pe.wait_ge(probs_ready, n.next(probs_ready))
                        for c in range(3):
                            last = pe.transpose(ps[:, 6 + u, c * P:(c + 1) * P], A.p[:, u, c * P:(c + 1) * P], ident[:])
                        last.then_inc(probsT_ready, 1)
                    pe.wait_ge(o_used, n.now(o_used, 1))
                    for u in range(A.outs):
                        pe.wait_ge(probsT_out, n.next(probsT_out))
                        a, b = A.at(u)
                        o = ps[a:b, 2, 0:S] if A.kind == "swa" else ps[:, 2 + u, 0:S]
                        v = v_of(u)
                        pe.matmul(o, v[:, 0, :], A.pT[:, u, 0:S], start=True, stop=False)
                        last = pe.matmul(o[:, P:S], v[:, 1, :], A.pT[:, u, S:384], start=False, stop=True)
                    last.then_inc(o_ready, 1)
                pe.wait_ge(o_used, n.now(o_used))

            def square_sums(src, heads, tiles):
                pe.wait_ge(sq_ready, n.next(sq_ready))
                for g in range(heads // 2):
                    if g >= 4:
                        pe.wait_ge(root_ready, n.next(root_ready))
                    for e in range(tiles):
                        v = src[:, 2 * g * tiles:(2 * g + 2) * tiles, :].rearrange("p (h e) s -> p h e s", e=tiles)
                        last = pe.matmul(ps[:, 4 + g % 4, :].rearrange("p (h s) -> p h s", h=2), ones[:], v[:, :, e, :],
                                         start=(e == 0), stop=(e == tiles - 1))
                    last.then_inc(ss_ready, 1)
                pe.wait_ge(root_ready, n.next(root_ready, min(4, heads // 2)))

            def hidden_down(name, kt):
                sec = plan[name]
                nch = sec.chunks
                per = [sum(1 for c in range(nch) if c % RING == s) for s in range(RING)]
                for t, u, it in tiles_of(pe, sec.n):
                    pe.wait_ge(tile_free[u], sec.tiles[u] + it)
                    if u == 0:
                        pe.wait_ge(tile_free[1], sec.tiles[1])
                    for c in range(nch):
                        s = c % RING
                        pe.wait_ge(w_landed[s], (sec.loads[s] + t * per[s] + c // RING + 1) * 16)
                        for k in range(c * CH, min((c + 1) * CH, kt)):
                            for h in range(2):
                                last = pe.matmul(ps[:, 2 * u + h, :], hid[:, k, h * P:(h + 1) * P], ring[:, s, k % CH, :],
                                                 start=(k == 0), stop=(k == kt - 1))
                        last.then_inc(w_used[s] if c < nch - 1 else tile_done[u], 1)

            pe.sem_inc(o_ready, 1)
            pe.wait_ge(consts, 1)
            pe.wait_ge(par_landed, 16 * 18)
            for t in range(8):
                last = pe.transpose(ps[:, 0, t * R_ALL:(t + 1) * R_ALL], table[0:R_ALL, t * P:(t + 1) * P],
                                    ident[0:R_ALL, 0:R_ALL])
            last.then_inc(tableT_ready, 1)
            transpose_x()
            pe.wait_ge(xTp_used, n.now(xTp_used))
            pe.wait_ge(table_ready, 1)

            project("aqk", "F")
            project("av", "T")
            project_pieces("alr", [("F", 0, G_RANK, 0, 0)], 1)
            project("ag", "F")
            pe.wait_ge(vec_ready, n.next(vec_ready))
            for h in range(G_H):
                last = pe.matmul(ps[:, 4 + h // 2, (h % 2) * S:(h % 2 + 1) * S], gwu[:, h * P:(h + 1) * P], alrT,
                                 start=True, stop=True)
            last.then_inc(mm_ready, 1)
            for lv in range(8):
                pe.wait_ge(fac_ready, n.next(fac_ready))
                b = 4 + 2 * (lv % 2)
                if lv < 7:
                    pe.wait_ge(mm_used, max(0, n.now(mm_used, 1) - 1))
                    for h in range(G_H):
                        for c in range(2):
                            last = pe.matmul(ps[:, b + h // 2, (h % 2) * S + c * P:(h % 2) * S + (c + 1) * P],
                                             a_ke[:, lv % 2, h, c * P:(c + 1) * P], a_qe[:, lv % 2, h, c * P:(c + 1) * P],
                                             start=True, stop=True)
                else:
                    pe.wait_ge(mm_used, max(0, n.now(mm_used, 1) - 1))
                    for h in range(G_H):
                        last = pe.matmul(ps[:, b, h * P:(h + 1) * P], a_ke[:, 1, h, 0:P], a_qe[:, 1, h, P:S],
                                         start=True, stop=True)
                last.then_inc(mm_ready, 1)
            pe.wait_ge(fac_ready, n.next(fac_ready))
            pe.wait_ge(mm_used, max(0, n.now(mm_used, 1) - 1))
            for h in range(G_H):
                for c in range(2):
                    last = pe.matmul(ps[:, 4 + h // 2, (h % 2) * S + c * P:(h % 2) * S + (c + 1) * P],
                                     a_qk[:, 4 + h, c * P:(c + 1) * P], a_qe[:, 0, h, c * P:(c + 1) * P],
                                     start=True, stop=True)
            last.then_inc(mm_ready, 1)
            pe.wait_ge(mm_used, n.now(mm_used))
            for h in range(G_H):
                for e in range(2):
                    o = ps[:, 4 + h, e * S:(e + 1) * S]
                    v = a_v[:, :, h * S + e * P:h * S + (e + 1) * P]
                    pe.matmul(o, v[:, 0, :], a_at[:, h, 0:S], start=True, stop=False)
                    last = pe.matmul(o[:, P:S], v[:, 1, :], a_at[:, h, S:384], start=False, stop=True)
            last.then_inc(mm_ready, 1)
            square_sums(a_sq, G_H, 2)

            pe.wait_ge(stage_over, 1)
            project("bq", "F")
            project_pieces("bkv", [("F", 0, P, 0, 0), ("F", P, P, 0, S), ("T", 2 * P, P, 1, 0)], 5)
            project("bg", "F")
            pe.wait_ge(gate_ready, n.next(gate_ready))
            for g in range(2):
                attend(swa[g], lambda u: s_kd[64 * u:64 * u + 64, g], lambda u: s_v[:, :, g * 64:(g + 1) * 64])

            project("cqk", "F")
            project("cv", "T")
            project("cg", "F")
            attend(moba, lambda u: moba.ks[:, u], lambda u: moba.vs[:, u])

            sec = plan["merge"]
            with pe.Fori(0, 4) as j:
                for b in range(3):
                    it = 3 * j + b
                    pe.wait_ge(tile_free[0], sec.tiles[0] + it)
                    tile_F(0, xT, TW, waits=lambda c: pe.wait_ge(w_landed[c], (sec.loads[c] + it + 1) * 16))\
                        .then_inc(tile_done[0], 1)
                    pe.wait_ge(tile_free[1], sec.tiles[1] + it)
                    tile_F(1, y1[:, 8 * b:8 * b + 8], TW, kt=8, slots=(2,),
                           waits=lambda c: pe.wait_ge(w_landed[2], (sec.loads[2] + it + 1) * 16))\
                        .then_inc(tile_done[1], 1)
            pe.wait_ge(stage_over, 4)
            project("wo", "T", mergedT)
            transpose_x()
            pe.wait_ge(xTp_used, n.now(xTp_used))
            project("cval", "F")
            project("cgate", "F")
            project("qkv", "F")
            project("z", "F")
            project_pieces("ba", [("T", 0, 16, 0, 0)], 1)
            for b, src in ((4, c_acc), (5, c_sq)):
                pe.wait_ge(conv_ready, n.next(conv_ready))
                for t in range(8):
                    last = pe.matmul(ps[:, b, 0:S], ones[:], src[:, t, :], start=(t == 0), stop=(t == 7))
                last.then_inc(mm_ready, 1)
            square_sums(l2_sq, 16, 1)
            pe.wait_ge(fac_ready, n.next(fac_ready))
            pe.matmul(ps[:, 0, 0:8], upper[:, 0:P], t_g[:, 0], start=True, stop=True)
            pe.matmul(ps[:, 0, 8:16], ones[:], t_g[:, 0], start=True, stop=False)
            pe.matmul(ps[:, 0, 8:16], upper[:, 0:P], t_g[:, 1], start=False, stop=True)
            for t in range(2):
                for h in range(GD_H):
                    last = pe.transpose(ps[:, 4 + 2 * t + h // 4, (h % 4) * P:(h % 4 + 1) * P],
                                        c_qkv[:, 16 + h, t * P:(t + 1) * P], ident[:])
            last.then_inc(mm_ready, 1)
            pe.wait_ge(fac_ready, n.next(fac_ready))
            for h in range(GD_H):
                b = 2 + 3 * (h % 2)
                if h >= 2:
                    pe.wait_ge(fac_ready, n.next(fac_ready))
                g = [t_g[:, t, h:h + 1].to_broadcast([P, P]) for t in range(2)]
                beta = [t_beta[:, t, h:h + 1].to_broadcast([P, P]) for t in range(2)]
                pe.matmul(ps[:, b, 0:S], g[0], upper[:], start=True, stop=False)
                pe.matmul(ps[:, b, P:S], g[1], upper[:, 0:P], start=False, stop=True)
                for t in range(2):
                    pe.matmul(ps[:, b, S + t * P:S + (t + 1) * P], beta[t], ident[:], start=True, stop=True)
                q, k = c_qkv[:, h], c_qkv[:, 8 + h]
                for c, r in ((1, k), (2, q)):
                    pe.matmul(ps[:, b + c, 0:S], k[:, 0:P], r, start=True, stop=True)
                    last = pe.matmul(ps[:, b + c, S:384], k[:, P:S], r[:, P:S], start=True, stop=True)
                last.then_inc(mm_ready, 1)
            pe.wait_ge(fac_ready, n.next(fac_ready, 2))
            pe.wait_ge(inv_ready, n.next(inv_ready, 4))
            with n.loop(pe, 7, {lm_ready: 4, xs_ready: 4, inv_ready: 4}):
                for g in range(4):
                    pe.wait_ge(lm_ready, n.next(lm_ready))
                    for e in range(4):
                        last = pe.matmul(ps[:, g, e * P:(e + 1) * P], d_lm[:, 4 * g + e], d_t[:, 4 * g + e],
                                         start=True, stop=True)
                    last.then_inc(xp_ready, 1)
                for g in range(4):
                    pe.wait_ge(xs_ready, n.next(xs_ready))
                    if g >= 2:
                        pe.wait_ge(inv_ready, n.next(inv_ready))
                    for e in range(4):
                        pe.matmul(ps[:, 4 + g % 2, e * P:(e + 1) * P], d_tt[:, 4 * g + e], d_xs[:, 4 * g + e],
                                  start=True, stop=True)
                    for e in range(4):
                        last = pe.matmul(ps[:, 6 + g % 2, e * P:(e + 1) * P], d_xs[:, 4 * g + e], d_tt[:, 4 * g + e],
                                         start=True, stop=True)
                    last.then_inc(yp_ready, 1)
                pe.wait_ge(inv_ready, n.next(inv_ready, 2))
            def by_head(b, left, right):
                for h in range(GD_H):
                    last = pe.matmul(ps[:, b + h // 4, (h % 4) * P:(h % 4 + 1) * P], left(h), right(h),
                                     start=True, stop=True)
                last.then_inc(mm_ready, 1)
            head = lambda v, t: lambda h: v[:, t, h * P:(h + 1) * P]
            by_head(0, lambda h: d_tt[:, 2 * h], head(d_vb, 0))
            pe.wait_ge(fac_ready, n.next(fac_ready))
            by_head(2, lambda h: d_l21[:, h], head(d_vn, 0))
            pe.wait_ge(fac_ready, n.next(fac_ready))
            by_head(0, lambda h: d_tt[:, 2 * h + 1], head(d_vb, 1))
            pe.wait_ge(fac_ready, n.next(fac_ready))
            for h in range(GD_H):
                o = ps[:, 4 + h // 2, (h % 2) * S:(h % 2 + 1) * S]
                pe.matmul(o, d_vn[:, 0, h * P:(h + 1) * P], d_at[:, h, 0:S], start=True, stop=False)
                last = pe.matmul(o[:, P:S], d_vn[:, 1, h * P:(h + 1) * P], d_at[:, h, S:384], start=False, stop=True)
            last.then_inc(mm_ready, 1)
            square_sums(d_sq, GD_H, 1)
            pe.wait_ge(stage_over, 5)
            project("wout2", "T", y2)
            transpose_x()
            pe.wait_ge(xTp_used, n.now(xTp_used))
            project("gu", "F")
            hidden_down("down2", D_FF2 // P)
            transpose_x()
            pe.wait_ge(xTp_used, n.now(xTp_used))
            project("qka", "F")
            project("va", "T", width=384)
            project("qi", "F")
            project_pieces("kwi", [("F", 0, P, 0, 0), ("T", P, 8, 0, S)], 3)
            pe.wait_ge(fac_ready, 23)
            for h in range(8):
                b = 4 + h % 4
                if h >= 4:
                    pe.wait_ge(mm_used, n.next(mm_used))
                q, k = i_q[64 * (h % 2):64 * (h % 2) + 64, h // 2], i_k[64 * (h % 2):64 * (h % 2) + 64]
                pe.matmul(ps[:, b, 0:P], q[:, 0:P], k[:, 0:P], start=True, stop=True)
                pe.matmul(ps[:, b, P:384], q[:, P:S], k, start=True, stop=True).then_inc(mm_ready, 1)
            pe.wait_ge(mm_used, n.next(mm_used, 4))
            attend(dsa, lambda u: dsa.ks[:, u], lambda u: dsa.vs[:, u])
            project("qkm", "F")
            project("vm", "T", width=384)
            project("om", "F", width=384)
            project_pieces("if", [("T", 0, 12, 0, 0)], 1)
            pe.wait_ge(fac_ready, 24)
            pe.matmul(ps[:, 0, 0:6], upper[:, 0:P], t_lf[:, 0], start=True, stop=True)
            pe.matmul(ps[:, 0, 6:12], ones[:], t_lf[:, 0], start=True, stop=False)
            pe.matmul(ps[:, 0, 6:12], upper[:, 0:P], t_lf[:, 1], start=False, stop=True).then_inc(mm_ready, 1)
            for h in range(M_H):
                o = ps[:, 4 + h // 2, (h % 2) * S:(h % 2 + 1) * S]
                lf = [t_ef[:, t, h:h + 1].to_broadcast([P, P]) for t in range(2)]
                li = [t_if[:, t, h:h + 1].to_broadcast([P, P]) for t in range(2)]
                pe.matmul(o, lf[0], upper[:], start=True, stop=False)
                pe.matmul(o[:, P:S], lf[1], upper[:, 0:P], start=False, stop=False)
                pe.matmul(o[:, 0:P], li[0], ident[:], start=False, stop=False)
                last = pe.matmul(o[:, P:S], li[1], ident[:], start=False, stop=True)
            last.then_inc(mm_ready, 1)
            pe.wait_ge(mm_used, n.next(mm_used))
            attend(mls, lambda u: mls.ks[:, u], lambda u: mls.vs[:, u])
            square_sums(e_sq, M_H, 1)
            project("qkc", "F")
            project("vc", "T")
            attend(dif, lambda u: dif.ks[64 * u:64 * u + 64, 0], lambda u: dif.vs[:, 0])
            square_sums(e_sq, D_H, 1)
            pe.wait_ge(stage_over, 8)
            project("wout3", "T", y3)
            transpose_x()
            pe.wait_ge(xTp_used, n.now(xTp_used))
            project("up3", "F")
            pe.wait_ge(hid_ready, plan["up3"].n)
            hidden_down("down3", D_FF3 // P)

        @block.scalar
        def _(act):
            n = Count(FREE)

            def link(ins):
                ins.then_inc(act_order, 1)
                act.wait_ge(act_order, n.next(act_order))

            act.dma_start(xtok[:], I["x"].rearrange("(t p) c -> p t c", p=P)).then_inc(x_landed, 16)
            act.wait_ge(table_zeroed, 1)
            for dst, src in [
                (table[R_DWW:R_DWW + CONV_W, :], I["conv_dw_w_2"]),
                (table[R_DWB:R_DWB + 1, :], I["conv_dw_b_2"]),
                (table[R_CLG:R_CLG + 1, :], I["conv_ln_g_2"]),
                (table[R_CLB:R_CLB + 1, :], I["conv_ln_b_2"]),
                (table[R_SCW:R_SCW + 12, :], I["gdn_conv_w_2"].rearrange("k (a c) -> (k a) c", c=1024)),
                (table[R_BM:R_BM + 6, :], I["b_merge"].rearrange("b (a c) -> (b a) c", c=1024)),
                (table[R_GLAB:R_GLAB + 1, 0:512], I["gla_b"]),
                (table[R_MNG:R_MNG + 1, 0:768], I["m_norm_g_3"]),
                (table[R_CNG:R_CNG + 1, 0:512], I["c_norm_g_3"]),
                (table[R_GLAG:R_GLAG + 1, 0:256], I["gla_norm_g"]),
                (table[R_GLAG:R_GLAG + 1, T_GDNW * P:(T_GDNW + 1) * P], I["gdn_norm_w_2"]),
                (table[R_CM:R_CM + 8, 0:768], I["conv_m_3"].rearrange("k (a c) -> (k a) c", c=768)),
                (gwu, I["gla_w_up"]),
                (sinks, I["swa_sinks"].to_broadcast([P, 16])),
                (gdnA, I["gdn_A_log_2"].to_broadcast([P, 8])),
                (gdndt, I["gdn_dt_bias_2"].to_broadcast([P, 8])),
                (bib, I["b_i_3"].to_broadcast([P, 6])),
                (bfb, I["b_f_3"].to_broadcast([P, 6])),
            ]:
                act.dma_start(dst, src).then_inc(par_landed, 16)

            def load_ln(g, b):
                act.dma_start(ln_gb[:, 0, :], g.to_broadcast([P, D])).then_inc(ln_landed, 16)
                act.dma_start(ln_gb[:, 1, :], b.to_broadcast([P, D])).then_inc(ln_landed, 16)

            def gates(name, dst, func, width=TW):
                sec = plan[name]
                per = width // P
                for t, u, it in tiles_of(act, sec.n):
                    act.wait_ge(tile_done[u], sec.tiles[u] + it + 1)
                    act.activation(dst[:, ds(t * per, per), :].rearrange("p a s -> p (a s)"),
                                   ps[:, 2 * u:2 * u + 2, :].rearrange("p a s -> p (a s)")[:, 0:per * S],
                                   func).then_inc(tile_free[u], 1)

            def softmax_exp(A, sink=None):
                per = {max_ready: 2, probsT_ready: A.outs}
                with n.loop(act, A.pairs, per) as i:
                    for u in range(2):
                        act.wait_ge(max_ready, n.next(max_ready))
                        if sink is not None:
                            for t in range(2):
                                act.activation(esink[:, 2 * u + t:2 * u + t + 1], sink(i, u, t), ACT.Exp,
                                               bias=nmax[:, 2 * u + t:2 * u + t + 1])
                        sums = {} if A.kind == "mlstm" else {"accum_out": rsum[:, 2 * u:2 * u + 1]}
                        act.activation(A.p[:, u, 0:P], A.sm[:, u, 0:P], ACT.Exp, bias=nmax[:, 2 * u:2 * u + 1], **sums)
                        sums = {} if A.kind == "mlstm" else {"accum_out": rsum[:, 2 * u + 1:2 * u + 2]}
                        act.activation(A.p[:, u, P:384], A.sm[:, u, P:384], ACT.Exp, bias=nmax[:, 2 * u + 1:2 * u + 2],
                                       **sums).then_inc(exp_done, 1)
                    for u in range(A.outs):
                        act.wait_ge(probsT_ready, n.next(probsT_ready))
                        act.activation(A.pT[:, u], ps[:, 6 + u, 0:384], ACT.Copy).then_inc(probsT_out, 1)

            def roots(dst, heads, scale, eps):
                for g in range(heads // 2):
                    act.wait_ge(ss_ready, n.next(ss_ready))
                    last = act.activation(dst[:, 2 * g:2 * g + 2, :].rearrange("p a s -> p (a s)"), ps[:, 4 + g % 4, :],
                                          ACT.Sqrt, bias=eps, scale=scale)
                    last.then_inc(root_ready, 1)

            def ln_roots():
                act.wait_ge(var_ready, n.next(var_ready))
                act.activation(stat[:, 28:30], stat[:, 26:28], ACT.Sqrt, bias=eps_ln).then_inc(std_ready, 1)

            gates("ag", a_gate, ACT.Silu)
            act.wait_ge(vec_ready, n.next(vec_ready, 2))
            link(act.activation(a_e[:, 0], a_e[:, 0], ACT.Exp))
            act.activation(a_e[:, 0], a_e[:, 0], ACT.Ln, bias=one).then_inc(act_ready, 1)
            for lv in range(8):
                act.wait_ge(vec_ready, n.next(vec_ready))
                act.activation(a_e[:, lv % 2], a_e[:, lv % 2], ACT.Exp).then_inc(act_ready, 1)
            act.wait_ge(vec_ready, n.next(vec_ready))
            act.activation(a_sq, y1[:, 0:8, :], ACT.Square).then_inc(sq_ready, 1)
            roots(a_rn, G_H, 1.0 / S, eps_rms)
            act.wait_ge(stage_over, 1)
            gates("bg", s_gate, ACT.Silu)
            for g in range(2):
                softmax_exp(swa[g], lambda i, u, t: sinks[:, ds(8 * g + 2 * i + u, 1)])
            act.wait_ge(stage_over, 2)
            gates("cg", m_gate, ACT.Silu)
            softmax_exp(moba)
            act.wait_ge(stage_over, 3)
            load_ln(I["ln_g"], I["ln_b"])
            sec = plan["merge"]
            with act.Fori(0, 4) as j:
                for b in range(3):
                    act.wait_ge(tile_done[1], sec.tiles[1] + 3 * j + b)
                    act.dma_start(ring[:, 2], I["w_branch"][b * BW:(b + 1) * BW, ds(j * TW, TW)].rearrange(row, p=P))\
                       .then_inc(w_landed[2], 16)
                    act.wait_ge(tile_done[0], sec.tiles[0] + 3 * j + b + 1)
                    act.wait_ge(tile_free[1], sec.tiles[1] + 3 * j + b)
                    for cb in range(4):
                        last = act.activation(sig[:, cb], ps[:, cb // 2, (cb % 2) * S:(cb % 2 + 1) * S], ACT.Sigmoid,
                                              bias=bmc[:, b, ds(4 * j + cb, 1)])
                        if cb == 3:
                            last.then_inc(tile_free[0], 1)
            ln_roots()

            def hidden_gate(name):
                sec = plan[name]
                for t, u, it in tiles_of(act, sec.n):
                    if u == 0:
                        act.wait_ge(tile_done[0], sec.tiles[0] + it + 1)
                        act.wait_ge(tile_free[1], sec.tiles[1] + it)
                        act.activation(f_sg[:, 0].rearrange("p a s -> p (a s)"),
                                       ps[:, 0:2, :].rearrange("p a s -> p (a s)"), ACT.Silu).then_inc(tile_free[0], 1)

            act.wait_ge(x_ready, 2)
            gates("cgate", c_acc, ACT.Sigmoid)
            sec = plan["qkv"]
            with n.loop(act, sec.n, {silu_done: 0, conv_ready: 0, vec_ready: 1}) as t:
                act.wait_ge(vec_ready, n.next(vec_ready))
                v = c_qkv[:, ds(4 * t, 4), :].rearrange("p a s -> p (a s)")
                act.activation(v, v, ACT.Silu).then_inc(silu_done, 1)
            gates("z", c_z, ACT.Silu)
            act.wait_ge(vec_ready, n.next(vec_ready))
            act.activation(t_beta, t_ba[:, :, 0:8], ACT.Sigmoid)
            act.activation(t_A, gdnA, ACT.Exp)
            link(act.activation(t_e, t_e, ACT.Exp))
            act.activation(t_e, t_e, ACT.Ln, bias=one).then_inc(act_ready, 1)
            act.wait_ge(vec_ready, n.next(vec_ready))
            act.activation(c_sq, c_acc, ACT.Square).then_inc(conv_ready, 1)
            act.wait_ge(mm_ready, n.next(mm_ready, 13))
            act.activation(c_rs, ps[:, 5, 0:S], ACT.Sqrt, bias=eps_ln, scale=1.0 / 1024).then_inc(act_ready, 1)
            act.wait_ge(vec_ready, n.next(vec_ready))
            for t in range(8):
                last = act.activation(y2[:, t], c_acc[:, t], ACT.Silu, bias=colp[:, t, R_CLB:R_CLB + 1],
                                      scale=colp[:, t, R_CLG:R_CLG + 1])
            last.then_inc(act_ready, 1)
            act.wait_ge(act_ready, 12)
            act.activation(l2_sq[:], c_qkv[:, 0:16], ACT.Square).then_inc(sq_ready, 1)
            roots(l2_rn, 16, 1.0, eps_rms)
            for h in range(GD_H):
                act.wait_ge(vec_ready, n.next(vec_ready))
                act.activation(d_dt[:, h % 2], d_dt[:, h % 2], ACT.Exp).then_inc(act_ready, 1)
            with n.loop(act, 7, {xp_ready: 4}):
                for g in range(4):
                    act.wait_ge(xp_ready, n.next(xp_ready))
                    act.activation(d_xs[:, 4 * g:4 * g + 4].rearrange("p a b -> p (a b)"), ps[:, g, :],
                                   ACT.Copy).then_inc(xs_ready, 1)
            act.wait_ge(vec_ready, n.next(vec_ready))
            act.activation(d_sq, y2[:, 8:16], ACT.Square).then_inc(sq_ready, 1)
            roots(d_rn, GD_H, 1.0 / P, eps_rms)
            act.wait_ge(stage_over, 5)
            load_ln(I["ln1_g_2"], I["ln1_b_2"])
            ln_roots()
            act.wait_ge(x_ready, 3)
            load_ln(I["ln2_g_2"], I["ln2_b_2"])
            hidden_gate("gu")
            ln_roots()
            act.wait_ge(x_ready, 4)
            load_ln(I["ln1_g_3"], I["ln1_b_3"])
            for r, name in enumerate(("lam_q1_3", "lam_k1_3", "lam_q2_3", "lam_k2_3")):
                act.dma_start(lam_rows[:, r], I[name].to_broadcast([P, 64])).then_inc(lam_landed, 16)
            softmax_exp(dsa)
            act.wait_ge(stage_over, 6)
            for t in range(3):
                act.wait_ge(vec_ready, n.next(vec_ready))
                v = e_qk[:, 4 * t:4 * t + 4]
                act.activation(v, v, ACT.Silu).then_inc(silu_done, 1)
            gates("om", e_gate, ACT.Sigmoid, 384)
            act.wait_ge(vec_ready, n.next(vec_ready))
            link(act.activation(t_ef, t_ef, ACT.Exp))
            act.activation(t_ef, t_ef, ACT.Ln, bias=one).then_inc(act_ready, 1)
            act.wait_ge(vec_ready, n.next(vec_ready))
            softmax_exp(mls, lambda i, u, t: t_na[:, t, ds(2 * i + u, 1)])
            act.wait_ge(vec_ready, n.next(vec_ready))
            act.activation(e_sq, y3[:, 6:12], ACT.Square).then_inc(sq_ready, 1)
            roots(e_rn, M_H, 1.0 / P, eps_ln)
            act.wait_ge(vec_ready, n.next(vec_ready))
            act.activation(lam[:, 2:4], lam[:, 0:2], ACT.Exp).then_inc(act_ready, 1)
            softmax_exp(dif)
            act.wait_ge(vec_ready, n.next(vec_ready))
            act.activation(e_sq[:, 0:4], e_cut, ACT.Square, scale=SHRINK).then_inc(sq_ready, 1)
            roots(e_rn, D_H, 1.0 / P, eps_diff)
            ln_roots()
            act.wait_ge(x_ready, 5)
            load_ln(I["ln2_g_3"], I["ln2_b_3"])
            sec = plan["up3"]
            for t, u, it in tiles_of(act, sec.n):
                act.wait_ge(tile_done[u], sec.tiles[u] + it + 1)
                v = f_sg[:, u].rearrange("p a s -> p (a s)")
                act.activation(v, ps[:, 2 * u:2 * u + 2, :].rearrange("p a s -> p (a s)"), ACT.Relu)\
                   .then_inc(tile_free[u], 1)
                act.wait_ge(tile_free[u], sec.tiles[u] + it + 1)
                act.activation(hid[:, ds(4 * t, 4), :].rearrange("p a s -> p (a s)"), v, ACT.Square)\
                   .then_inc(hid_ready, 1)
            ln_roots()

        @block.vector
        def _(dve):
            n = Count(FREE)

            def link(ins):
                ins.then_inc(dve_order, 1)
                dve.wait_ge(dve_order, n.next(dve_order))

            def tt(o, a, b, op):
                return dve.tensor_tensor(o, a, b, op)

            def tsc(o, a, s1, op0, s2=None, op1=ALU.bypass):
                return dve.tensor_scalar(o, a, s1, s2, op0, op1)

            def stt(o, a, s, b, op0, op1, **kw):
                return dve.scalar_tensor_tensor(o, a, s, b, op0, op1, **kw)

            dve.sem_inc(logits_used, 1)
            dve.sem_inc(o_used, 1)
            dve.memset(table[:], 0.0).then_inc(table_zeroed, 1)
            dve.memset(eps_ln, LN_EPS)
            dve.memset(eps_rms, RMS_EPS)
            dve.memset(one, 1.0)
            dve.memset(eps_diff, LN_EPS * SHRINK ** 2)
            for h in range(A_H):
                dve.memset(slopes_a[:, h:h + 1], 2.0 ** (-8.0 * (h + 1) / A_H))
            for h in range(D_H):
                dve.memset(slopes_c[:, h:h + 1], 2.0 ** (-8.0 * (h + 1) / D_H))
            dve.memset(ones[:], 1.0)
            dve.memset(upper[:, P:S], 1.0)
            for m in (causal, causalT):
                dve.memset(m[:, P:S], 0.0)
            dve.wait_ge(iotas, 2)
            pi, pj, px, py = (v.bitcast(I32) for v in (posi, posj, posx, posy))
            tt(ident[:], pi, pj, ALU.is_equal)
            link(tt(upper[:, 0:P], pi, pj, ALU.is_ge))
            for dst, cmp in [(causal[:, 0:P], ALU.is_gt), (causal[:, S:384], ALU.is_gt), (causalT[:, 0:P], ALU.is_lt),
                             (causalT[:, S:384], ALU.is_lt), (band[:, 0:P], ALU.is_gt), (band[:, P:S], ALU.is_le),
                             (band[:, S:384], ALU.is_gt)]:
                link(tt(dst, pi, pj, cmp))
                dve.tensor_scalar(dst, dst, NEG, None, ALU.mult)
            for c in (0, 2):
                tt(ndist[:, c * P:(c + 1) * P], pi, pj, ALU.subtract)
            link(tt(ndist[:, P:S], pi, pj, ALU.subtract))
            link(tsc(ndist[:, P:S], ndist[:, P:S], -float(P), ALU.add))
            link(tt(px, pi, pj, ALU.bitwise_xor))
            for lv in range(7):
                link(tsc(py, px, lv, ALU.logical_shift_right))
                link(tsc(levels[:, lv], py, 1, ALU.is_equal))
                link(tt(levels[:, lv], levels[:, lv], upper[:, 0:P], ALU.mult))
            dve.wait_ge(x_landed, 16)
            dve.sem_inc(consts, 1)

            def x_ready_now():
                dve.sem_inc(x_ready, 1)

            x_ready_now()
            dve.wait_ge(tableT_ready, 1)
            link(dve.tensor_copy(colp[:].rearrange("p t r -> p (t r)"), ps[:, 0, :]))
            for b in range(3):
                last = dve.tensor_copy(bmc[:, b, :].rearrange("p (a t) -> p a t", a=2),
                                       colp[:, :, R_BM + 2 * b:R_BM + 2 * b + 2].rearrange("p t a -> p a t"))
            last.then_inc(table_ready, 1)

            def take_x():
                for g in range(KT // 2):
                    dve.wait_ge(xTp_ready, n.next(xTp_ready))
                    dve.tensor_copy(xT[:, 2 * g:2 * g + 2, :].rearrange("p a s -> p (a s)"), ps[:, 4 + g % 4, :])\
                       .then_inc(xTp_used, 1)

            def take(name, dst, kind, width=TW):
                sec = plan[name]
                for t, u, it in tiles_of(dve, sec.n):
                    dve.wait_ge(tile_done[u], sec.tiles[u] + it + 1)
                    if kind == "F":
                        per = width // P
                        dve.tensor_copy(dst[:, ds(t * per, per), :].rearrange("p a s -> p (a s)"),
                                        ps[:, 2 * u:2 * u + 2, :].rearrange("p a s -> p (a s)")[:, 0:per * S])\
                           .then_inc(tile_free[u], 1)
                    else:
                        dve.tensor_copy(dst[:, :, ds(t * width, width)], ps[:, 2 * u:2 * u + 2, 0:width])\
                           .then_inc(tile_free[u], 1)

            def wait_gates(name):
                sec = plan[name]
                for u in range(2):
                    dve.wait_ge(tile_free[u], sec.tiles[u] + (sec.n + 1 - u) // 2)

            def over():
                dve.sem_inc(stage_over, 1)

            def attention(A, scale, mask, y, gate=None, toff=0, sink=None, slopes=None):
                kind = A.kind
                per = {logits_ready: 2, logits_used: 2, exp_done: 2, o_ready: 1,
                       dve_order: {"swa": 8, "moba": 2, "dsa": 4, "mlstm": 10, "diff": 5}[kind]}
                with n.loop(dve, A.pairs, per) as i:
                    for u in range(2):
                        m, sm = nmax[:, 2 * u:2 * u + 2], A.sm[:, u]
                        if kind == "mlstm":
                            for c0, w in ((0, P), (P, S)):
                                last = tt(sm[:, c0:c0 + w],
                                          e_bbc[:, ds(2 * i + u, 1), 0:w].rearrange("p a s -> p (a s)"),
                                          causal[:, c0:c0 + w], ALU.add)
                            link(last)
                        else:
                            if slopes is not None:
                                link(stt(sm, ndist[:], slopes[:, ds(A.outs * i + (u if A.outs == 2 else 0), 1)], mask,
                                         ALU.mult, ALU.add))
                            dve.wait_ge(logits_ready, n.next(logits_ready))
                            stt(sm, ps[:, 4 + u, 0:384], scale, mask if slopes is None else sm, ALU.mult, ALU.add)\
                                .then_inc(logits_used, 1)
                            dve.wait_ge(logits_used, n.next(logits_used))
                        dve.tensor_reduce(m[:, 0:1], sm[:, 0:P], AX, ALU.max, negate=True)
                        last = dve.tensor_reduce(m[:, 1:2], sm[:, P:384], AX, ALU.max, negate=True)
                        if kind == "mlstm":
                            link(last)
                            tsc(m, m, 0.0, ALU.min).then_inc(max_ready, 1)
                        elif kind == "swa":
                            link(last)
                            link(tsc(esink[:, 2 * u:2 * u + 1], sinks[:, ds(8 * sink + 2 * i + u, 1)], -1.0, ALU.mult))
                            tsc(m, m, esink[:, 2 * u:2 * u + 1], ALU.min).then_inc(max_ready, 1)
                        else:
                            last.then_inc(max_ready, 1)
                    if kind == "diff":
                        p0, p1 = A.p[:, 0], A.p[:, 1]
                        dve.wait_ge(exp_done, n.next(exp_done, 2))
                        link(dve.reciprocal(rinv, rsum))
                        link(tsc(rinv[:, 2:4], rinv[:, 2:4], lam[:, 4:5], ALU.mult))
                        tsc(p0[:, 0:P], p0[:, 0:P], rinv[:, 0:1], ALU.mult)
                        link(tsc(p0[:, P:384], p0[:, P:384], rinv[:, 1:2], ALU.mult))
                        stt(p0[:, 0:P], p1[:, 0:P], rinv[:, 2:3], p0[:, 0:P], ALU.mult, ALU.add)
                        stt(p0[:, P:384], p1[:, P:384], rinv[:, 3:4], p0[:, P:384], ALU.mult, ALU.add)\
                            .then_inc(probs_ready, 1)
                    for u in range(2 if kind != "diff" else 0):
                        l, p = rsum[:, 2 * u:2 * u + 2], A.p[:, u]
                        dve.wait_ge(exp_done, n.next(exp_done))
                        if kind == "swa":
                            link(tt(l, l, esink[:, 2 * u:2 * u + 2], ALU.add))
                        if kind == "mlstm":
                            dve.wait_ge(logits_ready, n.next(logits_ready))
                            stt(p[:, 0:P], ps[:, 4 + u, 0:P], scale, p[:, 0:P], ALU.mult, ALU.mult, accum_out=l[:, 0:1])
                            stt(p[:, P:384], ps[:, 4 + u, P:384], scale, p[:, P:384], ALU.mult, ALU.mult,
                                accum_out=l[:, 1:2]).then_inc(logits_used, 1)
                            dve.wait_ge(logits_used, n.next(logits_used))
                            link(stt(l, l, -1.0, l, ALU.mult, ALU.max))
                            link(tt(l, l, esink[:, 2 * u:2 * u + 2], ALU.max))
                        link(dve.reciprocal(rinv[:, 2 * u:2 * u + 2], l))
                        tsc(p[:, 0:P], p[:, 0:P], rinv[:, 2 * u:2 * u + 1], ALU.mult)
                        tsc(p[:, P:384], p[:, P:384], rinv[:, 2 * u + 1:2 * u + 2], ALU.mult).then_inc(probs_ready, 1)
                    dve.wait_ge(o_ready, n.next(o_ready))
                    one_tile = lambda v: v[:, ds(toff + i, 1), :].rearrange("p a s -> p (a s)")
                    if kind == "swa":
                        last = tt(one_tile(y), ps[:, 2, 0:S], one_tile(gate), ALU.mult)
                    elif kind == "diff":
                        last = dve.tensor_copy(one_tile(y), ps[:, 2, 0:S])
                    elif gate is None:
                        last = dve.tensor_copy(y[:, ds(2 * i, 2), :], ps[:, 2:4, 0:S])
                    else:
                        last = tt(y[:, ds(2 * i, 2), :], ps[:, 2:4, 0:S], gate[:, ds(2 * i, 2), :], ALU.mult)
                    last.then_inc(o_used, 1)
                dve.wait_ge(o_used, n.next(o_used, A.pairs))

            def inverse_roots(dst, heads):
                dve.wait_ge(root_ready, n.next(root_ready, heads // 2))
                link(dve.reciprocal(dst, dst))

            def layer_norm(name, after=None):
                sec = plan[name]
                for t, u, it in tiles_of(dve, sec.n):
                    dve.wait_ge(tile_done[u], sec.tiles[u] + it + 1)
                    xv = xtok[:, :, ds(t * TW, TW)]
                    stt(xv, xv, ALPHA, ps[:, 2 * u:2 * u + 2, :], ALU.mult, ALU.add).then_inc(tile_free[u], 1)
                for u in range(2):
                    dve.wait_ge(tile_free[u], sec.tiles[u] + sec.n // 2)
                for t in range(2):
                    for c in range(4):
                        last = dve.bn_stats(stat[:, 32 + 6 * c:38 + 6 * c] if t == 0 else tokc[:, 6 * c:6 * c + 6],
                                            xtok[:, t, c * TW:(c + 1) * TW])
                link(last)
                link(dve.bn_aggr(stat[:, 2:4], stat[:, 32:56]))
                link(dve.bn_aggr(stat[:, 4:6], tokc[:, 0:24]))
                for t in range(2):
                    link(dve.tensor_copy(stat[:, 26 + t:27 + t], stat[:, 3 + 2 * t:4 + 2 * t]))
                dve.sem_inc(var_ready, 1)
                dve.wait_ge(std_ready, n.next(std_ready))
                link(dve.reciprocal(stat[:, 28:30], stat[:, 28:30]))
                dve.wait_ge(ln_landed, n.next(ln_landed, 32))
                for t in range(2):
                    link(tsc(xtok[:, t], xtok[:, t], stat[:, 2 + 2 * t:3 + 2 * t], ALU.subtract,
                             stat[:, 28 + t:29 + t], ALU.mult))
                    link(tt(xtok[:, t], xtok[:, t], ln_gb[:, 0], ALU.mult))
                    link(tt(xtok[:, t], xtok[:, t], ln_gb[:, 1], ALU.add))

            take_x()
            take("aqk", a_qk, "F")
            take("av", a_v, "T")
            dve.wait_ge(tile_done[0], plan["alr"].tiles[0] + 1)
            link(dve.tensor_copy(alrT, ps[0:G_RANK, 0, 0:S]))
            dve.sem_inc(tile_free[0], 1)
            dve.sem_inc(vec_ready, 1)
            dve.wait_ge(mm_ready, n.next(mm_ready))
            for h in range(G_H):
                tsc(a_b[:, h], ps[:, 4 + h // 2, (h % 2) * S:(h % 2 + 1) * S], colp[:, h, R_GLAB:R_GLAB + 1], ALU.add)\
                    .then_inc(dve_order, 1)
            dve.wait_ge(dve_order, n.next(dve_order, G_H))
            stt(a_e[:, 0], a_b, -1.0, a_b, ALU.mult, ALU.min).then_inc(vec_ready, 1)
            link(tsc(a_b, a_b, 0.0, ALU.min))
            dve.wait_ge(act_ready, n.next(act_ready))
            link(tt(a_b, a_b, a_e[:, 0], ALU.subtract))
            link(tsc(a_e[:, 1], a_b, 1.0 / G_TAU, ALU.mult))
            for h in range(G_H):
                last = dve.tensor_tensor_scan(a_b[:, h], ones[:, 0:1].to_broadcast([P, S]), a_e[:, 1, h], 0.0, ALU.mult, ALU.add)
            link(last)
            link(dve.memset(a_at, 0.0))
            QS = float(P) ** -0.5
            q4, k4 = a_qk[:, 0:4], a_qk[:, 4:8]

            def level_factors(lv):
                half = 1 << lv
                bv = a_b.rearrange("p h (c w) -> p (h c) w", w=2 * half)
                mid = bv[:, :, half - 1:half].to_broadcast([P, 4 * S // (2 * half), 2 * half])
                e = a_e[:, lv % 2]
                link(tt(e.rearrange("p h (c w) -> p (h c) w", w=2 * half), bv, mid, ALU.subtract))
                stt(e, e, -1.0, e, ALU.mult, ALU.min).then_inc(vec_ready, 1)

            def merge_level(lv):
                dve.wait_ge(mm_ready, n.next(mm_ready))
                b = 4 + 2 * (lv % 2)
                if lv == 7:
                    dve.tensor_copy(a_at[:, :, P:S], ps[:, b, :].rearrange("p (h s) -> p h s", h=4)).then_inc(mm_used, 1)
                    return
                m = ident[:] if lv == 8 else levels[:, lv]
                b = 4 if lv == 8 else b
                for g in range(2):
                    for c in range(2):
                        o = a_at[:, 2 * g:2 * g + 2, c * S:c * S + P]
                        d = ps[:, b + g, :].rearrange("p (h s) -> p h s", h=2)[:, :, c * P:(c + 1) * P]
                        mk = m.unsqueeze(1).to_broadcast([P, 2, P]).bitcast(I32)
                        last = dve.copy_predicated(o, mk, d)
                last.then_inc(mm_used, 1)

            level_factors(0)
            for lv in range(8):
                if lv < 7:
                    level_factors(lv + 1)
                dve.wait_ge(act_ready, n.next(act_ready))
                if lv >= 2:
                    pass
                stt(a_qe[:, lv % 2], q4, QS, a_e[:, lv % 2], ALU.mult, ALU.mult)
                link(tt(a_ke[:, lv % 2], k4, a_e[:, lv % 2], ALU.mult))
                dve.sem_inc(fac_ready, 1)
                if lv >= 1:
                    merge_level(lv - 1)
            merge_level(7)
            link(tsc(a_qe[:, 0], q4, QS, ALU.mult))
            dve.sem_inc(fac_ready, 1)
            merge_level(8)
            dve.wait_ge(mm_ready, n.next(mm_ready))
            link(dve.tensor_copy(y1[:, 0:8, :].rearrange("p a s -> p (a s)"), ps[:, 4:8, :].rearrange("p a s -> p (a s)")))
            dve.sem_inc(vec_ready, 1)
            wait_gates("ag")
            dve.wait_ge(sq_ready, n.next(sq_ready))
            for e in range(2):
                ya = y1[:, 0:8].rearrange("p (h e) s -> p h e s", e=2)[:, :, e, :]
                ga = a_gate.rearrange("p (h e) s -> p h e s", e=2)[:, :, e, :]
                stt(ya, ya, colp[:, e, R_GLAG:R_GLAG + 1], ga, ALU.mult, ALU.mult).then_inc(dve_order, 1)
            dve.wait_ge(dve_order, n.next(dve_order, 2))
            inverse_roots(a_rn, G_H)
            for e in range(2):
                ya = y1[:, 0:8].rearrange("p (h e) s -> p h e s", e=2)[:, :, e, :]
                last = tt(ya, ya, a_rn, ALU.mult)
            link(last)
            over()
            take("bq", s_q, "F")
            dve.wait_ge(tile_done[0], plan["bkv"].tiles[0] + 1)
            dve.tensor_copy(s_kd[:].rearrange("p a s -> p (a s)"), ps[:, 0, :])
            dve.tensor_copy(s_v[:].rearrange("p a s -> p (a s)"), ps[:, 1, 0:S]).then_inc(tile_free[0], 1)
            wait_gates("bg")
            dve.sem_inc(gate_ready, 1)
            for g in range(2):
                attention(swa[g], 64.0 ** -0.5, band[:], y1[:, 8:16], s_gate, 4 * g, sink=g)
            over()
            take("cqk", m_qk, "F")
            take("cv", m_v, "T")
            wait_gates("cg")
            dve.sem_inc(gate_ready, 1)
            attention(moba, float(P) ** -0.5, causal[:], y1[:, 16:24], m_gate, 0)
            over()
            sec = plan["merge"]
            with n.loop(dve, 4, {dve_order: 2}) as j:
                for b in range(3):
                    dve.wait_ge(tile_done[1], sec.tiles[1] + 3 * j + b + 1)
                    dve.wait_ge(tile_free[0], sec.tiles[0] + 3 * j + b + 1)
                    up = ps[:, 2:4, :].rearrange("p a s -> p (a s)")
                    sg = sig.rearrange("p a s -> p (a s)")
                    mt = mtmp.rearrange("p a s -> p (a s)")
                    md = mergedT[:, ds(4 * j, 4), :].rearrange("p a s -> p (a s)")
                    tt(md if b == 0 else mt, sg, up, ALU.mult).then_inc(tile_free[1], 1)
                    dve.wait_ge(tile_free[1], sec.tiles[1] + 3 * j + b + 1)
                    if b:
                        link(tt(md, md, mt, ALU.add))
            over()
            layer_norm("wo")
            dve.sem_inc(x_ready, 1)

            def hidden_up(name):
                sec = plan[name]
                for t, u, it in tiles_of(dve, sec.n):
                    if u == 1:
                        dve.wait_ge(tile_done[1], sec.tiles[1] + it + 1)
                        dve.wait_ge(tile_free[0], sec.tiles[0] + it + 1)
                        tt(hid[:, ds(4 * it, 4), :].rearrange("p a s -> p (a s)"), f_sg[:, 0].rearrange("p a s -> p (a s)"),
                           ps[:, 2:4, :].rearrange("p a s -> p (a s)"), ALU.mult).then_inc(tile_free[1], 1)

            take_x()
            for k in range(SHORT_W):
                link(dve.tensor_copy(scw[:, k, :].rearrange("p (a t) -> p a t", a=3),
                                     colp[:, :, R_SCW + 3 * k:R_SCW + 3 * k + 3].rearrange("p t a -> p a t")))
            dve.memset(c_h[:, :, 0:HP], 0.0)
            dve.memset(c_raw[:, :, :, 0:RP], 0.0)
            sec = plan["cval"]
            for t, u, it in tiles_of(dve, sec.n):
                dve.wait_ge(tile_done[u], sec.tiles[u] + it + 1)
                dve.tensor_copy(c_h[:, 4 * t:4 * t + 4, HP:HP + S],
                                ps[:, 2 * u:2 * u + 2, :].rearrange("p a (c s) -> p (a c) s", c=2))\
                   .then_inc(tile_free[u], 1)
            wait_gates("cgate")
            link(tt(c_h[:, :, HP:HP + S], c_h[:, :, HP:HP + S], c_acc, ALU.mult))

            def wide_conv(t):
                acc = c_acc[:, ds(t, 1), :].rearrange("p a s -> p (a s)")
                win = lambda k: c_h[:, ds(t, 1), k:k + S].rearrange("p a s -> p (a s)")
                tap = lambda r: colp[:, ds(t, 1), r:r + 1].rearrange("p a s -> p (a s)")
                link(tsc(acc, win(0), tap(R_DWW), ALU.mult, tap(R_DWB), ALU.add))
                for k in range(1, CONV_W):
                    link(stt(acc, win(k), tap(R_DWW + k), acc, ALU.mult, ALU.add))

            sec = plan["qkv"]
            with n.loop(dve, sec.n // 2, {dve_order: 2 * (CONV_W + 3)}) as i:
                for u in range(2):
                    t = 2 * i + u
                    dve.wait_ge(tile_done[u], sec.tiles[u] + i + 1)
                    dve.tensor_copy(c_raw[:, u, :, RP:RP + S],
                                    ps[:, 2 * u:2 * u + 2, :].rearrange("p a (c s) -> p (a c) s", c=2))\
                       .then_inc(tile_free[u], 1)
                    dve.wait_ge(tile_free[u], sec.tiles[u] + i + 1)
                    for k in range(SHORT_W):
                        for c in range(4):
                            o = c_qkv[:, ds(4 * t + c, 1), :].rearrange("p a s -> p (a s)")
                            r = c_raw[:, u, c, k:k + S]
                            wk = scw[:, k, ds(4 * t + c, 1)]
                            last = tsc(o, r, wk, ALU.mult) if k == 0 else stt(o, r, wk, o, ALU.mult, ALU.add)
                        if k < SHORT_W - 1:
                            link(last)
                        else:
                            last.then_inc(vec_ready, 1)
                    wide_conv(t)
            with n.loop(dve, 2, {dve_order: CONV_W}) as i:
                wide_conv(6 + i)
            dve.sem_inc(conv_ready, 1)
            dve.wait_ge(tile_done[0], plan["ba"].tiles[0] + 1)
            dve.tensor_copy(t_ba.rearrange("p t c -> p (t c)"), ps[:, 0, 0:32]).then_inc(tile_free[0], 1)
            dve.wait_ge(tile_free[0], plan["ba"].tiles[0] + 1)
            link(tt(t_x, t_ba[:, :, 8:16], gdndt.unsqueeze(1).to_broadcast([P, 2, 8]), ALU.add))
            stt(t_e, t_x, -1.0, t_x, ALU.mult, ALU.min).then_inc(vec_ready, 1)
            dve.wait_ge(mm_ready, n.next(mm_ready))
            link(tsc(c_mu, ps[:, 4, 0:S], 1.0 / 1024, ALU.mult))
            tt(c_acc, c_acc, c_mu.unsqueeze(1).to_broadcast([P, 8, S]), ALU.subtract).then_inc(vec_ready, 1)
            dve.wait_ge(act_ready, n.next(act_ready))
            link(stt(t_x, t_x, 0.0, t_e, ALU.max, ALU.add))
            link(stt(t_g, t_x, -1.0, t_A.unsqueeze(1).to_broadcast([P, 2, 8]), ALU.mult, ALU.mult))
            dve.wait_ge(act_ready, n.next(act_ready))
            link(dve.reciprocal(c_rs, c_rs))
            dve.wait_ge(mm_ready, n.next(mm_ready))
            tt(c_acc, c_acc, c_rs.unsqueeze(1).to_broadcast([P, 8, S]), ALU.mult).then_inc(vec_ready, 1)
            dve.wait_ge(act_ready, n.next(act_ready))
            dve.wait_ge(root_ready, n.next(root_ready, 8))
            link(dve.reciprocal(l2_rn, l2_rn))
            stt(c_qkv[:, 0:8], c_qkv[:, 0:8], float(P) ** -0.5, l2_rn[:, 0:8], ALU.mult, ALU.mult)
            link(tt(c_qkv[:, 8:16], c_qkv[:, 8:16], l2_rn[:, 8:16], ALU.mult))
            dve.sem_inc(fac_ready, 1)
            dve.wait_ge(mm_ready, n.next(mm_ready))
            dve.tensor_copy(t_gc.rearrange("p t c -> p (t c)"), ps[:, 0, 0:16])
            for t in range(2):
                last = tt(d_vb[:, t].rearrange("p (h c) -> p h c", h=8),
                          ps[:, 4 + 2 * t:6 + 2 * t, :].rearrange("p a (h c) -> p (a h) c", h=4),
                          t_beta[:, t].unsqueeze(2).to_broadcast([P, 8, P]), ALU.mult)
            link(last)
            dve.sem_inc(fac_ready, 1)
            for h in range(GD_H):
                b, dt, db = 2 + 3 * (h % 2), d_dt[:, h % 2], d_db[:, h % 2]
                dve.wait_ge(mm_ready, n.next(mm_ready))
                stt(dt[:, 0:S], ps[:, b, 0:S], t_gc[:, 0, h:h + 1], causalT[:, 0:S], ALU.subtract, ALU.add)
                stt(dt[:, S:384], ps[:, b, P:S], t_gc[:, 1, h:h + 1], causalT[:, S:384], ALU.subtract, ALU.add)\
                    .then_inc(vec_ready, 1)
                dve.wait_ge(act_ready, n.next(act_ready))
                tt(d_at[:, h], ps[:, b + 2, 0:384], dt, ALU.mult)
                tt(db[:, 0:S], dt[:, 0:S], ps[:, b, S:512], ALU.mult)
                link(tt(db[:, S:384], dt[:, S:384], ps[:, b, S + P:512], ALU.mult))
                tt(d_lt[:, 2 * h:2 * h + 2], ps[:, b + 1, 0:384].rearrange("p (a c) -> p a c", a=3)[:, 0:3:2],
                   db.rearrange("p (a c) -> p a c", a=3)[:, 0:3:2], ALU.mult)
                tt(d_l21[:, h], ps[:, b + 1, P:S], db[:, P:S], ALU.mult).then_inc(fac_ready, 1)
                dve.wait_ge(fac_ready, n.next(fac_ready, 12 if h == 0 else 1))
            for g in range(4):
                for m in (d_t, d_tt):
                    last = dve.tensor_copy(m[:, 4 * g:4 * g + 4], ident[:].unsqueeze(1).to_broadcast([P, 4, P]))
                last.then_inc(inv_ready, 1)
            dve.wait_ge(inv_ready, n.next(inv_ready, 4))
            with n.loop(dve, 7, {yp_ready: 4, inv_ready: 4}) as lv:
                for g in range(4):
                    mk = levels[:, ds(lv, 1), :].to_broadcast([P, 4, P])
                    tt(d_lm[:, 4 * g:4 * g + 4], d_lt[:, 4 * g:4 * g + 4], mk, ALU.mult).then_inc(lm_ready, 1)
                for g in range(4):
                    dve.wait_ge(yp_ready, n.next(yp_ready))
                    for m, b in ((d_t, 4), (d_tt, 6)):
                        v = m[:, 4 * g:4 * g + 4].rearrange("p a b -> p (a b)")
                        last = tt(v, v, ps[:, b + g % 2, :], ALU.subtract)
                    last.then_inc(inv_ready, 1)
                    dve.wait_ge(inv_ready, n.next(inv_ready))
            flat = lambda b: ps[:, b:b + 2, :].rearrange("p a s -> p (a s)")
            dve.wait_ge(mm_ready, n.next(mm_ready))
            dve.tensor_copy(d_vn[:, 0], flat(0)).then_inc(fac_ready, 1)
            dve.wait_ge(mm_ready, n.next(mm_ready))
            tt(d_vb[:, 1], d_vb[:, 1], flat(2), ALU.subtract).then_inc(fac_ready, 1)
            dve.wait_ge(mm_ready, n.next(mm_ready))
            dve.tensor_copy(d_vn[:, 1], flat(0)).then_inc(fac_ready, 1)
            dve.wait_ge(mm_ready, n.next(mm_ready))
            dve.tensor_copy(y2[:, 8:16].rearrange("p a s -> p (a s)"), ps[:, 4:8, :].rearrange("p a s -> p (a s)"))\
               .then_inc(vec_ready, 1)
            wait_gates("z")
            dve.wait_ge(sq_ready, 3)
            link(stt(y2[:, 8:16], y2[:, 8:16], colp[:, T_GDNW, R_GLAG:R_GLAG + 1], c_z, ALU.mult, ALU.mult))
            inverse_roots(d_rn, GD_H)
            link(tt(y2[:, 8:16], y2[:, 8:16], d_rn, ALU.mult))
            over()
            layer_norm("wout2")
            dve.sem_inc(x_ready, 1)
            take_x()
            hidden_up("gu")
            layer_norm("down2")
            dve.sem_inc(x_ready, 1)
            take_x()
            for k in range(SHORT_W):
                last = dve.tensor_copy(mcw[:, k, :].rearrange("p (a t) -> p a t", a=2),
                                       colp[:, 0:6, R_CM + 2 * k:R_CM + 2 * k + 2].rearrange("p t a -> p a t"))
            link(last)
            take("qka", e_qk, "F")
            take("va", e_v, "T", 384)
            take("qi", i_q, "F")
            sec = plan["kwi"]
            dve.wait_ge(tile_done[0], sec.tiles[0] + 1)
            dve.tensor_copy(i_k, ps[:, 0, 0:S])
            dve.tensor_copy(t_w.rearrange("p t c -> p (t c)"), ps[:, 0, S:S + 16]).then_inc(tile_free[0], 1)
            dve.wait_ge(tile_free[0], sec.tiles[0] + 1)
            dve.sem_inc(fac_ready, 1)
            dve.sem_inc(gate_ready, 1)
            for h in range(8):
                dve.wait_ge(mm_ready, n.next(mm_ready))
                o = i_work if h == 0 else i_tmp
                tsc(o[:, 0:P], ps[:, 4 + h % 4, 0:P], 0.0, ALU.max, t_w[:, 0, h:h + 1], ALU.mult)
                tsc(o[:, P:384], ps[:, 4 + h % 4, P:384], 0.0, ALU.max, t_w[:, 1, h:h + 1], ALU.mult)\
                    .then_inc(mm_used, 1)
                dve.wait_ge(mm_used, n.next(mm_used, 10 if h == 0 else 1))
                if h:
                    link(tt(i_work, i_work, i_tmp, ALU.add))
            link(tt(i_work, i_work, causal[:], ALU.add))
            for _ in range(TOPK // 8):
                dve.max(top8[:, 0], i_work[:, 0:P])
                link(dve.max(top8[:, 1], i_work[:, P:384]))
                dve.match_replace(i_work[:, 0:P], top8[:, 0], i_work[:, 0:P], TAKEN)
                link(dve.match_replace(i_work[:, P:384], top8[:, 1], i_work[:, P:384], TAKEN))
            link(tsc(i_sel, i_work, TAKEN / 2, ALU.is_gt, NEG, ALU.mult))
            link(tt(i_sel, i_sel, causal[:], ALU.add))
            attention(dsa, float(P) ** -0.5, i_sel, y3[:, 0:6], slopes=slopes_a)
            over()
            dve.memset(e_raw[:, :, :, 0:RP], 0.0)
            sec = plan["qkm"]
            for t in range(3):
                u = t % 2
                dve.wait_ge(tile_done[u], sec.tiles[u] + t // 2 + 1)
                dve.tensor_copy(e_raw[:, u, :, RP:RP + S],
                                ps[:, 2 * u:2 * u + 2, :].rearrange("p a (c s) -> p (a c) s", c=2))\
                   .then_inc(tile_free[u], 1)
                dve.wait_ge(tile_free[u], sec.tiles[u] + t // 2 + 1)
                for k in range(SHORT_W):
                    for c in range(4):
                        o, r, wk = e_qk[:, 4 * t + c], e_raw[:, u, c, k:k + S], mcw[:, k, 4 * t + c:4 * t + c + 1]
                        last = tsc(o, r, wk, ALU.mult) if k == 0 else stt(o, r, wk, o, ALU.mult, ALU.add)
                    if k < SHORT_W - 1:
                        link(last)
                    else:
                        last.then_inc(vec_ready, 1)
            take("vm", e_v, "T", 384)
            sec = plan["if"]
            dve.wait_ge(tile_done[0], sec.tiles[0] + 1)
            dve.tensor_copy(t_if.rearrange("p t c -> p (t c)"), ps[:, 0, 0:24]).then_inc(tile_free[0], 1)
            dve.wait_ge(tile_free[0], sec.tiles[0] + 1)
            tt(t_if[:, :, 0:6], t_if[:, :, 0:6], bib.unsqueeze(1).to_broadcast([P, 2, 6]), ALU.add)
            link(tt(t_lf, t_if[:, :, 6:12], bfb.unsqueeze(1).to_broadcast([P, 2, 6]), ALU.add))
            stt(t_ef, t_lf, -1.0, t_lf, ALU.mult, ALU.min).then_inc(vec_ready, 1)
            dve.wait_ge(act_ready, 21)
            link(stt(t_lf, t_lf, 0.0, t_ef, ALU.min, ALU.subtract))
            link(tsc(t_ef, t_lf, -1.0, ALU.mult))
            dve.sem_inc(fac_ready, 1)
            dve.wait_ge(mm_ready, n.next(mm_ready))
            tsc(t_na.rearrange("p t c -> p (t c)"), ps[:, 0, 0:12], -1.0, ALU.mult).then_inc(vec_ready, 1)
            dve.wait_ge(mm_ready, n.next(mm_ready))
            dve.tensor_copy(e_bbc.rearrange("p a s -> p (a s)"),
                            ps[:, 4:7, :].rearrange("p a s -> p (a s)")).then_inc(mm_used, 1)
            dve.wait_ge(mm_used, n.next(mm_used))
            dve.wait_ge(silu_done, 9)
            dve.sem_inc(gate_ready, 1)
            attention(mls, float(P) ** -0.5, None, y3[:, 6:12])
            dve.sem_inc(vec_ready, 1)
            wait_gates("om")
            dve.wait_ge(sq_ready, 4)
            for h in range(M_H):
                last = stt(y3[:, 6 + h], y3[:, 6 + h], colp[:, h, R_MNG:R_MNG + 1], e_gate[:, h], ALU.mult, ALU.mult)
            link(last)
            inverse_roots(e_rn, M_H)
            link(tt(y3[:, 6:12], y3[:, 6:12], e_rn, ALU.mult))
            over()
            dve.wait_ge(lam_landed, 64)
            tt(lam_prod[:, 0], lam_rows[:, 0], lam_rows[:, 1], ALU.mult)
            link(tt(lam_prod[:, 1], lam_rows[:, 2], lam_rows[:, 3], ALU.mult))
            dve.tensor_reduce(lam[:, 0:2], lam_prod, AX, ALU.add).then_inc(vec_ready, 1)
            take("qkc", e_qk, "F")
            take("vc", e_v[:, :, 0:512], "T")
            LAM0 = 0.8 - 0.6 * math.exp(0.0)
            dve.wait_ge(act_ready, 22)
            link(tt(lam[:, 4:5], lam[:, 3:4], lam[:, 2:3], ALU.subtract))
            link(tsc(lam[:, 4:5], lam[:, 4:5], -LAM0, ALU.add))
            dve.sem_inc(gate_ready, 1)
            attention(dif, 64.0 ** -0.5, causal[:], y3[:, 12:16], slopes=slopes_c)
            tsc(e_cut, y3[:, 12:16], LARGE, ALU.min, -LARGE, ALU.max).then_inc(vec_ready, 1)
            dve.wait_ge(root_ready, n.next(root_ready, D_H // 2))
            rn = e_rn[:, 0:4]
            link(tsc(e_fits, rn, ROOT_MAX, ALU.is_lt, SHRINK, ALU.mult))
            link(dve.reciprocal(rn, rn))
            link(tt(rn, rn, e_fits, ALU.mult))
            link(tt(y3[:, 12:16], y3[:, 12:16], rn, ALU.mult))
            for h in range(D_H):
                last = tsc(y3[:, 12 + h], y3[:, 12 + h], colp[:, h, R_CNG:R_CNG + 1], ALU.mult, 1.0 - LAM0, ALU.mult)
            link(last)
            over()
            layer_norm("wout3")
            dve.sem_inc(x_ready, 1)
            take_x()
            layer_norm("down3")
            dve.sem_inc(x_ready, 1)


_INS = [
    "x", "w_in", "gla_w_up", "gla_b", "gla_norm_g", "swa_sinks", "b_merge", "w_branch", "w_o", "ln_g", "ln_b", "w_in_2",
    "conv_dw_w_2", "conv_dw_b_2", "conv_ln_g_2", "conv_ln_b_2", "gdn_conv_w_2", "gdn_A_log_2",
    "gdn_dt_bias_2", "gdn_norm_w_2", "w_out_2", "ln1_g_2", "ln1_b_2", "w_gate_up_2", "w_down_2", "ln2_g_2",
    "ln2_b_2", "w_in_3", "conv_m_3", "b_i_3", "b_f_3", "m_norm_g_3", "lam_q1_3", "lam_k1_3", "lam_q2_3", "lam_k2_3",
    "c_norm_g_3", "w_out_3", "ln1_g_3", "ln1_b_3", "w_up_3", "w_down_3", "ln2_g_3", "ln2_b_3",
]


def _flat(name, a):
    if name == "w_branch":
        return a.reshape(-1, a.shape[-1])
    if name == "x":
        return a.reshape(a.shape[1:])
    return a.reshape(-1, a.shape[-1])


def kernel(**inputs):
    import concourse.bacc as _bacc
    from concourse.bass_utils import run_bass_kernel_spmd as _run

    nc = _bacc.Bacc("TRN2", target_bir_lowering=False, num_devices=1)
    arrays, aps = {}, {}
    for name in _INS:
        a = np.ascontiguousarray(_flat(name, np.asarray(inputs[name])))
        arrays[f"in_{name}"] = a
        aps[name] = nc.dram_tensor(f"in_{name}", a.shape, mybir.dt.from_np(a.dtype), kind="ExternalInput").ap()
    out = nc.dram_tensor("out", (S, D), F32, kind="ExternalOutput").ap()
    build(nc, aps, out)
    r = _run(nc, [arrays], core_ids=[0])
    return r.results[0]["out"].reshape(1, S, D)
```

```python
import math
from contextlib import ExitStack, contextmanager

import concourse.bass as bass
from concourse import mybir
import numpy as np

F32 = mybir.dt.float32
F32R = mybir.dt.float32r
I32 = mybir.dt.int32
ALU = mybir.AluOpType
ACT = mybir.ActivationFunctionType
AX = mybir.AxisListType.X
ds = bass.ds

P = 128
S = 256
D = 2048
KT = D // P
CH = 2
TW = 512
RING = 4
AHEAD = RING - 1
NEG = -1.0e30
TAKEN = -3.0e38
ALPHA = 2.0 ** 0.25
LN_EPS, RMS_EPS = 1e-5, 1e-6

G_H, G_RANK, G_TAU = 4, 16, 16.0
BW = 1024
C_AQ, C_AV, C_ALR, C_AG = 0, 1024, 2048, 2064
C_BQ = C_AG + BW
C_BK = C_BQ + 1024
C_BV = C_BK + 128
C_BG = C_BV + 128
C_CQ = C_BG + BW
C_CV = C_CQ + 2048
C_CG = C_CV + 1024
C_MG = C_CG + BW
CONV_W, SHORT_W, GD_H = 31, 4, 8
D_FF2 = 5632
C_QKV2, C_Z2, C_BA2 = 2048, 5120, 6144
A_H, M_H, D_H = 6, 6, 4
C_VA = 1536
C_QI = 2304
C_KI = C_QI + 512
C_WI = C_KI + 64
C_QM = C_WI + 8
C_VM = C_QM + 1536
C_OM = C_VM + 768
C_IF = C_OM + 768
C_QC = C_IF + 12
C_VC = C_QC + 1024
TOPK = 64
D_FF3 = 8192
SHRINK = 2.0 ** -40
LARGE = 1.0e20
ROOT_MAX = math.sqrt(2.0 ** 128 / P) * SHRINK

R_DWW, R_DWB, R_CLG, R_CLB = 0, 31, 32, 33
R_SCW = 34
R_BM = R_SCW + SHORT_W * 3
R_GLAB = R_BM + 6
R_MNG, R_CNG, R_GLAG = R_GLAB + 1, R_GLAB + 2, R_GLAB + 3
R_CM = R_GLAG + 1
T_GDNW = 2
R_ALL = 64

MERGE = KT // CH + BW // P // CH
WIDTHS = {"alr": G_RANK, "bkv": 3 * P, "ba": 16, "va": 384, "kwi": P + 8, "vm": 384, "om": 384, "if": 12}
PIECES = {"bkv": 3, "kwi": 2}


class Count:

    def __init__(self, start):
        self.n, self.i, self.per = dict(start), None, {}

    def now(self, sem, k=0):
        v = self.n.get(sem, 0)
        self.n[sem] = v + k
        return v if self.i is None else v + self.i * self.per[sem]

    def next(self, sem, k=1):
        self.now(sem, k)
        return self.now(sem)

    @contextmanager
    def loop(self, eng, times, per):
        start = {s: self.n.get(s, 0) for s in per}
        with eng.Fori(0, times) as i:
            self.i, self.per = i, per
            yield i
        self.i, self.per = None, {}
        for s, k in per.items():
            assert self.n.get(s, 0) == start[s] + k, (s, self.n.get(s, 0) - start[s], k)
            self.n[s] = start[s] + times * k


class Section:

    def __init__(self, n, chunks, first, tiles, last):
        self.n, self.chunks, self.first, self.tiles, self.last = n, chunks, first, tuple(tiles), last

    def more(self, it):
        return it * (2 * self.chunks // RING)

    def chunk(self, u, c):
        return self.first + u * self.chunks + c


def plan_weights():
    first = [("aqk", 2), ("av", 2), ("alr", 1), ("ag", 2), ("bq", 2), ("bkv", 1), ("bg", 2),
             ("cqk", 4), ("cv", 2), ("cg", 2), ("merge", 12), ("wo", 4)]
    second = [("cval", 2), ("cgate", 2), ("qkv", 6), ("z", 2), ("ba", 1), ("wout2", 4),
              ("gu", 2 * D_FF2 // TW), ("down2", 4)]
    third = [("qka", 3), ("va", 2), ("qi", 1), ("kwi", 1), ("qkm", 3), ("vm", 2), ("om", 2), ("if", 1),
             ("qkc", 2), ("vc", 1), ("wout3", 4), ("up3", D_FF3 // TW), ("down3", 4)]
    order = first + second + third
    tiles, plan, widths, landed = [0, 0], {}, [], []
    for name, n in order:
        chunks = {"down2": D_FF2 // P // CH, "down3": D_FF3 // P // CH}.get(name, KT // CH)
        plan[name] = Section(n, chunks, len(widths), tiles, name == order[-1][0])
        total = n * (chunks + BW // P // CH) if name == "merge" else n * chunks
        for c in range(total):
            widths.append(WIDTHS.get(name, TW))
            before = landed[-RING] if len(landed) >= RING else 0
            landed.append(before + 16 * PIECES.get(name, 1))
        if name == "merge":
            tiles = [t + n for t in tiles]
        else:
            tiles = [tiles[0] + (n + 1) // 2, tiles[1] + n // 2]
    return plan, widths, landed


def tiles_of(eng, n, unroll=False):
    pairs = n // 2
    if pairs > 1 and not unroll:
        with eng.Fori(0, pairs) as i:
            for u in (0, 1):
                yield 2 * i + u, u, i
    else:
        for i in range(pairs):
            yield 2 * i, 0, i
            yield 2 * i + 1, 1, i
    if n % 2:
        yield n - 1, 0, pairs


def build(nc, I, out):
    plan, widths, landed = plan_weights()
    ctx = ExitStack()
    with ctx:
        free = [-(-nc.sbuf_base // 32) * 32]

        def sb(name, shape, dt=F32, at=None):
            if at is None:
                at = free[0]
                free[0] += -(-4 * int(np.prod(shape[1:])) // 32) * 32
            return nc.alloc_sbuf_tensor_at(name, shape, dt, offset=at)

        def sem(name):
            return ctx.enter_context(nc.semaphore(name))

        ring = sb("ring", [P, RING, CH, TW])
        w_hi = sb("w_hi", [P, RING, CH, TW], F32R)
        w_lo = sb("w_lo", [P, RING, CH, TW], F32R)
        xT_at = free[0]
        x_hi = sb("x_hi", [P, KT, S], F32R)
        x_lo = sb("x_lo", [P, KT, S], F32R)
        xT = sb("xT", [P, 2 * KT, S], at=xT_at)
        xtok = sb("xtok", [P, 2, D])
        ln_gb = sb("ln_gb", [P, 2, D])
        ARENA = 20480
        arena_at = free[0]
        arena = sb("arena", [P, ARENA])

        def rounded(name, at, *shape):
            return sb(name, [P, *shape], F32R, arena_at + 4 * at)

        y1_hi, y1_lo = rounded("y1_hi", 10240, 24, S), rounded("y1_lo", 0, 24, S)
        m_hi, m_lo = rounded("m_hi", 16384, KT, S), rounded("m_lo", 6144, KT, S)
        y_hi, y_lo = rounded("y_hi", 4096, KT, S), rounded("y_lo", 0, KT, S)
        h_hi, h_lo = rounded("h_hi", 16384, RING, CH, S), rounded("h_lo", 18432, RING, CH, S)
        ident = sb("ident", [P, P])
        ones = sb("ones", [P, P])
        upper = sb("upper", [P, S])
        causal = sb("causal", [P, 384])
        band = sb("band", [P, 384])
        causalT = sb("causalT", [P, 384])
        ndist = sb("ndist", [P, 384])
        levels = sb("levels", [P, 7, P])
        colp = sb("colp", [P, 8, R_ALL])
        bmc = sb("bmc", [P, 3, KT])
        small = sb("small", [P, 512])
        alrT = arena[0:G_RANK, 19456:19456 + S]
        gwu = arena[0:G_RANK, 19712:19712 + 512]
        ps = ctx.enter_context(nc.psum_tensor("ps", [P, 8, 512], F32))

        def area(at, *shape):
            n = int(np.prod(shape))
            assert at + n <= ARENA, (at, shape)
            v = arena[:, at:at + n]
            if len(shape) == 2:
                v = v.rearrange("p (a b) -> p a b", b=shape[1])
            elif len(shape) == 3:
                v = v.rearrange("p (a b c) -> p a b c", b=shape[1], c=shape[2])
            return v

        def cols(at, n):
            return small[:, at:at + n]

        eps_ln, eps_rms, one, eps_diff = cols(0, 1), cols(1, 1), cols(2, 1), cols(3, 1)
        sinks = cols(4, 16)
        lam = cols(20, 12)
        gdnA, gdndt = cols(32, 8), cols(40, 8)
        bib, bfb = cols(48, 6), cols(54, 6)
        slopes_a, slopes_c = cols(60, 6), cols(66, 4)
        stat = cols(72, 64)
        nmax, rsum, rinv, esink = cols(136, 4), cols(140, 4), cols(144, 4), cols(148, 4)
        tokc = cols(160, 128)

        w_landed = [sem(f"w_landed{s}") for s in range(RING)]
        hi_ready = [sem(f"hi_ready{s}") for s in range(RING)]
        lo_ready = [sem(f"lo_ready{s}") for s in range(RING)]
        w_used = [sem(f"w_used{s}") for s in range(RING)]
        xh_ready, y_hi_ready, y_split = sem("xh_ready"), sem("y_hi_ready"), sem("y_split")
        h_primed_hi, h_primed = sem("h_primed_hi"), sem("h_primed")
        tile_done = [sem(f"tile_done{u}") for u in range(2)]
        tile_free = [sem(f"tile_free{u}") for u in range(2)]
        x_landed, par_landed, ln_landed = sem("x_landed"), sem("par_landed"), sem("ln_landed")
        out_written = sem("out_written")
        iotas, consts = sem("iotas"), sem("consts")
        dve_order, act_order, pool_order = sem("dve_order"), sem("act_order"), sem("pool_order")
        table_ready, tableT_ready, table_zeroed = sem("table_ready"), sem("tableT_ready"), sem("table_zeroed")
        x_ready, xTp_ready, xTp_used = sem("x_ready"), sem("xTp_ready"), sem("xTp_used")
        var_ready, std_ready = sem("var_ready"), sem("std_ready")
        stage_over = sem("stage_over")
        gate_ready = sem("gate_ready")
        staged = sem("staged")
        logits_ready, logits_used = sem("logits_ready"), sem("logits_used")
        max_ready, exp_done, probs_ready = sem("max_ready"), sem("exp_done"), sem("probs_ready")
        probsT_ready, probsT_out, o_ready, o_used = sem("probsT_ready"), sem("probsT_out"), sem("o_ready"), sem("o_used")
        FREE = {logits_used: 1, o_used: 1, o_ready: 1}
        sq_ready, ss_ready, root_ready = sem("sq_ready"), sem("ss_ready"), sem("root_ready")
        mm_ready, mm_used, vec_ready, act_ready = sem("mm_ready"), sem("mm_used"), sem("vec_ready"), sem("act_ready")
        fac_ready, fac_used = sem("fac_ready"), sem("fac_used")
        lam_landed, hid_ready = sem("lam_landed"), sem("hid_ready")
        conv_ready, silu_done = sem("conv_ready"), sem("silu_done")
        lm_ready, xp_ready, xs_ready, yp_ready, inv_ready = (sem(k) for k in (
            "lm_ready", "xp_ready", "xs_ready", "yp_ready", "inv_ready"))

        y1 = area(0, 24, S)
        mergedT = area(6144, KT, S)
        sig = ln_gb[:, 0, 0:4 * S].rearrange("p (a s) -> p a s", a=4)
        mtmp = ln_gb[:, 0, 4 * S:8 * S].rearrange("p (a s) -> p a s", a=4)
        a_qk, a_v, a_gate = area(6144, 8, S), area(8192, 2, BW), area(10240, 8, S)
        a_b, a_e = area(12288, 4, S), area(13312, 2, 4, S)
        a_qe = area(15360, 2, 4, S)
        a_ke = area(17408, 2, 4, S)
        a_sq, a_rn = area(13312, 8, S), area(15360, 4, S)
        a_at = ln_gb[:, 0, 0:4 * 384].rearrange("p (h n) -> p h n", h=4)
        s_q, s_kd, s_v, s_gate = area(6144, 8, S), area(8192, 2, S), area(10240, 2, P), area(12288, 8, S)
        m_qk, m_v, m_gate = area(6144, 16, S), area(10240, 2, BW), area(12288, 8, S)
        AT1 = 14336
        y2 = area(0, KT, S)
        c_qkv, c_z = area(4096, 24, S), area(10240, 8, S)
        HP, RP = CONV_W - 1, SHORT_W - 1
        c_h = area(12288, 8, HP + S)
        c_acc = area(14576, 8, S)
        c_raw = area(16624, 2, 4, RP + S)
        c_sq = area(12288, 8, S)
        c_mu, c_rs = area(18696, S), area(18952, S)
        l2_sq, l2_rn = xT[:, 0:KT, :], area(12288, 16, S)
        d_at, d_lt, d_l21 = area(12288, 8, 384), area(15360, 16, P), area(17408, 8, P)
        d_xs = area(18432, 16, P)
        d_lm = ln_gb[:, 1, :].rearrange("p (a b) -> p a b", b=P)
        d_dt = ln_gb[:, 1, 0:768].rearrange("p (a b) -> p a b", b=384)
        d_db = ln_gb[:, 1, 768:1536].rearrange("p (a b) -> p a b", b=384)
        d_vb = ln_gb[:, 0, :].rearrange("p (t n) -> p t n", t=2)
        d_t = xT[:, 0:8, :].rearrange("p a (c i) -> p (a c) i", c=2)
        d_tt = xT[:, 8:16, :].rearrange("p a (c i) -> p (a c) i", c=2)
        d_vn = area(8192, 2, 1024)
        d_sq, d_rn = xT[:, 0:8, :], xT[:, 8:16, :]
        hid = area(0, D_FF3 // P, S)
        f_sg = area(16384, 2, 4, S)
        t_ba = tokc[:, 0:32].rearrange("p (t c) -> p t c", t=2)
        t_beta = tokc[:, 32:48].rearrange("p (t c) -> p t c", t=2)
        t_x = tokc[:, 48:64].rearrange("p (t c) -> p t c", t=2)
        t_e = tokc[:, 64:80].rearrange("p (t c) -> p t c", t=2)
        t_A = tokc[:, 80:88]
        t_g = tokc[:, 88:104].rearrange("p (t c) -> p t c", t=2)
        t_gc = tokc[:, 104:120].rearrange("p (t c) -> p t c", t=2)
        scw = small[:, 288:384].rearrange("p (k c) -> p k c", k=SHORT_W)
        y3 = area(0, KT, S)
        e_qk, e_v, e_gate = area(4096, 12, S), area(7168, 2, 768), area(8704, 6, S)
        AT3 = 10240
        i_q, i_k = area(14080, 4, S), area(15104, S)
        i_sel, i_work, i_tmp = area(15360, 384), area(15744, 384), area(16128, 384)
        e_raw = area(14080, 2, 4, RP + S)
        e_bbc = area(16896, 6, S)
        e_cut, e_fits = area(16896, 4, S), area(17920, 4, S)
        e_sq, e_rn = area(AT3, 6, S), area(AT3 + 1536, 6, S)
        lam_rows = area(18944, 4, 64)
        lam_prod = area(19200, 2, 64)
        t_w = tokc[:, 0:16].rearrange("p (t c) -> p t c", t=2)
        top8 = tokc[:, 16:32].rearrange("p (t c) -> p t c", t=2)
        t_if = tokc[:, 32:56].rearrange("p (t c) -> p t c", t=2)
        t_lf = tokc[:, 56:68].rearrange("p (t c) -> p t c", t=2)
        t_ef = tokc[:, 68:80].rearrange("p (t c) -> p t c", t=2)
        t_na = tokc[:, 80:92].rearrange("p (t c) -> p t c", t=2)
        mcw = small[:, 384:432].rearrange("p (k c) -> p k c", k=SHORT_W)
        table = area(0, 1024)
        row = "(k p) c -> p k c"

        block = ctx.enter_context(nc.Block())

        class Heads:

            def __init__(self, kind, pairs, d, dv, at):
                self.kind, self.pairs, self.d, self.dv = kind, pairs, d, dv
                self.qs, self.ks = area(at, 2, S), area(at + 512, 2, S)
                self.vs = area(at + 1024, 2, 2, P)
                self.sm = area(at + 1536, 2, 384)
                self.p = area(at + 2304, 2, 384)
                self.pT = area(at + 3072, 2, 384)
                self.outs = 1 if kind == "diff" else 2
                self.halves = kind in ("swa", "diff")

            def at(self, u):
                return (64 * u, 64 * u + 64) if self.halves else (0, P)

        swa = [Heads("swa", 4, 64, 64, AT1) for _ in range(2)]
        moba = Heads("moba", 4, P, P, AT1)
        dsa = Heads("dsa", A_H // 2, P, P, AT3)
        mls = Heads("mlstm", M_H // 2, P, P, AT3)
        dif = Heads("diff", D_H, 64, P, AT3)

        @block.sync
        def _(sp):
            n = Count(FREE)

            def held(v):
                return v if isinstance(v, int) else sp.snap(v)

            def load(g, more, pieces):
                if g >= RING:
                    sp.wait_ge(lo_ready[g % RING], g // RING + more)
                at = 0
                for src in pieces:
                    sp.dma_start(ring[:, g % RING, :, at:at + src.shape[1]], src.rearrange(row, p=P))\
                      .then_inc(w_landed[g % RING], 16)
                    at += src.shape[1]

            def rows(c):
                return slice(c * CH * P, (c + 1) * CH * P)

            def tile_loads(name, w, col, width=TW, second=None):
                sec = plan[name]
                for t, u, it in tiles_of(sp, sec.n):
                    at = held(col + t * width if second is None else col + u * second + it * width)
                    for c in range(sec.chunks):
                        load(sec.chunk(u, c), sec.more(it), [w[rows(c), ds(at, width)]])

            def piece_loads(name, w, pieces):
                sec = plan[name]
                for c in range(sec.chunks):
                    load(sec.chunk(0, c), 0, [w[rows(c), col:col + width] for col, width in pieces])

            w = I["w_in"]
            tile_loads("aqk", w, C_AQ)
            tile_loads("av", w, C_AV)
            piece_loads("alr", w, [(C_ALR, G_RANK)])
            tile_loads("ag", w, C_AG)
            tile_loads("bq", w, C_BQ)
            piece_loads("bkv", w, [(C_BK, 64), (C_BK, P), (C_BK + 64, 64 + P)])
            tile_loads("bg", w, C_BG)
            tile_loads("cqk", w, C_CQ)
            tile_loads("cv", w, C_CV)
            tile_loads("cg", w, C_CG)
            sec = plan["merge"]
            with sp.Fori(0, 4) as j:
                for b in range(3):
                    gate_at = held(C_MG + b * D + j * TW)
                    branch_at = held(j * TW)
                    for c in range(MERGE):
                        g, more = sec.first + b * MERGE + c, j * (3 * MERGE // RING)
                        if c < sec.chunks:
                            load(g, more, [w[rows(c), ds(gate_at, TW)]])
                        elif c > sec.chunks:
                            load(g, more, [I["w_branch"][rows(b * (BW // P // CH) + c - sec.chunks), ds(branch_at, TW)]])
            tile_loads("wo", I["w_o"], 0)
            w = I["w_in_2"]
            tile_loads("cval", w, 0)
            tile_loads("cgate", w, 1024)
            tile_loads("qkv", w, C_QKV2)
            tile_loads("z", w, C_Z2)
            piece_loads("ba", w, [(C_BA2, 16)])
            tile_loads("wout2", I["w_out_2"], 0)
            tile_loads("gu", I["w_gate_up_2"], 0, second=D_FF2)
            tile_loads("down2", I["w_down_2"], 0)
            w = I["w_in_3"]
            tile_loads("qka", w, 0)
            tile_loads("va", w, C_VA, 384)
            tile_loads("qi", w, C_QI)
            piece_loads("kwi", w, [(C_KI, 64), (C_KI, 64 + 8)])
            tile_loads("qkm", w, C_QM)
            tile_loads("vm", w, C_VM, 384)
            tile_loads("om", w, C_OM, 384)
            piece_loads("if", w, [(C_IF, 12)])
            tile_loads("qkc", w, C_QC)
            tile_loads("vc", w, C_VC)
            tile_loads("wout3", I["w_out_3"], 0)
            tile_loads("up3", I["w_up_3"], 0)
            tile_loads("down3", I["w_down_3"], 0)
            sp.wait_ge(x_ready, 6)
            sp.dma_start(out.rearrange("(t p) c -> p t c", p=P), xtok[:]).then_inc(out_written, 16)
            sp.wait_ge(out_written, 16)

        posi = area(2048, P)
        posj = area(2048 + P, P)
        posx = area(2048 + 2 * P, P)
        posy = area(2048 + 3 * P, P)

        @block.gpsimd
        def _(pool):
            n = Count(FREE)
            pool.iota(posi.bitcast(I32), [[1, P]], base=0, channel_multiplier=0).then_inc(iotas, 1)
            pool.iota(posj.bitcast(I32), [[0, P]], base=0, channel_multiplier=1).then_inc(iotas, 1)

            def stage_pair(A, items):
                pool.wait_ge(o_ready, n.now(o_ready, 1))
                for dst, src in items[:-1]:
                    pool.tensor_copy(dst, src)
                pool.tensor_copy(*items[-1]).then_inc(staged, 1)

            def stage_heads(A, q, k, v, koff):
                pool.wait_ge(gate_ready, n.next(gate_ready))
                with n.loop(pool, A.pairs, {o_ready: 1}) as i:
                    items = []
                    for u in range(A.outs):
                        h = A.outs * i + u
                        items += [(A.qs[:, u], q[:, ds(h, 1), :].rearrange("p a s -> p (a s)")),
                                  (A.ks[:, u], k[:, ds(koff + h, 1), :].rearrange("p a s -> p (a s)")),
                                  (A.vs[:, u], v[:, :, ds(h * A.dv, A.dv)])]
                    stage_pair(A, items)

            def stage_swa(A, g):
                if g == 0:
                    pool.wait_ge(gate_ready, n.next(gate_ready))
                with n.loop(pool, A.pairs, {o_ready: 1}) as i:
                    stage_pair(A, [(A.qs[:, 0], s_q[:, ds(4 * g + i, 1), :].rearrange("p a s -> p (a s)"))])

            for g in range(2):
                stage_swa(swa[g], g)
            stage_heads(moba, m_qk, m_qk, m_v, 8)
            stage_heads(dsa, e_qk, e_qk, e_v, 6)
            stage_heads(mls, e_qk, e_qk, e_v, 6)
            stage_heads(dif, e_qk, e_qk, e_v, 4)

        @block.tensor
        def _(pe):
            n = Count(FREE)

            def products(out, left, right, start, stop):
                first = pe.matmul(out, left[0], right[0], start=start, stop=False)
                pe.matmul(out, left[0], right[1], start=False, stop=False)
                return first, pe.matmul(out, left[1], right[0], start=False, stop=stop)

            def chunk(g, more):
                pe.wait_ge(lo_ready[g % RING], g // RING + 1 + more)

            def tile(kind, u, g, more, chunks, src, width):
                for c in range(chunks):
                    s = (g + c) % RING
                    chunk(g + c, more)
                    x = src(c, s)
                    for k in range(CH):
                        for e in range(width // P if kind == "F" else 2):
                            go, end = c == 0 and k == 0, c == chunks - 1 and k == CH - 1
                            if kind == "F":
                                out, go = ps[:, 2 * u + e // 2, (e % 2) * S:(e % 2) * S + S], go and e % 2 == 0
                                end = end and (e % 2 == 1 or e == width // P - 1)
                                wv = [v[:, s, k, e * P:(e + 1) * P] for v in (w_hi, w_lo)]
                                first, last = products(out, wv, [v[:, k, :] for v in x], go, end)
                            else:
                                out = ps[:, 2 * u + e, 0:width]
                                wv = [v[:, s, k, 0:width] for v in (w_hi, w_lo)]
                                first, last = products(out, [v[:, k, e * P:(e + 1) * P] for v in x], wv, go, end)
                            if k == 0 and e == 0 and g + c > 0:
                                first.then_inc(w_used[(g + c - 1) % RING], 1)
                return last

            def stationary(hi, lo, at=0):
                return lambda c, s: [v[:, at + c * CH:at + (c + 1) * CH, :] for v in (hi, lo)]

            def project(name, kind, src=stationary(x_hi, x_lo), width=TW):
                sec = plan[name]
                for t, u, it in tiles_of(pe, sec.n):
                    pe.wait_ge(tile_free[u], sec.tiles[u] + it)
                    tile(kind, u, sec.chunk(u, 0), sec.more(it), sec.chunks, src, width).then_inc(tile_done[u], 1)

            def project_pieces(name, ops):
                sec = plan[name]
                closes = {bank: (kind, col, int(kind == "T")) for kind, col, m, bank, at in ops}
                pe.wait_ge(tile_free[0], sec.tiles[0])
                for c in range(sec.chunks):
                    g = sec.chunk(0, c)
                    chunk(g, 0)
                    for k in range(CH):
                        x = [v[:, c * CH + k, :] for v in (x_hi, x_lo)]
                        banks = set()
                        for kind, col, m, bank, at in ops:
                            w = [v[:, g % RING, k, col:col + m] for v in (w_hi, w_lo)]
                            for e in range(1 if kind == "F" else 2):
                                go = c == 0 and k == 0 and bank not in banks
                                end = c == sec.chunks - 1 and k == CH - 1 and (kind, col, e) == closes[bank]
                                if kind == "F":
                                    first, last = products(ps[0:m, bank, at:at + S], w, x, go, end)
                                else:
                                    first, last = products(ps[:, bank, at + e * m:at + e * m + m],
                                                           [v[:, e * P:(e + 1) * P] for v in x], w, go, end)
                                if not banks and k == 0 and g > 0:
                                    first.then_inc(w_used[(g - 1) % RING], 1)
                                banks.add(bank)
                last.then_inc(tile_done[0], 1)

            def transpose_x():
                pe.wait_ge(x_ready, n.next(x_ready))
                for g in range(KT // 2):
                    pe.wait_ge(xTp_used, max(0, n.now(xTp_used, 1) - 3))
                    for k in range(2):
                        for t in range(2):
                            last = pe.transpose(ps[:, 4 + g % 4, k * S + t * P:k * S + (t + 1) * P],
                                                xtok[:, t, (2 * g + k) * P:(2 * g + k + 1) * P], ident[:])
                    last.then_inc(xTp_ready, 1)

            def attend(A, k_of, v_of, first=True, stages=True):
                with n.loop(pe, A.pairs, {staged: 1, logits_used: 2, probs_ready: A.outs, probsT_out: A.outs, o_used: 1}):
                    pe.wait_ge(staged, n.next(staged))
                    pe.wait_ge(logits_used, n.now(logits_used, 2))
                    for u in range(2):
                        a, b = A.at(u)
                        q = A.qs[a:b, 0 if A.halves else u]
                        k = k_of(u)
                        pe.matmul(ps[:, 4 + u, 0:P], q[:, 0:P], k[:, 0:P], start=True, stop=True)
                        pe.matmul(ps[:, 4 + u, P:384], q[:, P:S], k[:, 0:S], start=True, stop=True).then_inc(logits_ready, 1)
                    for u in range(A.outs):
                        pe.wait_ge(probs_ready, n.next(probs_ready))
                        for c in range(3):
                            last = pe.transpose(ps[:, 6 + u, c * P:(c + 1) * P], A.p[:, u, c * P:(c + 1) * P], ident[:])
                        last.then_inc(probsT_ready, 1)
                    pe.wait_ge(o_used, n.now(o_used, 1))
                    for u in range(A.outs):
                        pe.wait_ge(probsT_out, n.next(probsT_out))
                        a, b = A.at(u)
                        o = ps[a:b, 2, 0:S] if A.kind == "swa" else ps[:, 2 + u, 0:S]
                        v = v_of(u)
                        pe.matmul(o, v[:, 0, :], A.pT[:, u, 0:S], start=True, stop=False)
                        last = pe.matmul(o[:, P:S], v[:, 1, :], A.pT[:, u, S:384], start=False, stop=True)
                    last.then_inc(o_ready, 1)
                pe.wait_ge(o_used, n.now(o_used))

            def square_sums(src, heads, tiles):
                pe.wait_ge(sq_ready, n.next(sq_ready))
                for g in range(heads // 2):
                    if g >= 4:
                        pe.wait_ge(root_ready, n.next(root_ready))
                    for e in range(tiles):
                        v = src[:, 2 * g * tiles:(2 * g + 2) * tiles, :].rearrange("p (h e) s -> p h e s", e=tiles)
                        last = pe.matmul(ps[:, 4 + g % 4, :].rearrange("p (h s) -> p h s", h=2), ones[:], v[:, :, e, :],
                                         start=(e == 0), stop=(e == tiles - 1))
                    last.then_inc(ss_ready, 1)
                pe.wait_ge(root_ready, n.next(root_ready, min(4, heads // 2)))

            hidden = lambda c, s: (h_hi[:, s], h_lo[:, s])

            pe.sem_inc(o_ready, 1)
            pe.wait_ge(consts, 1)
            pe.wait_ge(par_landed, 16 * 18)
            for t in range(8):
                last = pe.transpose(ps[:, 0, t * R_ALL:(t + 1) * R_ALL], table[0:R_ALL, t * P:(t + 1) * P],
                                    ident[0:R_ALL, 0:R_ALL])
            last.then_inc(tableT_ready, 1)
            transpose_x()
            pe.wait_ge(xTp_used, n.now(xTp_used))
            pe.wait_ge(table_ready, 1)

            project("aqk", "F")
            project("av", "T")
            project_pieces("alr", [("F", 0, G_RANK, 0, 0)])
            project("ag", "F")
            pe.wait_ge(vec_ready, n.next(vec_ready))
            for h in range(G_H):
                last = pe.matmul(ps[:, 4 + h // 2, (h % 2) * S:(h % 2 + 1) * S], gwu[:, h * P:(h + 1) * P], alrT,
                                 start=True, stop=True)
            last.then_inc(mm_ready, 1)
            for lv in range(8):
                pe.wait_ge(fac_ready, n.next(fac_ready))
                b = 4 + 2 * (lv % 2)
                if lv < 7:
                    pe.wait_ge(mm_used, max(0, n.now(mm_used, 1) - 1))
                    for h in range(G_H):
                        for c in range(2):
                            last = pe.matmul(ps[:, b + h // 2, (h % 2) * S + c * P:(h % 2) * S + (c + 1) * P],
                                             a_ke[:, lv % 2, h, c * P:(c + 1) * P], a_qe[:, lv % 2, h, c * P:(c + 1) * P],
                                             start=True, stop=True)
                else:
                    pe.wait_ge(mm_used, max(0, n.now(mm_used, 1) - 1))
                    for h in range(G_H):
                        last = pe.matmul(ps[:, b, h * P:(h + 1) * P], a_ke[:, 1, h, 0:P], a_qe[:, 1, h, P:S],
                                         start=True, stop=True)
                last.then_inc(mm_ready, 1)
            pe.wait_ge(fac_ready, n.next(fac_ready))
            pe.wait_ge(mm_used, max(0, n.now(mm_used, 1) - 1))
            for h in range(G_H):
                for c in range(2):
                    last = pe.matmul(ps[:, 4 + h // 2, (h % 2) * S + c * P:(h % 2) * S + (c + 1) * P],
                                     a_qk[:, 4 + h, c * P:(c + 1) * P], a_qe[:, 0, h, c * P:(c + 1) * P],
                                     start=True, stop=True)
            last.then_inc(mm_ready, 1)
            pe.wait_ge(mm_used, n.now(mm_used))
            for h in range(G_H):
                for e in range(2):
                    o = ps[:, 4 + h, e * S:(e + 1) * S]
                    v = a_v[:, :, h * S + e * P:h * S + (e + 1) * P]
                    pe.matmul(o, v[:, 0, :], a_at[:, h, 0:S], start=True, stop=False)
                    last = pe.matmul(o[:, P:S], v[:, 1, :], a_at[:, h, S:384], start=False, stop=True)
            last.then_inc(mm_ready, 1)
            square_sums(a_sq, G_H, 2)

            pe.wait_ge(stage_over, 1)
            project("bq", "F")
            project_pieces("bkv", [("F", 0, P, 0, 0), ("F", P, P, 0, S), ("T", 2 * P, P, 1, 0)])
            project("bg", "F")
            pe.wait_ge(gate_ready, n.next(gate_ready))
            for g in range(2):
                attend(swa[g], lambda u: s_kd[64 * u:64 * u + 64, g], lambda u: s_v[:, :, g * 64:(g + 1) * 64])

            project("cqk", "F")
            project("cv", "T")
            project("cg", "F")
            attend(moba, lambda u: moba.ks[:, u], lambda u: moba.vs[:, u])

            sec = plan["merge"]
            with pe.Fori(0, 4) as j:
                for b in range(3):
                    it, g, more = 3 * j + b, sec.first + b * MERGE, j * (3 * MERGE // RING)
                    pe.wait_ge(tile_free[0], sec.tiles[0] + it)
                    tile("F", 0, g, more, sec.chunks, stationary(x_hi, x_lo), TW).then_inc(tile_done[0], 1)
                    pe.wait_ge(tile_free[1], sec.tiles[1] + it)
                    if b == 0:
                        pe.wait_ge(y_split, 3)
                    tile("F", 1, g + sec.chunks, more, MERGE - sec.chunks, stationary(y1_hi, y1_lo, 8 * b), TW)\
                        .then_inc(tile_done[1], 1)
            pe.wait_ge(stage_over, 4)
            project("wo", "T", stationary(m_hi, m_lo))
            transpose_x()
            pe.wait_ge(xTp_used, n.now(xTp_used))
            project("cval", "F")
            project("cgate", "F")
            project("qkv", "F")
            project("z", "F")
            project_pieces("ba", [("T", 0, 16, 0, 0)])
            for b, src in ((4, c_acc), (5, c_sq)):
                pe.wait_ge(conv_ready, n.next(conv_ready))
                for t in range(8):
                    last = pe.matmul(ps[:, b, 0:S], ones[:], src[:, t, :], start=(t == 0), stop=(t == 7))
                last.then_inc(mm_ready, 1)
            square_sums(l2_sq, 16, 1)
            pe.wait_ge(fac_ready, n.next(fac_ready))
            pe.matmul(ps[:, 0, 0:8], upper[:, 0:P], t_g[:, 0], start=True, stop=True)
            pe.matmul(ps[:, 0, 8:16], ones[:], t_g[:, 0], start=True, stop=False)
            pe.matmul(ps[:, 0, 8:16], upper[:, 0:P], t_g[:, 1], start=False, stop=True)
            for t in range(2):
                for h in range(GD_H):
                    last = pe.transpose(ps[:, 4 + 2 * t + h // 4, (h % 4) * P:(h % 4 + 1) * P],
                                        c_qkv[:, 16 + h, t * P:(t + 1) * P], ident[:])
            last.then_inc(mm_ready, 1)
            pe.wait_ge(fac_ready, n.next(fac_ready))
            for h in range(GD_H):
                b = 2 + 3 * (h % 2)
                if h >= 2:
                    pe.wait_ge(fac_ready, n.next(fac_ready))
                g = [t_g[:, t, h:h + 1].to_broadcast([P, P]) for t in range(2)]
                beta = [t_beta[:, t, h:h + 1].to_broadcast([P, P]) for t in range(2)]
                pe.matmul(ps[:, b, 0:S], g[0], upper[:], start=True, stop=False)
                pe.matmul(ps[:, b, P:S], g[1], upper[:, 0:P], start=False, stop=True)
                for t in range(2):
                    pe.matmul(ps[:, b, S + t * P:S + (t + 1) * P], beta[t], ident[:], start=True, stop=True)
                q, k = c_qkv[:, h], c_qkv[:, 8 + h]
                for c, r in ((1, k), (2, q)):
                    pe.matmul(ps[:, b + c, 0:S], k[:, 0:P], r, start=True, stop=True)
                    last = pe.matmul(ps[:, b + c, S:384], k[:, P:S], r[:, P:S], start=True, stop=True)
                last.then_inc(mm_ready, 1)
            pe.wait_ge(fac_ready, n.next(fac_ready, 2))
            pe.wait_ge(inv_ready, n.next(inv_ready, 4))
            with n.loop(pe, 7, {lm_ready: 4, xs_ready: 4, inv_ready: 4}):
                for g in range(4):
                    pe.wait_ge(lm_ready, n.next(lm_ready))
                    for e in range(4):
                        last = pe.matmul(ps[:, g, e * P:(e + 1) * P], d_lm[:, 4 * g + e], d_t[:, 4 * g + e],
                                         start=True, stop=True)
                    last.then_inc(xp_ready, 1)
                for g in range(4):
                    pe.wait_ge(xs_ready, n.next(xs_ready))
                    if g >= 2:
                        pe.wait_ge(inv_ready, n.next(inv_ready))
                    for e in range(4):
                        pe.matmul(ps[:, 4 + g % 2, e * P:(e + 1) * P], d_tt[:, 4 * g + e], d_xs[:, 4 * g + e],
                                  start=True, stop=True)
                    for e in range(4):
                        last = pe.matmul(ps[:, 6 + g % 2, e * P:(e + 1) * P], d_xs[:, 4 * g + e], d_tt[:, 4 * g + e],
                                         start=True, stop=True)
                    last.then_inc(yp_ready, 1)
                pe.wait_ge(inv_ready, n.next(inv_ready, 2))
            def by_head(b, left, right):
                for h in range(GD_H):
                    last = pe.matmul(ps[:, b + h // 4, (h % 4) * P:(h % 4 + 1) * P], left(h), right(h),
                                     start=True, stop=True)
                last.then_inc(mm_ready, 1)
            head = lambda v, t: lambda h: v[:, t, h * P:(h + 1) * P]
            by_head(0, lambda h: d_tt[:, 2 * h], head(d_vb, 0))
            pe.wait_ge(fac_ready, n.next(fac_ready))
            by_head(2, lambda h: d_l21[:, h], head(d_vn, 0))
            pe.wait_ge(fac_ready, n.next(fac_ready))
            by_head(0, lambda h: d_tt[:, 2 * h + 1], head(d_vb, 1))
            pe.wait_ge(fac_ready, n.next(fac_ready))
            for h in range(GD_H):
                o = ps[:, 4 + h // 2, (h % 2) * S:(h % 2 + 1) * S]
                pe.matmul(o, d_vn[:, 0, h * P:(h + 1) * P], d_at[:, h, 0:S], start=True, stop=False)
                last = pe.matmul(o[:, P:S], d_vn[:, 1, h * P:(h + 1) * P], d_at[:, h, S:384], start=False, stop=True)
            last.then_inc(mm_ready, 1)
            square_sums(d_sq, GD_H, 1)
            pe.wait_ge(stage_over, 5)
            project("wout2", "T", stationary(y_hi, y_lo))
            transpose_x()
            pe.wait_ge(xTp_used, n.now(xTp_used))
            project("gu", "F")
            pe.wait_ge(h_primed, AHEAD)
            project("down2", "T", hidden)
            transpose_x()
            pe.wait_ge(xTp_used, n.now(xTp_used))
            project("qka", "F")
            project("va", "T", width=384)
            project("qi", "F")
            project_pieces("kwi", [("F", 0, P, 0, 0), ("T", P, 8, 0, S)])
            pe.wait_ge(fac_ready, 23)
            for h in range(8):
                b = 4 + h % 4
                if h >= 4:
                    pe.wait_ge(mm_used, n.next(mm_used))
                q, k = i_q[64 * (h % 2):64 * (h % 2) + 64, h // 2], i_k[64 * (h % 2):64 * (h % 2) + 64]
                pe.matmul(ps[:, b, 0:P], q[:, 0:P], k[:, 0:P], start=True, stop=True)
                pe.matmul(ps[:, b, P:384], q[:, P:S], k, start=True, stop=True).then_inc(mm_ready, 1)
            pe.wait_ge(mm_used, n.next(mm_used, 4))
            attend(dsa, lambda u: dsa.ks[:, u], lambda u: dsa.vs[:, u])
            project("qkm", "F")
            project("vm", "T", width=384)
            project("om", "F", width=384)
            project_pieces("if", [("T", 0, 12, 0, 0)])
            pe.wait_ge(fac_ready, 24)
            pe.matmul(ps[:, 0, 0:6], upper[:, 0:P], t_lf[:, 0], start=True, stop=True)
            pe.matmul(ps[:, 0, 6:12], ones[:], t_lf[:, 0], start=True, stop=False)
            pe.matmul(ps[:, 0, 6:12], upper[:, 0:P], t_lf[:, 1], start=False, stop=True).then_inc(mm_ready, 1)
            for h in range(M_H):
                o = ps[:, 4 + h // 2, (h % 2) * S:(h % 2 + 1) * S]
                lf = [t_ef[:, t, h:h + 1].to_broadcast([P, P]) for t in range(2)]
                li = [t_if[:, t, h:h + 1].to_broadcast([P, P]) for t in range(2)]
                pe.matmul(o, lf[0], upper[:], start=True, stop=False)
                pe.matmul(o[:, P:S], lf[1], upper[:, 0:P], start=False, stop=False)
                pe.matmul(o[:, 0:P], li[0], ident[:], start=False, stop=False)
                last = pe.matmul(o[:, P:S], li[1], ident[:], start=False, stop=True)
            last.then_inc(mm_ready, 1)
            pe.wait_ge(mm_used, n.next(mm_used))
            attend(mls, lambda u: mls.ks[:, u], lambda u: mls.vs[:, u])
            square_sums(e_sq, M_H, 1)
            project("qkc", "F")
            project("vc", "T")
            attend(dif, lambda u: dif.ks[64 * u:64 * u + 64, 0], lambda u: dif.vs[:, 0])
            square_sums(e_sq, D_H, 1)
            pe.wait_ge(stage_over, 8)
            project("wout3", "T", stationary(y_hi, y_lo))
            transpose_x()
            pe.wait_ge(xTp_used, n.now(xTp_used))
            project("up3", "F")
            pe.wait_ge(h_primed, 2 * AHEAD)
            project("down3", "T", hidden)

        @block.scalar
        def _(act):
            n = Count(FREE)

            def link(ins):
                ins.then_inc(act_order, 1)
                act.wait_ge(act_order, n.next(act_order))

            act.dma_start(xtok[:], I["x"].rearrange("(t p) c -> p t c", p=P)).then_inc(x_landed, 16)
            act.wait_ge(table_zeroed, 1)
            for dst, src in [
                (table[R_DWW:R_DWW + CONV_W, :], I["conv_dw_w_2"]),
                (table[R_DWB:R_DWB + 1, :], I["conv_dw_b_2"]),
                (table[R_CLG:R_CLG + 1, :], I["conv_ln_g_2"]),
                (table[R_CLB:R_CLB + 1, :], I["conv_ln_b_2"]),
                (table[R_SCW:R_SCW + 12, :], I["gdn_conv_w_2"].rearrange("k (a c) -> (k a) c", c=1024)),
                (table[R_BM:R_BM + 6, :], I["b_merge"].rearrange("b (a c) -> (b a) c", c=1024)),
                (table[R_GLAB:R_GLAB + 1, 0:512], I["gla_b"]),
                (table[R_MNG:R_MNG + 1, 0:768], I["m_norm_g_3"]),
                (table[R_CNG:R_CNG + 1, 0:512], I["c_norm_g_3"]),
                (table[R_GLAG:R_GLAG + 1, 0:256], I["gla_norm_g"]),
                (table[R_GLAG:R_GLAG + 1, T_GDNW * P:(T_GDNW + 1) * P], I["gdn_norm_w_2"]),
                (table[R_CM:R_CM + 8, 0:768], I["conv_m_3"].rearrange("k (a c) -> (k a) c", c=768)),
                (gwu, I["gla_w_up"]),
                (sinks, I["swa_sinks"].to_broadcast([P, 16])),
                (gdnA, I["gdn_A_log_2"].to_broadcast([P, 8])),
                (gdndt, I["gdn_dt_bias_2"].to_broadcast([P, 8])),
                (bib, I["b_i_3"].to_broadcast([P, 6])),
                (bfb, I["b_f_3"].to_broadcast([P, 6])),
            ]:
                act.dma_start(dst, src).then_inc(par_landed, 16)

            def split(g, more=0, rows=None):
                s, width = g % RING, TW
                if isinstance(more, int):
                    g, more = g + more * RING, 0
                    if g >= len(widths):
                        return
                    width = widths[g]
                act.wait_ge(w_landed[s], landed[g] + more * 16)
                if g >= RING:
                    act.wait_ge(w_used[s], g // RING + more)
                last = act.activation(w_hi[:, s, :, 0:width], ring[:, s, :, 0:width], ACT.Copy)
                if rows is not None:
                    last = act.activation(h_hi[:, s], hid[:, rows:rows + CH, :], ACT.Copy)
                last.then_inc(hi_ready[s], 1)

            def splits(sec, u, it, hidden=False):
                for c in range(AHEAD, AHEAD + sec.chunks):
                    split(sec.chunk(u, c), sec.more(it), c % sec.chunks * CH if hidden else None)

            def pass_by(*names, hidden=False):
                for name in names:
                    for t, u, it in tiles_of(act, plan[name].n, plan[name].last):
                        splits(plan[name], u, it, hidden)

            def prime_hidden(name):
                for c in range(AHEAD):
                    s = plan[name].chunk(0, c) % RING
                    act.activation(h_hi[:, s], hid[:, c * CH:(c + 1) * CH, :], ACT.Copy).then_inc(h_primed_hi, 1)

            def take_x():
                for g in range(KT // 2):
                    act.wait_ge(xTp_ready, n.next(xTp_ready))
                    act.activation(x_hi[:, 2 * g:2 * g + 2, :].rearrange("p a s -> p (a s)"), ps[:, 4 + g % 4, :], ACT.Copy)\
                       .then_inc(xh_ready, 1)

            def load_ln(g, b):
                act.dma_start(ln_gb[:, 0, :], g.to_broadcast([P, D])).then_inc(ln_landed, 16)
                act.dma_start(ln_gb[:, 1, :], b.to_broadcast([P, D])).then_inc(ln_landed, 16)

            def gates(name, dst, func, width=TW):
                sec = plan[name]
                per = width // P
                for t, u, it in tiles_of(act, sec.n):
                    splits(sec, u, it)
                    act.wait_ge(tile_done[u], sec.tiles[u] + it + 1)
                    act.activation(dst[:, ds(t * per, per), :].rearrange("p a s -> p (a s)"),
                                   ps[:, 2 * u:2 * u + 2, :].rearrange("p a s -> p (a s)")[:, 0:per * S],
                                   func).then_inc(tile_free[u], 1)

            def softmax_exp(A, sink=None):
                per = {max_ready: 2, probsT_ready: A.outs}
                with n.loop(act, A.pairs, per) as i:
                    for u in range(2):
                        act.wait_ge(max_ready, n.next(max_ready))
                        if sink is not None:
                            for t in range(2):
                                act.activation(esink[:, 2 * u + t:2 * u + t + 1], sink(i, u, t), ACT.Exp,
                                               bias=nmax[:, 2 * u + t:2 * u + t + 1])
                        sums = {} if A.kind == "mlstm" else {"accum_out": rsum[:, 2 * u:2 * u + 1]}
                        act.activation(A.p[:, u, 0:P], A.sm[:, u, 0:P], ACT.Exp, bias=nmax[:, 2 * u:2 * u + 1], **sums)
                        sums = {} if A.kind == "mlstm" else {"accum_out": rsum[:, 2 * u + 1:2 * u + 2]}
                        act.activation(A.p[:, u, P:384], A.sm[:, u, P:384], ACT.Exp, bias=nmax[:, 2 * u + 1:2 * u + 2],
                                       **sums).then_inc(exp_done, 1)
                    for u in range(A.outs):
                        act.wait_ge(probsT_ready, n.next(probsT_ready))
                        act.activation(A.pT[:, u], ps[:, 6 + u, 0:384], ACT.Copy).then_inc(probsT_out, 1)

            def roots(dst, heads, scale, eps):
                for g in range(heads // 2):
                    act.wait_ge(ss_ready, n.next(ss_ready))
                    last = act.activation(dst[:, 2 * g:2 * g + 2, :].rearrange("p a s -> p (a s)"), ps[:, 4 + g % 4, :],
                                          ACT.Sqrt, bias=eps, scale=scale)
                    last.then_inc(root_ready, 1)

            def ln_roots():
                act.wait_ge(var_ready, n.next(var_ready))
                act.activation(stat[:, 28:30], stat[:, 26:28], ACT.Sqrt, bias=eps_ln).then_inc(std_ready, 1)

            for g in range(AHEAD):
                split(g)
            take_x()
            pass_by("aqk", "av", "alr")
            gates("ag", a_gate, ACT.Silu)
            act.wait_ge(vec_ready, n.next(vec_ready, 2))
            link(act.activation(a_e[:, 0], a_e[:, 0], ACT.Exp))
            act.activation(a_e[:, 0], a_e[:, 0], ACT.Ln, bias=one).then_inc(act_ready, 1)
            for lv in range(8):
                act.wait_ge(vec_ready, n.next(vec_ready))
                act.activation(a_e[:, lv % 2], a_e[:, lv % 2], ACT.Exp).then_inc(act_ready, 1)
            act.wait_ge(vec_ready, n.next(vec_ready))
            act.activation(a_sq, y1[:, 0:8, :], ACT.Square).then_inc(sq_ready, 1)
            roots(a_rn, G_H, 1.0 / S, eps_rms)
            pass_by("bq", "bkv")
            act.wait_ge(stage_over, 1)
            gates("bg", s_gate, ACT.Silu)
            for g in range(2):
                softmax_exp(swa[g], lambda i, u, t: sinks[:, ds(8 * g + 2 * i + u, 1)])
            pass_by("cqk", "cv")
            act.wait_ge(stage_over, 2)
            gates("cg", m_gate, ACT.Silu)
            softmax_exp(moba)
            act.wait_ge(stage_over, 3)
            for b in range(3):
                act.activation(y1_hi[:, 8 * b:8 * b + 8, :], y1[:, 8 * b:8 * b + 8, :], ACT.Copy).then_inc(y_hi_ready, 1)
            sec = plan["merge"]
            with act.Fori(0, 4) as j:
                for b in range(3):
                    g, more = sec.first + b * MERGE + AHEAD, j * (3 * MERGE // RING)
                    for c in range(sec.chunks):
                        if c + AHEAD == sec.chunks - 1:
                            new = g - AHEAD + sec.chunks
                            act.wait_ge(lo_ready[new % RING], new // RING + more)
                            act.dma_start(ring[:, new % RING],
                                          I["w_branch"][b * BW:b * BW + CH * P, ds(j * TW, TW)].rearrange(row, p=P))                               .then_inc(w_landed[new % RING], 16)
                        split(g + c, more)
                    act.wait_ge(tile_done[0], sec.tiles[0] + 3 * j + b + 1)
                    act.wait_ge(tile_free[1], sec.tiles[1] + 3 * j + b)
                    for cb in range(4):
                        last = act.activation(sig[:, cb], ps[:, cb // 2, (cb % 2) * S:(cb % 2 + 1) * S], ACT.Sigmoid,
                                              bias=bmc[:, b, ds(4 * j + cb, 1)])
                        if cb == 3:
                            last.then_inc(tile_free[0], 1)
                    for c in range(sec.chunks, MERGE):
                        split(g + c, more)
            act.wait_ge(stage_over, 4)
            load_ln(I["ln_g"], I["ln_b"])
            pass_by("wo")
            ln_roots()

            def hidden_gate(name):
                sec = plan[name]
                for t, u, it in tiles_of(act, sec.n):
                    splits(sec, u, it)
                    if u == 0:
                        act.wait_ge(tile_done[0], sec.tiles[0] + it + 1)
                        act.wait_ge(tile_free[1], sec.tiles[1] + it)
                        act.activation(f_sg[:, 0].rearrange("p a s -> p (a s)"),
                                       ps[:, 0:2, :].rearrange("p a s -> p (a s)"), ACT.Silu).then_inc(tile_free[0], 1)

            take_x()
            pass_by("cval")
            gates("cgate", c_acc, ACT.Sigmoid)
            sec = plan["qkv"]
            with n.loop(act, sec.n // 2, {silu_done: 0, conv_ready: 0, vec_ready: 2}) as i:
                for u in range(2):
                    splits(sec, u, i)
                    act.wait_ge(vec_ready, n.next(vec_ready))
                    v = c_qkv[:, ds(4 * (2 * i + u), 4), :].rearrange("p a s -> p (a s)")
                    act.activation(v, v, ACT.Silu).then_inc(silu_done, 1)
            gates("z", c_z, ACT.Silu)
            pass_by("ba")
            act.wait_ge(vec_ready, n.next(vec_ready))
            act.activation(t_beta, t_ba[:, :, 0:8], ACT.Sigmoid)
            act.activation(t_A, gdnA, ACT.Exp)
            link(act.activation(t_e, t_e, ACT.Exp))
            act.activation(t_e, t_e, ACT.Ln, bias=one).then_inc(act_ready, 1)
            act.wait_ge(vec_ready, n.next(vec_ready))
            act.activation(c_sq, c_acc, ACT.Square).then_inc(conv_ready, 1)
            act.wait_ge(mm_ready, n.next(mm_ready, 13))
            act.activation(c_rs, ps[:, 5, 0:S], ACT.Sqrt, bias=eps_ln, scale=1.0 / 1024).then_inc(act_ready, 1)
            act.wait_ge(vec_ready, n.next(vec_ready))
            for t in range(8):
                last = act.activation(y2[:, t], c_acc[:, t], ACT.Silu, bias=colp[:, t, R_CLB:R_CLB + 1],
                                      scale=colp[:, t, R_CLG:R_CLG + 1])
            last.then_inc(act_ready, 1)
            act.wait_ge(act_ready, 12)
            act.activation(l2_sq, c_qkv[:, 0:16], ACT.Square).then_inc(sq_ready, 1)
            roots(l2_rn, 16, 1.0, eps_rms)
            for h in range(GD_H):
                act.wait_ge(vec_ready, n.next(vec_ready))
                act.activation(d_dt[:, h % 2], d_dt[:, h % 2], ACT.Exp).then_inc(act_ready, 1)
            with n.loop(act, 7, {xp_ready: 4}):
                for g in range(4):
                    act.wait_ge(xp_ready, n.next(xp_ready))
                    act.activation(d_xs[:, 4 * g:4 * g + 4].rearrange("p a b -> p (a b)"), ps[:, g, :],
                                   ACT.Copy).then_inc(xs_ready, 1)
            act.wait_ge(vec_ready, n.next(vec_ready))
            act.activation(d_sq, y2[:, 8:16], ACT.Square).then_inc(sq_ready, 1)
            roots(d_rn, GD_H, 1.0 / P, eps_rms)
            act.wait_ge(stage_over, 5)
            load_ln(I["ln1_g_2"], I["ln1_b_2"])
            pass_by("wout2")
            ln_roots()
            take_x()
            load_ln(I["ln2_g_2"], I["ln2_b_2"])
            hidden_gate("gu")
            act.wait_ge(tile_free[1], plan["gu"].tiles[1] + plan["gu"].n // 2)
            prime_hidden("down2")
            pass_by("down2", hidden=True)
            ln_roots()
            take_x()
            load_ln(I["ln1_g_3"], I["ln1_b_3"])
            for r, name in enumerate(("lam_q1_3", "lam_k1_3", "lam_q2_3", "lam_k2_3")):
                act.dma_start(lam_rows[:, r], I[name].to_broadcast([P, 64])).then_inc(lam_landed, 16)
            pass_by("qka", "va", "qi", "kwi")
            softmax_exp(dsa)
            act.wait_ge(stage_over, 6)
            for t, u, it in tiles_of(act, 3):
                splits(plan["qkm"], u, it)
                act.wait_ge(vec_ready, n.next(vec_ready))
                v = e_qk[:, 4 * t:4 * t + 4]
                act.activation(v, v, ACT.Silu).then_inc(silu_done, 1)
            pass_by("vm")
            gates("om", e_gate, ACT.Sigmoid, 384)
            pass_by("if")
            act.wait_ge(vec_ready, n.next(vec_ready))
            link(act.activation(t_ef, t_ef, ACT.Exp))
            act.activation(t_ef, t_ef, ACT.Ln, bias=one).then_inc(act_ready, 1)
            act.wait_ge(vec_ready, n.next(vec_ready))
            softmax_exp(mls, lambda i, u, t: t_na[:, t, ds(2 * i + u, 1)])
            act.wait_ge(vec_ready, n.next(vec_ready))
            act.activation(e_sq, y3[:, 6:12], ACT.Square).then_inc(sq_ready, 1)
            roots(e_rn, M_H, 1.0 / P, eps_ln)
            act.wait_ge(vec_ready, n.next(vec_ready))
            act.activation(lam[:, 2:4], lam[:, 0:2], ACT.Exp).then_inc(act_ready, 1)
            pass_by("qkc", "vc")
            softmax_exp(dif)
            act.wait_ge(vec_ready, n.next(vec_ready))
            act.activation(e_sq[:, 0:4], e_cut, ACT.Square, scale=SHRINK).then_inc(sq_ready, 1)
            roots(e_rn, D_H, 1.0 / P, eps_diff)
            pass_by("wout3")
            ln_roots()
            take_x()
            load_ln(I["ln2_g_3"], I["ln2_b_3"])
            sec = plan["up3"]
            for t, u, it in tiles_of(act, sec.n):
                splits(sec, u, it)
                act.wait_ge(tile_done[u], sec.tiles[u] + it + 1)
                v = f_sg[:, u].rearrange("p a s -> p (a s)")
                act.activation(v, ps[:, 2 * u:2 * u + 2, :].rearrange("p a s -> p (a s)"), ACT.Relu)\
                   .then_inc(tile_free[u], 1)
                act.wait_ge(tile_free[u], sec.tiles[u] + it + 1)
                act.activation(hid[:, ds(4 * t, 4), :].rearrange("p a s -> p (a s)"), v, ACT.Square)\
                   .then_inc(hid_ready, 1)
            act.wait_ge(hid_ready, sec.n)
            prime_hidden("down3")
            pass_by("down3", hidden=True)
            ln_roots()

        @block.vector
        def _(dve):
            n = Count(FREE)

            def link(ins):
                ins.then_inc(dve_order, 1)
                dve.wait_ge(dve_order, n.next(dve_order))

            def tt(o, a, b, op):
                return dve.tensor_tensor(o, a, b, op)

            def tsc(o, a, s1, op0, s2=None, op1=ALU.bypass):
                return dve.tensor_scalar(o, a, s1, s2, op0, op1)

            def stt(o, a, s, b, op0, op1, **kw):
                return dve.scalar_tensor_tensor(o, a, s, b, op0, op1, **kw)

            dve.sem_inc(logits_used, 1)
            dve.sem_inc(o_used, 1)
            dve.memset(table[:], 0.0).then_inc(table_zeroed, 1)
            dve.memset(eps_ln, LN_EPS)
            dve.memset(eps_rms, RMS_EPS)
            dve.memset(one, 1.0)
            dve.memset(eps_diff, LN_EPS * SHRINK ** 2)
            for h in range(A_H):
                dve.memset(slopes_a[:, h:h + 1], 2.0 ** (-8.0 * (h + 1) / A_H))
            for h in range(D_H):
                dve.memset(slopes_c[:, h:h + 1], 2.0 ** (-8.0 * (h + 1) / D_H))
            dve.memset(ones[:], 1.0)
            dve.memset(upper[:, P:S], 1.0)
            for m in (causal, causalT):
                dve.memset(m[:, P:S], 0.0)
            dve.wait_ge(iotas, 2)
            pi, pj, px, py = (v.bitcast(I32) for v in (posi, posj, posx, posy))
            tt(ident[:], pi, pj, ALU.is_equal)
            link(tt(upper[:, 0:P], pi, pj, ALU.is_ge))
            for dst, cmp in [(causal[:, 0:P], ALU.is_gt), (causal[:, S:384], ALU.is_gt), (causalT[:, 0:P], ALU.is_lt),
                             (causalT[:, S:384], ALU.is_lt), (band[:, 0:P], ALU.is_gt), (band[:, P:S], ALU.is_le),
                             (band[:, S:384], ALU.is_gt)]:
                link(tt(dst, pi, pj, cmp))
                dve.tensor_scalar(dst, dst, NEG, None, ALU.mult)
            for c in (0, 2):
                tt(ndist[:, c * P:(c + 1) * P], pi, pj, ALU.subtract)
            link(tt(ndist[:, P:S], pi, pj, ALU.subtract))
            link(tsc(ndist[:, P:S], ndist[:, P:S], -float(P), ALU.add))
            link(tt(px, pi, pj, ALU.bitwise_xor))
            for lv in range(7):
                link(tsc(py, px, lv, ALU.logical_shift_right))
                link(tsc(levels[:, lv], py, 1, ALU.is_equal))
                link(tt(levels[:, lv], levels[:, lv], upper[:, 0:P], ALU.mult))
            dve.wait_ge(x_landed, 16)
            dve.sem_inc(consts, 1)

            def x_ready_now():
                dve.sem_inc(x_ready, 1)

            x_ready_now()
            dve.wait_ge(tableT_ready, 1)
            link(dve.tensor_copy(colp[:].rearrange("p t r -> p (t r)"), ps[:, 0, :]))
            for b in range(3):
                last = dve.tensor_copy(bmc[:, b, :].rearrange("p (a t) -> p a t", a=2),
                                       colp[:, :, R_BM + 2 * b:R_BM + 2 * b + 2].rearrange("p t a -> p a t"))
            last.then_inc(table_ready, 1)

            def split(g, more=0, rows=None):
                s, width = g % RING, TW
                if isinstance(more, int):
                    g, more = g + more * RING, 0
                    if g >= len(widths):
                        return
                    width = widths[g]
                dve.wait_ge(hi_ready[s], g // RING + 1 + more)
                last = tt(w_lo[:, s, :, 0:width], ring[:, s, :, 0:width], w_hi[:, s, :, 0:width].bitcast(F32), ALU.subtract)
                if rows is not None:
                    last = tt(h_lo[:, s], hid[:, rows:rows + CH, :], h_hi[:, s].bitcast(F32), ALU.subtract)
                last.then_inc(lo_ready[s], 1)

            def splits(sec, u, it, hidden=False):
                for c in range(AHEAD, AHEAD + sec.chunks):
                    split(sec.chunk(u, c), sec.more(it), c % sec.chunks * CH if hidden else None)

            def pass_by(*names):
                for name in names:
                    for t, u, it in tiles_of(dve, plan[name].n):
                        splits(plan[name], u, it)

            def prime_hidden(name, times):
                for c in range(AHEAD):
                    s = plan[name].chunk(0, c) % RING
                    dve.wait_ge(h_primed_hi, AHEAD * times + c + 1)
                    tt(h_lo[:, s], hid[:, c * CH:(c + 1) * CH, :], h_hi[:, s].bitcast(F32), ALU.subtract)\
                        .then_inc(h_primed, 1)

            def take_x():
                for g in range(KT // 2):
                    dve.wait_ge(xh_ready, n.next(xh_ready))
                    lo, hi = (v[:, 2 * g:2 * g + 2, :].rearrange("p a s -> p (a s)") for v in (x_lo, x_hi))
                    tt(lo, ps[:, 4 + g % 4, :], hi.bitcast(F32), ALU.subtract).then_inc(xTp_used, 1)

            def split_y(y):
                link(dve.tensor_copy(y_hi[:], y))
                link(tt(y_lo[:], y, y_hi[:].bitcast(F32), ALU.subtract))

            def take(name, dst, kind, width=TW):
                sec = plan[name]
                for t, u, it in tiles_of(dve, sec.n):
                    splits(sec, u, it)
                    dve.wait_ge(tile_done[u], sec.tiles[u] + it + 1)
                    if kind == "F":
                        per = width // P
                        dve.tensor_copy(dst[:, ds(t * per, per), :].rearrange("p a s -> p (a s)"),
                                        ps[:, 2 * u:2 * u + 2, :].rearrange("p a s -> p (a s)")[:, 0:per * S])\
                           .then_inc(tile_free[u], 1)
                    else:
                        dve.tensor_copy(dst[:, :, ds(t * width, width)], ps[:, 2 * u:2 * u + 2, 0:width])\
                           .then_inc(tile_free[u], 1)

            def wait_gates(name):
                sec = plan[name]
                for u in range(2):
                    dve.wait_ge(tile_free[u], sec.tiles[u] + (sec.n + 1 - u) // 2)

            def over():
                dve.sem_inc(stage_over, 1)

            def attention(A, scale, mask, y, gate=None, toff=0, sink=None, slopes=None):
                kind = A.kind
                per = {logits_ready: 2, logits_used: 2, exp_done: 2, o_ready: 1,
                       dve_order: {"swa": 8, "moba": 2, "dsa": 4, "mlstm": 10, "diff": 5}[kind]}
                with n.loop(dve, A.pairs, per) as i:
                    for u in range(2):
                        m, sm = nmax[:, 2 * u:2 * u + 2], A.sm[:, u]
                        if kind == "mlstm":
                            for c0, w in ((0, P), (P, S)):
                                last = tt(sm[:, c0:c0 + w],
                                          e_bbc[:, ds(2 * i + u, 1), 0:w].rearrange("p a s -> p (a s)"),
                                          causal[:, c0:c0 + w], ALU.add)
                            link(last)
                        else:
                            if slopes is not None:
                                link(stt(sm, ndist[:], slopes[:, ds(A.outs * i + (u if A.outs == 2 else 0), 1)], mask,
                                         ALU.mult, ALU.add))
                            dve.wait_ge(logits_ready, n.next(logits_ready))
                            stt(sm, ps[:, 4 + u, 0:384], scale, mask if slopes is None else sm, ALU.mult, ALU.add)\
                                .then_inc(logits_used, 1)
                            dve.wait_ge(logits_used, n.next(logits_used))
                        dve.tensor_reduce(m[:, 0:1], sm[:, 0:P], AX, ALU.max, negate=True)
                        last = dve.tensor_reduce(m[:, 1:2], sm[:, P:384], AX, ALU.max, negate=True)
                        if kind == "mlstm":
                            link(last)
                            tsc(m, m, 0.0, ALU.min).then_inc(max_ready, 1)
                        elif kind == "swa":
                            link(last)
                            link(tsc(esink[:, 2 * u:2 * u + 1], sinks[:, ds(8 * sink + 2 * i + u, 1)], -1.0, ALU.mult))
                            tsc(m, m, esink[:, 2 * u:2 * u + 1], ALU.min).then_inc(max_ready, 1)
                        else:
                            last.then_inc(max_ready, 1)
                    if kind == "diff":
                        p0, p1 = A.p[:, 0], A.p[:, 1]
                        dve.wait_ge(exp_done, n.next(exp_done, 2))
                        link(dve.reciprocal(rinv, rsum))
                        link(tsc(rinv[:, 2:4], rinv[:, 2:4], lam[:, 4:5], ALU.mult))
                        tsc(p0[:, 0:P], p0[:, 0:P], rinv[:, 0:1], ALU.mult)
                        link(tsc(p0[:, P:384], p0[:, P:384], rinv[:, 1:2], ALU.mult))
                        stt(p0[:, 0:P], p1[:, 0:P], rinv[:, 2:3], p0[:, 0:P], ALU.mult, ALU.add)
                        stt(p0[:, P:384], p1[:, P:384], rinv[:, 3:4], p0[:, P:384], ALU.mult, ALU.add)\
                            .then_inc(probs_ready, 1)
                    for u in range(2 if kind != "diff" else 0):
                        l, p = rsum[:, 2 * u:2 * u + 2], A.p[:, u]
                        dve.wait_ge(exp_done, n.next(exp_done))
                        if kind == "swa":
                            link(tt(l, l, esink[:, 2 * u:2 * u + 2], ALU.add))
                        if kind == "mlstm":
                            dve.wait_ge(logits_ready, n.next(logits_ready))
                            stt(p[:, 0:P], ps[:, 4 + u, 0:P], scale, p[:, 0:P], ALU.mult, ALU.mult, accum_out=l[:, 0:1])
                            stt(p[:, P:384], ps[:, 4 + u, P:384], scale, p[:, P:384], ALU.mult, ALU.mult,
                                accum_out=l[:, 1:2]).then_inc(logits_used, 1)
                            dve.wait_ge(logits_used, n.next(logits_used))
                            link(stt(l, l, -1.0, l, ALU.mult, ALU.max))
                            link(tt(l, l, esink[:, 2 * u:2 * u + 2], ALU.max))
                        link(dve.reciprocal(rinv[:, 2 * u:2 * u + 2], l))
                        tsc(p[:, 0:P], p[:, 0:P], rinv[:, 2 * u:2 * u + 1], ALU.mult)
                        tsc(p[:, P:384], p[:, P:384], rinv[:, 2 * u + 1:2 * u + 2], ALU.mult).then_inc(probs_ready, 1)
                    dve.wait_ge(o_ready, n.next(o_ready))
                    one_tile = lambda v: v[:, ds(toff + i, 1), :].rearrange("p a s -> p (a s)")
                    if kind == "swa":
                        last = tt(one_tile(y), ps[:, 2, 0:S], one_tile(gate), ALU.mult)
                    elif kind == "diff":
                        last = dve.tensor_copy(one_tile(y), ps[:, 2, 0:S])
                    elif gate is None:
                        last = dve.tensor_copy(y[:, ds(2 * i, 2), :], ps[:, 2:4, 0:S])
                    else:
                        last = tt(y[:, ds(2 * i, 2), :], ps[:, 2:4, 0:S], gate[:, ds(2 * i, 2), :], ALU.mult)
                    last.then_inc(o_used, 1)
                dve.wait_ge(o_used, n.next(o_used, A.pairs))

            def inverse_roots(dst, heads):
                dve.wait_ge(root_ready, n.next(root_ready, heads // 2))
                link(dve.reciprocal(dst, dst))

            def layer_norm(name, hidden=False):
                sec = plan[name]
                for t, u, it in tiles_of(dve, sec.n, sec.last):
                    splits(sec, u, it, hidden)
                    dve.wait_ge(tile_done[u], sec.tiles[u] + it + 1)
                    xv = xtok[:, :, ds(t * TW, TW)]
                    stt(xv, xv, ALPHA, ps[:, 2 * u:2 * u + 2, :], ALU.mult, ALU.add).then_inc(tile_free[u], 1)
                for u in range(2):
                    dve.wait_ge(tile_free[u], sec.tiles[u] + sec.n // 2)
                for t in range(2):
                    for c in range(4):
                        last = dve.bn_stats(stat[:, 32 + 6 * c:38 + 6 * c] if t == 0 else tokc[:, 6 * c:6 * c + 6],
                                            xtok[:, t, c * TW:(c + 1) * TW])
                link(last)
                link(dve.bn_aggr(stat[:, 2:4], stat[:, 32:56]))
                link(dve.bn_aggr(stat[:, 4:6], tokc[:, 0:24]))
                for t in range(2):
                    link(dve.tensor_copy(stat[:, 26 + t:27 + t], stat[:, 3 + 2 * t:4 + 2 * t]))
                dve.sem_inc(var_ready, 1)
                dve.wait_ge(std_ready, n.next(std_ready))
                link(dve.reciprocal(stat[:, 28:30], stat[:, 28:30]))
                dve.wait_ge(ln_landed, n.next(ln_landed, 32))
                for t in range(2):
                    link(tsc(xtok[:, t], xtok[:, t], stat[:, 2 + 2 * t:3 + 2 * t], ALU.subtract,
                             stat[:, 28 + t:29 + t], ALU.mult))
                    link(tt(xtok[:, t], xtok[:, t], ln_gb[:, 0], ALU.mult))
                    link(tt(xtok[:, t], xtok[:, t], ln_gb[:, 1], ALU.add))

            for g in range(AHEAD):
                split(g)
            take_x()
            take("aqk", a_qk, "F")
            take("av", a_v, "T")
            pass_by("alr")
            dve.wait_ge(tile_done[0], plan["alr"].tiles[0] + 1)
            link(dve.tensor_copy(alrT, ps[0:G_RANK, 0, 0:S]))
            dve.sem_inc(tile_free[0], 1)
            dve.sem_inc(vec_ready, 1)
            pass_by("ag")
            dve.wait_ge(mm_ready, n.next(mm_ready))
            for h in range(G_H):
                tsc(a_b[:, h], ps[:, 4 + h // 2, (h % 2) * S:(h % 2 + 1) * S], colp[:, h, R_GLAB:R_GLAB + 1], ALU.add)\
                    .then_inc(dve_order, 1)
            dve.wait_ge(dve_order, n.next(dve_order, G_H))
            stt(a_e[:, 0], a_b, -1.0, a_b, ALU.mult, ALU.min).then_inc(vec_ready, 1)
            link(tsc(a_b, a_b, 0.0, ALU.min))
            dve.wait_ge(act_ready, n.next(act_ready))
            link(tt(a_b, a_b, a_e[:, 0], ALU.subtract))
            link(tsc(a_e[:, 1], a_b, 1.0 / G_TAU, ALU.mult))
            for h in range(G_H):
                last = dve.tensor_tensor_scan(a_b[:, h], ones[:, 0:1].to_broadcast([P, S]), a_e[:, 1, h], 0.0, ALU.mult, ALU.add)
            link(last)
            link(dve.memset(a_at, 0.0))
            QS = float(P) ** -0.5
            q4, k4 = a_qk[:, 0:4], a_qk[:, 4:8]

            def level_factors(lv):
                half = 1 << lv
                bv = a_b.rearrange("p h (c w) -> p (h c) w", w=2 * half)
                mid = bv[:, :, half - 1:half].to_broadcast([P, 4 * S // (2 * half), 2 * half])
                e = a_e[:, lv % 2]
                link(tt(e.rearrange("p h (c w) -> p (h c) w", w=2 * half), bv, mid, ALU.subtract))
                stt(e, e, -1.0, e, ALU.mult, ALU.min).then_inc(vec_ready, 1)

            def merge_level(lv):
                dve.wait_ge(mm_ready, n.next(mm_ready))
                b = 4 + 2 * (lv % 2)
                if lv == 7:
                    dve.tensor_copy(a_at[:, :, P:S], ps[:, b, :].rearrange("p (h s) -> p h s", h=4)).then_inc(mm_used, 1)
                    return
                m = ident[:] if lv == 8 else levels[:, lv]
                b = 4 if lv == 8 else b
                for g in range(2):
                    for c in range(2):
                        o = a_at[:, 2 * g:2 * g + 2, c * S:c * S + P]
                        d = ps[:, b + g, :].rearrange("p (h s) -> p h s", h=2)[:, :, c * P:(c + 1) * P]
                        mk = m.unsqueeze(1).to_broadcast([P, 2, P]).bitcast(I32)
                        last = dve.copy_predicated(o, mk, d)
                last.then_inc(mm_used, 1)

            level_factors(0)
            for lv in range(8):
                if lv < 7:
                    level_factors(lv + 1)
                dve.wait_ge(act_ready, n.next(act_ready))
                if lv >= 2:
                    pass
                stt(a_qe[:, lv % 2], q4, QS, a_e[:, lv % 2], ALU.mult, ALU.mult)
                link(tt(a_ke[:, lv % 2], k4, a_e[:, lv % 2], ALU.mult))
                dve.sem_inc(fac_ready, 1)
                if lv >= 1:
                    merge_level(lv - 1)
            merge_level(7)
            link(tsc(a_qe[:, 0], q4, QS, ALU.mult))
            dve.sem_inc(fac_ready, 1)
            merge_level(8)
            dve.wait_ge(mm_ready, n.next(mm_ready))
            link(dve.tensor_copy(y1[:, 0:8, :].rearrange("p a s -> p (a s)"), ps[:, 4:8, :].rearrange("p a s -> p (a s)")))
            dve.sem_inc(vec_ready, 1)
            wait_gates("ag")
            dve.wait_ge(sq_ready, n.next(sq_ready))
            for e in range(2):
                ya = y1[:, 0:8].rearrange("p (h e) s -> p h e s", e=2)[:, :, e, :]
                ga = a_gate.rearrange("p (h e) s -> p h e s", e=2)[:, :, e, :]
                stt(ya, ya, colp[:, e, R_GLAG:R_GLAG + 1], ga, ALU.mult, ALU.mult).then_inc(dve_order, 1)
            dve.wait_ge(dve_order, n.next(dve_order, 2))
            inverse_roots(a_rn, G_H)
            for e in range(2):
                ya = y1[:, 0:8].rearrange("p (h e) s -> p h e s", e=2)[:, :, e, :]
                last = tt(ya, ya, a_rn, ALU.mult)
            link(last)
            over()
            take("bq", s_q, "F")
            pass_by("bkv")
            dve.wait_ge(tile_done[0], plan["bkv"].tiles[0] + 1)
            dve.tensor_copy(s_kd[:].rearrange("p a s -> p (a s)"), ps[:, 0, :])
            dve.tensor_copy(s_v[:].rearrange("p a s -> p (a s)"), ps[:, 1, 0:S]).then_inc(tile_free[0], 1)
            pass_by("bg")
            wait_gates("bg")
            dve.sem_inc(gate_ready, 1)
            for g in range(2):
                attention(swa[g], 64.0 ** -0.5, band[:], y1[:, 8:16], s_gate, 4 * g, sink=g)
            over()
            take("cqk", m_qk, "F")
            take("cv", m_v, "T")
            pass_by("cg")
            wait_gates("cg")
            dve.sem_inc(gate_ready, 1)
            attention(moba, float(P) ** -0.5, causal[:], y1[:, 16:24], m_gate, 0)
            over()
            for b in range(3):
                dve.wait_ge(y_hi_ready, b + 1)
                y = y1[:, 8 * b:8 * b + 8, :]
                tt(y1_lo[:, 8 * b:8 * b + 8, :], y, y1_hi[:, 8 * b:8 * b + 8, :].bitcast(F32), ALU.subtract)\
                    .then_inc(y_split, 1)
            sec = plan["merge"]
            with n.loop(dve, 4, {dve_order: 4}) as j:
                for b in range(3):
                    for c in range(MERGE):
                        split(sec.first + b * MERGE + c + AHEAD, j * (3 * MERGE // RING))
                    dve.wait_ge(tile_done[1], sec.tiles[1] + 3 * j + b + 1)
                    dve.wait_ge(tile_free[0], sec.tiles[0] + 3 * j + b + 1)
                    up = ps[:, 2:4, :].rearrange("p a s -> p (a s)")
                    sg = sig.rearrange("p a s -> p (a s)")
                    mt = mtmp.rearrange("p a s -> p (a s)")
                    md = mergedT[:, ds(4 * j, 4), :].rearrange("p a s -> p (a s)")
                    tt(md if b == 0 else mt, sg, up, ALU.mult).then_inc(tile_free[1], 1)
                    dve.wait_ge(tile_free[1], sec.tiles[1] + 3 * j + b + 1)
                    if b:
                        link(tt(md, md, mt, ALU.add))
                hi, lo = (v[:, ds(4 * j, 4), :].rearrange("p a s -> p (a s)") for v in (m_hi, m_lo))
                link(dve.tensor_copy(hi, md))
                link(tt(lo, md, hi.bitcast(F32), ALU.subtract))
            over()
            layer_norm("wo")
            dve.sem_inc(x_ready, 1)

            def hidden_up(name):
                sec = plan[name]
                for t, u, it in tiles_of(dve, sec.n):
                    splits(sec, u, it)
                    if u == 1:
                        dve.wait_ge(tile_done[1], sec.tiles[1] + it + 1)
                        dve.wait_ge(tile_free[0], sec.tiles[0] + it + 1)
                        tt(hid[:, ds(4 * it, 4), :].rearrange("p a s -> p (a s)"), f_sg[:, 0].rearrange("p a s -> p (a s)"),
                           ps[:, 2:4, :].rearrange("p a s -> p (a s)"), ALU.mult).then_inc(tile_free[1], 1)

            take_x()
            for k in range(SHORT_W):
                link(dve.tensor_copy(scw[:, k, :].rearrange("p (a t) -> p a t", a=3),
                                     colp[:, :, R_SCW + 3 * k:R_SCW + 3 * k + 3].rearrange("p t a -> p a t")))
            dve.memset(c_h[:, :, 0:HP], 0.0)
            dve.memset(c_raw[:, :, :, 0:RP], 0.0)
            sec = plan["cval"]
            for t, u, it in tiles_of(dve, sec.n):
                splits(sec, u, it)
                dve.wait_ge(tile_done[u], sec.tiles[u] + it + 1)
                dve.tensor_copy(c_h[:, 4 * t:4 * t + 4, HP:HP + S],
                                ps[:, 2 * u:2 * u + 2, :].rearrange("p a (c s) -> p (a c) s", c=2))\
                   .then_inc(tile_free[u], 1)
            pass_by("cgate")
            wait_gates("cgate")
            link(tt(c_h[:, :, HP:HP + S], c_h[:, :, HP:HP + S], c_acc, ALU.mult))

            def wide_conv(t, taps=range(CONV_W)):
                acc = c_acc[:, ds(t, 1), :].rearrange("p a s -> p (a s)")
                win = lambda k: c_h[:, ds(t, 1), k:k + S].rearrange("p a s -> p (a s)")
                tap = lambda r: colp[:, ds(t, 1), r:r + 1].rearrange("p a s -> p (a s)")
                for k in taps:
                    if k == 0:
                        link(tsc(acc, win(0), tap(R_DWW), ALU.mult, tap(R_DWB), ALU.add))
                    else:
                        link(stt(acc, win(k), tap(R_DWW + k), acc, ALU.mult, ALU.add))

            sec = plan["qkv"]
            with n.loop(dve, sec.n // 2, {dve_order: 2 * (CONV_W + 3)}) as i:
                for u in range(2):
                    t = 2 * i + u
                    for c in range(sec.chunks):
                        split(sec.chunk(u, c + AHEAD), sec.more(i))
                        wide_conv(t, range(c * CONV_W // sec.chunks, (c + 1) * CONV_W // sec.chunks))
                    dve.wait_ge(tile_done[u], sec.tiles[u] + i + 1)
                    dve.tensor_copy(c_raw[:, u, :, RP:RP + S],
                                    ps[:, 2 * u:2 * u + 2, :].rearrange("p a (c s) -> p (a c) s", c=2))\
                       .then_inc(tile_free[u], 1)
                    dve.wait_ge(tile_free[u], sec.tiles[u] + i + 1)
                    for k in range(SHORT_W):
                        for c in range(4):
                            o = c_qkv[:, ds(4 * t + c, 1), :].rearrange("p a s -> p (a s)")
                            r = c_raw[:, u, c, k:k + S]
                            wk = scw[:, k, ds(4 * t + c, 1)]
                            last = tsc(o, r, wk, ALU.mult) if k == 0 else stt(o, r, wk, o, ALU.mult, ALU.add)
                        if k < SHORT_W - 1:
                            link(last)
                        else:
                            last.then_inc(vec_ready, 1)
            sec = plan["z"]
            for u in range(2):
                for c in range(sec.chunks):
                    split(sec.chunk(u, c + AHEAD))
                    wide_conv(6 + u, range(c * CONV_W // sec.chunks, (c + 1) * CONV_W // sec.chunks))
            dve.sem_inc(conv_ready, 1)
            pass_by("ba")
            dve.wait_ge(tile_done[0], plan["ba"].tiles[0] + 1)
            dve.tensor_copy(t_ba.rearrange("p t c -> p (t c)"), ps[:, 0, 0:32]).then_inc(tile_free[0], 1)
            dve.wait_ge(tile_free[0], plan["ba"].tiles[0] + 1)
            link(tt(t_x, t_ba[:, :, 8:16], gdndt.unsqueeze(1).to_broadcast([P, 2, 8]), ALU.add))
            stt(t_e, t_x, -1.0, t_x, ALU.mult, ALU.min).then_inc(vec_ready, 1)
            dve.wait_ge(mm_ready, n.next(mm_ready))
            link(tsc(c_mu, ps[:, 4, 0:S], 1.0 / 1024, ALU.mult))
            tt(c_acc, c_acc, c_mu.unsqueeze(1).to_broadcast([P, 8, S]), ALU.subtract).then_inc(vec_ready, 1)
            dve.wait_ge(act_ready, n.next(act_ready))
            link(stt(t_x, t_x, 0.0, t_e, ALU.max, ALU.add))
            link(stt(t_g, t_x, -1.0, t_A.unsqueeze(1).to_broadcast([P, 2, 8]), ALU.mult, ALU.mult))
            dve.wait_ge(act_ready, n.next(act_ready))
            link(dve.reciprocal(c_rs, c_rs))
            dve.wait_ge(mm_ready, n.next(mm_ready))
            tt(c_acc, c_acc, c_rs.unsqueeze(1).to_broadcast([P, 8, S]), ALU.mult).then_inc(vec_ready, 1)
            dve.wait_ge(act_ready, n.next(act_ready))
            dve.wait_ge(root_ready, n.next(root_ready, 8))
            link(dve.reciprocal(l2_rn, l2_rn))
            stt(c_qkv[:, 0:8], c_qkv[:, 0:8], float(P) ** -0.5, l2_rn[:, 0:8], ALU.mult, ALU.mult)
            link(tt(c_qkv[:, 8:16], c_qkv[:, 8:16], l2_rn[:, 8:16], ALU.mult))
            dve.sem_inc(fac_ready, 1)
            dve.wait_ge(mm_ready, n.next(mm_ready))
            dve.tensor_copy(t_gc.rearrange("p t c -> p (t c)"), ps[:, 0, 0:16])
            for t in range(2):
                last = tt(d_vb[:, t].rearrange("p (h c) -> p h c", h=8),
                          ps[:, 4 + 2 * t:6 + 2 * t, :].rearrange("p a (h c) -> p (a h) c", h=4),
                          t_beta[:, t].unsqueeze(2).to_broadcast([P, 8, P]), ALU.mult)
            link(last)
            dve.sem_inc(fac_ready, 1)
            for h in range(GD_H):
                b, dt, db = 2 + 3 * (h % 2), d_dt[:, h % 2], d_db[:, h % 2]
                dve.wait_ge(mm_ready, n.next(mm_ready))
                stt(dt[:, 0:S], ps[:, b, 0:S], t_gc[:, 0, h:h + 1], causalT[:, 0:S], ALU.subtract, ALU.add)
                stt(dt[:, S:384], ps[:, b, P:S], t_gc[:, 1, h:h + 1], causalT[:, S:384], ALU.subtract, ALU.add)\
                    .then_inc(vec_ready, 1)
                dve.wait_ge(act_ready, n.next(act_ready))
                tt(d_at[:, h], ps[:, b + 2, 0:384], dt, ALU.mult)
                tt(db[:, 0:S], dt[:, 0:S], ps[:, b, S:512], ALU.mult)
                link(tt(db[:, S:384], dt[:, S:384], ps[:, b, S + P:512], ALU.mult))
                tt(d_lt[:, 2 * h:2 * h + 2], ps[:, b + 1, 0:384].rearrange("p (a c) -> p a c", a=3)[:, 0:3:2],
                   db.rearrange("p (a c) -> p a c", a=3)[:, 0:3:2], ALU.mult)
                tt(d_l21[:, h], ps[:, b + 1, P:S], db[:, P:S], ALU.mult).then_inc(fac_ready, 1)
                dve.wait_ge(fac_ready, n.next(fac_ready, 12 if h == 0 else 1))
            for g in range(4):
                for m in (d_t, d_tt):
                    last = dve.tensor_copy(m[:, 4 * g:4 * g + 4], ident[:].unsqueeze(1).to_broadcast([P, 4, P]))
                last.then_inc(inv_ready, 1)
            dve.wait_ge(inv_ready, n.next(inv_ready, 4))
            with n.loop(dve, 7, {yp_ready: 4, inv_ready: 4}) as lv:
                for g in range(4):
                    mk = levels[:, ds(lv, 1), :].to_broadcast([P, 4, P])
                    tt(d_lm[:, 4 * g:4 * g + 4], d_lt[:, 4 * g:4 * g + 4], mk, ALU.mult).then_inc(lm_ready, 1)
                for g in range(4):
                    dve.wait_ge(yp_ready, n.next(yp_ready))
                    for m, b in ((d_t, 4), (d_tt, 6)):
                        v = m[:, 4 * g:4 * g + 4].rearrange("p a b -> p (a b)")
                        last = tt(v, v, ps[:, b + g % 2, :], ALU.subtract)
                    last.then_inc(inv_ready, 1)
                    dve.wait_ge(inv_ready, n.next(inv_ready))
            flat = lambda b: ps[:, b:b + 2, :].rearrange("p a s -> p (a s)")
            dve.wait_ge(mm_ready, n.next(mm_ready))
            dve.tensor_copy(d_vn[:, 0], flat(0)).then_inc(fac_ready, 1)
            dve.wait_ge(mm_ready, n.next(mm_ready))
            tt(d_vb[:, 1], d_vb[:, 1], flat(2), ALU.subtract).then_inc(fac_ready, 1)
            dve.wait_ge(mm_ready, n.next(mm_ready))
            dve.tensor_copy(d_vn[:, 1], flat(0)).then_inc(fac_ready, 1)
            dve.wait_ge(mm_ready, n.next(mm_ready))
            dve.tensor_copy(y2[:, 8:16].rearrange("p a s -> p (a s)"), ps[:, 4:8, :].rearrange("p a s -> p (a s)"))\
               .then_inc(vec_ready, 1)
            wait_gates("z")
            dve.wait_ge(sq_ready, 3)
            link(stt(y2[:, 8:16], y2[:, 8:16], colp[:, T_GDNW, R_GLAG:R_GLAG + 1], c_z, ALU.mult, ALU.mult))
            inverse_roots(d_rn, GD_H)
            link(tt(y2[:, 8:16], y2[:, 8:16], d_rn, ALU.mult))
            split_y(y2)
            over()
            layer_norm("wout2")
            dve.sem_inc(x_ready, 1)
            take_x()
            hidden_up("gu")
            prime_hidden("down2", 0)
            layer_norm("down2", hidden=True)
            dve.sem_inc(x_ready, 1)
            take_x()
            for k in range(SHORT_W):
                last = dve.tensor_copy(mcw[:, k, :].rearrange("p (a t) -> p a t", a=2),
                                       colp[:, 0:6, R_CM + 2 * k:R_CM + 2 * k + 2].rearrange("p t a -> p a t"))
            link(last)
            take("qka", e_qk, "F")
            take("va", e_v, "T", 384)
            take("qi", i_q, "F")
            pass_by("kwi")
            sec = plan["kwi"]
            dve.wait_ge(tile_done[0], sec.tiles[0] + 1)
            dve.tensor_copy(i_k, ps[:, 0, 0:S])
            dve.tensor_copy(t_w.rearrange("p t c -> p (t c)"), ps[:, 0, S:S + 16]).then_inc(tile_free[0], 1)
            dve.wait_ge(tile_free[0], sec.tiles[0] + 1)
            dve.sem_inc(fac_ready, 1)
            dve.sem_inc(gate_ready, 1)
            for h in range(8):
                dve.wait_ge(mm_ready, n.next(mm_ready))
                o = i_work if h == 0 else i_tmp
                tsc(o[:, 0:P], ps[:, 4 + h % 4, 0:P], 0.0, ALU.max, t_w[:, 0, h:h + 1], ALU.mult)
                tsc(o[:, P:384], ps[:, 4 + h % 4, P:384], 0.0, ALU.max, t_w[:, 1, h:h + 1], ALU.mult)\
                    .then_inc(mm_used, 1)
                dve.wait_ge(mm_used, n.next(mm_used, 10 if h == 0 else 1))
                if h:
                    link(tt(i_work, i_work, i_tmp, ALU.add))
            link(tt(i_work, i_work, causal[:], ALU.add))
            for _ in range(TOPK // 8):
                dve.max(top8[:, 0], i_work[:, 0:P])
                link(dve.max(top8[:, 1], i_work[:, P:384]))
                dve.match_replace(i_work[:, 0:P], top8[:, 0], i_work[:, 0:P], TAKEN)
                link(dve.match_replace(i_work[:, P:384], top8[:, 1], i_work[:, P:384], TAKEN))
            link(tsc(i_sel, i_work, TAKEN / 2, ALU.is_gt, NEG, ALU.mult))
            link(tt(i_sel, i_sel, causal[:], ALU.add))
            attention(dsa, float(P) ** -0.5, i_sel, y3[:, 0:6], slopes=slopes_a)
            over()
            dve.memset(e_raw[:, :, :, 0:RP], 0.0)
            sec = plan["qkm"]
            for t, u, it in tiles_of(dve, 3):
                splits(sec, u, it)
                dve.wait_ge(tile_done[u], sec.tiles[u] + t // 2 + 1)
                dve.tensor_copy(e_raw[:, u, :, RP:RP + S],
                                ps[:, 2 * u:2 * u + 2, :].rearrange("p a (c s) -> p (a c) s", c=2))\
                   .then_inc(tile_free[u], 1)
                dve.wait_ge(tile_free[u], sec.tiles[u] + t // 2 + 1)
                for k in range(SHORT_W):
                    for c in range(4):
                        o, r, wk = e_qk[:, 4 * t + c], e_raw[:, u, c, k:k + S], mcw[:, k, 4 * t + c:4 * t + c + 1]
                        last = tsc(o, r, wk, ALU.mult) if k == 0 else stt(o, r, wk, o, ALU.mult, ALU.add)
                    if k < SHORT_W - 1:
                        link(last)
                    else:
                        last.then_inc(vec_ready, 1)
            take("vm", e_v, "T", 384)
            pass_by("om", "if")
            sec = plan["if"]
            dve.wait_ge(tile_done[0], sec.tiles[0] + 1)
            dve.tensor_copy(t_if.rearrange("p t c -> p (t c)"), ps[:, 0, 0:24]).then_inc(tile_free[0], 1)
            dve.wait_ge(tile_free[0], sec.tiles[0] + 1)
            tt(t_if[:, :, 0:6], t_if[:, :, 0:6], bib.unsqueeze(1).to_broadcast([P, 2, 6]), ALU.add)
            link(tt(t_lf, t_if[:, :, 6:12], bfb.unsqueeze(1).to_broadcast([P, 2, 6]), ALU.add))
            stt(t_ef, t_lf, -1.0, t_lf, ALU.mult, ALU.min).then_inc(vec_ready, 1)
            dve.wait_ge(act_ready, 21)
            link(stt(t_lf, t_lf, 0.0, t_ef, ALU.min, ALU.subtract))
            link(tsc(t_ef, t_lf, -1.0, ALU.mult))
            dve.sem_inc(fac_ready, 1)
            dve.wait_ge(mm_ready, n.next(mm_ready))
            tsc(t_na.rearrange("p t c -> p (t c)"), ps[:, 0, 0:12], -1.0, ALU.mult).then_inc(vec_ready, 1)
            dve.wait_ge(mm_ready, n.next(mm_ready))
            dve.tensor_copy(e_bbc.rearrange("p a s -> p (a s)"),
                            ps[:, 4:7, :].rearrange("p a s -> p (a s)")).then_inc(mm_used, 1)
            dve.wait_ge(mm_used, n.next(mm_used))
            dve.wait_ge(silu_done, 9)
            dve.sem_inc(gate_ready, 1)
            attention(mls, float(P) ** -0.5, None, y3[:, 6:12])
            dve.sem_inc(vec_ready, 1)
            wait_gates("om")
            dve.wait_ge(sq_ready, 4)
            for h in range(M_H):
                last = stt(y3[:, 6 + h], y3[:, 6 + h], colp[:, h, R_MNG:R_MNG + 1], e_gate[:, h], ALU.mult, ALU.mult)
            link(last)
            inverse_roots(e_rn, M_H)
            link(tt(y3[:, 6:12], y3[:, 6:12], e_rn, ALU.mult))
            over()
            dve.wait_ge(lam_landed, 64)
            tt(lam_prod[:, 0], lam_rows[:, 0], lam_rows[:, 1], ALU.mult)
            link(tt(lam_prod[:, 1], lam_rows[:, 2], lam_rows[:, 3], ALU.mult))
            dve.tensor_reduce(lam[:, 0:2], lam_prod, AX, ALU.add).then_inc(vec_ready, 1)
            take("qkc", e_qk, "F")
            take("vc", e_v[:, :, 0:512], "T")
            LAM0 = 0.8 - 0.6 * math.exp(0.0)
            dve.wait_ge(act_ready, 22)
            link(tt(lam[:, 4:5], lam[:, 3:4], lam[:, 2:3], ALU.subtract))
            link(tsc(lam[:, 4:5], lam[:, 4:5], -LAM0, ALU.add))
            dve.sem_inc(gate_ready, 1)
            attention(dif, 64.0 ** -0.5, causal[:], y3[:, 12:16], slopes=slopes_c)
            tsc(e_cut, y3[:, 12:16], LARGE, ALU.min, -LARGE, ALU.max).then_inc(vec_ready, 1)
            dve.wait_ge(root_ready, n.next(root_ready, D_H // 2))
            rn = e_rn[:, 0:4]
            link(tsc(e_fits, rn, ROOT_MAX, ALU.is_lt, SHRINK, ALU.mult))
            link(dve.reciprocal(rn, rn))
            link(tt(rn, rn, e_fits, ALU.mult))
            link(tt(y3[:, 12:16], y3[:, 12:16], rn, ALU.mult))
            for h in range(D_H):
                last = tsc(y3[:, 12 + h], y3[:, 12 + h], colp[:, h, R_CNG:R_CNG + 1], ALU.mult, 1.0 - LAM0, ALU.mult)
            link(last)
            split_y(y3)
            over()
            layer_norm("wout3")
            dve.sem_inc(x_ready, 1)
            take_x()
            pass_by("up3")
            prime_hidden("down3", 1)
            layer_norm("down3", hidden=True)
            dve.sem_inc(x_ready, 1)


_INS = [
    "x", "w_in", "gla_w_up", "gla_b", "gla_norm_g", "swa_sinks", "b_merge", "w_branch", "w_o", "ln_g", "ln_b", "w_in_2",
    "conv_dw_w_2", "conv_dw_b_2", "conv_ln_g_2", "conv_ln_b_2", "gdn_conv_w_2", "gdn_A_log_2",
    "gdn_dt_bias_2", "gdn_norm_w_2", "w_out_2", "ln1_g_2", "ln1_b_2", "w_gate_up_2", "w_down_2", "ln2_g_2",
    "ln2_b_2", "w_in_3", "conv_m_3", "b_i_3", "b_f_3", "m_norm_g_3", "lam_q1_3", "lam_k1_3", "lam_q2_3", "lam_k2_3",
    "c_norm_g_3", "w_out_3", "ln1_g_3", "ln1_b_3", "w_up_3", "w_down_3", "ln2_g_3", "ln2_b_3",
]


def _flat(name, a):
    if name == "w_branch":
        return a.reshape(-1, a.shape[-1])
    if name == "x":
        return a.reshape(a.shape[1:])
    return a.reshape(-1, a.shape[-1])


def kernel(**inputs):
    import concourse.bacc as _bacc
    from concourse.bass_utils import run_bass_kernel_spmd as _run

    nc = _bacc.Bacc("TRN2", target_bir_lowering=False, num_devices=1)
    arrays, aps = {}, {}
    for name in _INS:
        a = np.ascontiguousarray(_flat(name, np.asarray(inputs[name])))
        arrays[f"in_{name}"] = a
        aps[name] = nc.dram_tensor(f"in_{name}", a.shape, mybir.dt.from_np(a.dtype), kind="ExternalInput").ap()
    out = nc.dram_tensor("out", (S, D), F32, kind="ExternalOutput").ap()
    build(nc, aps, out)
    r = _run(nc, [arrays], core_ids=[0])
    return r.results[0]["out"].reshape(1, S, D)
```

```python
import math
from contextlib import ExitStack, contextmanager

import concourse.bass as bass
from concourse import mybir
import numpy as np

F32 = mybir.dt.float32
F32R = mybir.dt.float32r
I32 = mybir.dt.int32
ALU = mybir.AluOpType
ACT = mybir.ActivationFunctionType
AX = mybir.AxisListType.X
ds = bass.ds

P = 128
S = 256
D = 2048
KT = D // P
CH = 2
TW = 512
RING = 4
AHEAD = RING - 1
NEG = -1.0e30
TAKEN = -3.0e38
ALPHA = 2.0 ** 0.25
LN_EPS, RMS_EPS = 1e-5, 1e-6

G_H, G_RANK, G_TAU = 4, 16, 16.0
BW = 1024
C_AQ, C_AV, C_ALR, C_AG = 0, 1024, 2048, 2064
C_BQ = C_AG + BW
C_BK = C_BQ + 1024
C_BV = C_BK + 128
C_BG = C_BV + 128
C_CQ = C_BG + BW
C_CV = C_CQ + 2048
C_CG = C_CV + 1024
C_MG = C_CG + BW
CONV_W, SHORT_W, GD_H = 31, 4, 8
D_FF2 = 5632
C_QKV2, C_Z2, C_BA2 = 2048, 5120, 6144
A_H, M_H, D_H = 6, 6, 4
C_VA = 1536
C_QI = 2304
C_KI = C_QI + 512
C_WI = C_KI + 64
C_QM = C_WI + 8
C_VM = C_QM + 1536
C_OM = C_VM + 768
C_IF = C_OM + 768
C_QC = C_IF + 12
C_VC = C_QC + 1024
TOPK = 64
D_FF3 = 8192
SHRINK = 2.0 ** -40
LARGE = 1.0e20
ROOT_MAX = math.sqrt(2.0 ** 128 / P) * SHRINK

R_DWW, R_DWB, R_CLG, R_CLB = 0, 31, 32, 33
R_SCW = 34
R_BM = R_SCW + SHORT_W * 3
R_GLAB = R_BM + 6
R_MNG, R_CNG, R_GLAG = R_GLAB + 1, R_GLAB + 2, R_GLAB + 3
R_CM = R_GLAG + 1
T_GDNW = 2
R_ALL = 64

MERGE = KT // CH + BW // P // CH
WIDTHS = {"alr": G_RANK, "bkv": 3 * P, "ba": 16, "va": 384, "kwi": P + 8, "vm": 384, "om": 384, "if": 12}
PIECES = {"bkv": 3, "kwi": 2}


class Count:

    def __init__(self):
        self.n, self.i, self.per = {}, None, {}

    def now(self, sem, k=0):
        v = self.n.get(sem, 0)
        self.n[sem] = v + k
        return v if self.i is None else v + self.i * self.per[sem]

    def next(self, sem, k=1):
        self.now(sem, k)
        return self.now(sem)

    @contextmanager
    def loop(self, eng, times, per):
        start = {s: self.n.get(s, 0) for s in per}
        with eng.Fori(0, times) as i:
            self.i, self.per = i, per
            yield i
        self.i, self.per = None, {}
        for s, k in per.items():
            assert self.n.get(s, 0) == start[s] + k, (s, self.n.get(s, 0) - start[s], k)
            self.n[s] = start[s] + times * k


class Section:

    def __init__(self, n, chunks, first, tiles, last):
        self.n, self.chunks, self.first, self.tiles, self.last = n, chunks, first, tuple(tiles), last

    def more(self, it):
        return it * (2 * self.chunks // RING)

    def chunk(self, u, c):
        return self.first + u * self.chunks + c


def plan_weights():
    first = [("aqk", 2), ("av", 2), ("alr", 1), ("ag", 2), ("bq", 2), ("bkv", 1), ("bg", 2),
             ("cqk", 4), ("cv", 2), ("cg", 2), ("merge", 12), ("wo", 4)]
    second = [("cval", 2), ("cgate", 2), ("qkv", 6), ("z", 2), ("ba", 1), ("wout2", 4),
              ("gu", 2 * D_FF2 // TW), ("down2", 4)]
    third = [("qka", 3), ("va", 2), ("qi", 1), ("kwi", 1), ("qkm", 3), ("vm", 2), ("om", 2), ("if", 1),
             ("qkc", 2), ("vc", 1), ("wout3", 4), ("up3", D_FF3 // TW), ("down3", 4)]
    order = first + second + third
    tiles, plan, widths, landed = [0, 0], {}, [], []
    for name, n in order:
        chunks = {"down2": D_FF2 // P // CH, "down3": D_FF3 // P // CH}.get(name, KT // CH)
        plan[name] = Section(n, chunks, len(widths), tiles, name == order[-1][0])
        total = n * (chunks + BW // P // CH) if name == "merge" else n * chunks
        for c in range(total):
            widths.append(WIDTHS.get(name, TW))
            before = landed[-RING] if len(landed) >= RING else 0
            landed.append(before + 16 * PIECES.get(name, 1))
        if name == "merge":
            tiles = [t + n for t in tiles]
        else:
            tiles = [tiles[0] + (n + 1) // 2, tiles[1] + n // 2]
    return plan, widths, landed


def tiles_of(eng, n, unroll=False):
    pairs = n // 2
    if pairs > 1 and not unroll:
        with eng.Fori(0, pairs) as i:
            for u in (0, 1):
                yield 2 * i + u, u, i
    else:
        for i in range(pairs):
            yield 2 * i, 0, i
            yield 2 * i + 1, 1, i
    if n % 2:
        yield n - 1, 0, pairs


def build(nc, I, out):
    plan, widths, landed = plan_weights()
    ctx = ExitStack()
    with ctx:
        free = [-(-nc.sbuf_base // 32) * 32]

        def sb(name, shape, dt=F32, at=None):
            if at is None:
                at = free[0]
                free[0] += -(-4 * int(np.prod(shape[1:])) // 32) * 32
            return nc.alloc_sbuf_tensor_at(name, shape, dt, offset=at)

        def sem(name):
            return ctx.enter_context(nc.semaphore(name))

        ring = sb("ring", [P, RING, CH, TW])
        w_hi = sb("w_hi", [P, RING, CH, TW], F32R)
        w_lo = sb("w_lo", [P, RING, CH, TW], F32R)
        xT_at = free[0]
        x_hi = sb("x_hi", [P, KT, S], F32R)
        x_lo = sb("x_lo", [P, KT, S], F32R)
        xT = sb("xT", [P, 2 * KT, S], at=xT_at)
        xtok = sb("xtok", [P, 2, D])
        ln_gb = sb("ln_gb", [P, 2, D])
        ARENA = 20480
        arena_at = free[0]
        arena = sb("arena", [P, ARENA])

        def rounded(name, at, *shape):
            return sb(name, [P, *shape], F32R, arena_at + 4 * at)

        y1_hi, y1_lo = rounded("y1_hi", 10240, 24, S), rounded("y1_lo", 0, 24, S)
        m_hi, m_lo = rounded("m_hi", 16384, KT, S), rounded("m_lo", 6144, KT, S)
        y_hi, y_lo = rounded("y_hi", 4096, KT, S), rounded("y_lo", 0, KT, S)
        h_hi, h_lo = rounded("h_hi", 16384, RING, CH, S), rounded("h_lo", 18432, RING, CH, S)
        ident = sb("ident", [P, P])
        ones = sb("ones", [P, P])
        upper = sb("upper", [P, S])
        causal = sb("causal", [P, 384])
        band = sb("band", [P, 384])
        causalT = sb("causalT", [P, 384])
        ndist = sb("ndist", [P, 384])
        levels = sb("levels", [P, 7, P])
        colp = sb("colp", [P, 8, R_ALL])
        bmc = sb("bmc", [P, 3, KT])
        small = sb("small", [P, 512])
        alrT = arena[0:G_RANK, 19456:19456 + S]
        gwu = arena[0:G_RANK, 19712:19712 + 512]
        ps = ctx.enter_context(nc.psum_tensor("ps", [P, 8, 512], F32))

        def area(at, *shape):
            n = int(np.prod(shape))
            assert at + n <= ARENA, (at, shape)
            v = arena[:, at:at + n]
            if len(shape) == 2:
                v = v.rearrange("p (a b) -> p a b", b=shape[1])
            elif len(shape) == 3:
                v = v.rearrange("p (a b c) -> p a b c", b=shape[1], c=shape[2])
            return v

        def cols(at, n):
            return small[:, at:at + n]

        eps_ln, eps_rms, one, eps_diff = cols(0, 1), cols(1, 1), cols(2, 1), cols(3, 1)
        sinks = cols(4, 16)
        lam = cols(20, 12)
        gdnA, gdndt = cols(32, 8), cols(40, 8)
        bib, bfb = cols(48, 6), cols(54, 6)
        slopes_a, slopes_c = cols(60, 6), cols(66, 4)
        stat = cols(72, 64)
        nmax, rsum, rinv, esink = ([cols(at + k, 4) for at in (136, 432)] for k in (0, 4, 8, 12))
        tokc = cols(160, 128)

        w_landed = [sem(f"w_landed{s}") for s in range(RING)]
        hi_ready = [sem(f"hi_ready{s}") for s in range(RING)]
        lo_ready = [sem(f"lo_ready{s}") for s in range(RING)]
        w_used = [sem(f"w_used{s}") for s in range(RING)]
        xh_ready, y_hi_ready, y_split = sem("xh_ready"), sem("y_hi_ready"), sem("y_split")
        narrow_ready, narrowT_ready, y_part = sem("narrow_ready"), sem("narrowT_ready"), sem("y_part")
        h_primed_hi, h_primed = sem("h_primed_hi"), sem("h_primed")
        tile_done = [sem(f"tile_done{u}") for u in range(2)]
        tile_free = [sem(f"tile_free{u}") for u in range(2)]
        x_landed, par_landed, ln_landed = sem("x_landed"), sem("par_landed"), sem("ln_landed")
        out_written = sem("out_written")
        iotas, consts = sem("iotas"), sem("consts")
        dve_order, act_order = sem("dve_order"), sem("act_order")
        table_ready, tableT_ready, table_zeroed = sem("table_ready"), sem("tableT_ready"), sem("table_zeroed")
        xTp_ready, xTp_used = sem("xTp_ready"), sem("xTp_used")
        norm_ready, xn_ready, xg_ready = sem("norm_ready"), sem("xn_ready"), sem("xg_ready")
        x_even, x_odd = sem("x_even"), sem("x_odd")
        var_ready, std_ready = sem("var_ready"), sem("std_ready")
        stage_over = sem("stage_over")
        gate_ready = sem("gate_ready")
        logits_ready, logits_used = sem("logits_ready"), sem("logits_used")
        max_ready, exp_done, probs_ready = sem("max_ready"), sem("exp_done"), sem("probs_ready")
        probsT_ready, probsT_out, o_ready, o_used = sem("probsT_ready"), sem("probsT_out"), sem("o_ready"), sem("o_used")
        sq_ready, ss_ready, root_ready = sem("sq_ready"), sem("ss_ready"), sem("root_ready")
        mm_ready, mm_used, vec_ready, act_ready = sem("mm_ready"), sem("mm_used"), sem("vec_ready"), sem("act_ready")
        fac_ready = sem("fac_ready")
        lam_landed, hid_ready = sem("lam_landed"), sem("hid_ready")
        conv_ready, silu_done = sem("conv_ready"), sem("silu_done")
        lm_ready, xp_ready, xs_ready, yp_ready, inv_ready = (sem(k) for k in (
            "lm_ready", "xp_ready", "xs_ready", "yp_ready", "inv_ready"))

        y1 = area(0, 24, S)
        mergedT = area(6144, KT, S)
        sig = ln_gb[:, 0, 0:4 * S].rearrange("p (a s) -> p a s", a=4)
        mtmp = ln_gb[:, 0, 4 * S:8 * S].rearrange("p (a s) -> p a s", a=4)
        a_qk, a_v, a_gate = area(6144, 8, S), area(8192, 2, BW), area(10240, 8, S)
        a_b, a_e = area(12288, 4, S), area(13312, 2, 4, S)
        a_qe = area(15360, 2, 4, S)
        a_ke = area(17408, 2, 4, S)
        a_sq, a_rn = area(13312, 8, S), area(15360, 4, S)
        a_at = ln_gb[:, 0, 0:4 * 384].rearrange("p (h n) -> p h n", h=4)
        s_q, s_kd, s_v, s_gate = area(6144, 8, S), area(8192, 2, S), area(10240, 2, P), area(12288, 8, S)
        m_qk, m_v, m_gate = area(6144, 16, S), area(10240, 2, BW), area(12288, 8, S)
        AT1 = 14336
        y2 = area(0, KT, S)
        c_qkv, c_z = area(4096, 24, S), area(10240, 8, S)
        HP, RP = CONV_W - 1, SHORT_W - 1
        c_h = area(12288, 8, HP + S)
        c_acc = area(14576, 8, S)
        c_raw = area(16624, 2, 4, RP + S)
        c_sq = area(12288, 8, S)
        c_mu, c_rs = area(18696, S), area(18952, S)
        l2_sq, l2_rn = xT[:, 0:KT, :], area(12288, 16, S)
        d_at, d_lt, d_l21 = area(12288, 8, 384), area(15360, 16, P), area(17408, 8, P)
        d_xs = area(18432, 16, P)
        d_lm = ln_gb[:, 1, :].rearrange("p (a b) -> p a b", b=P)
        d_dt = ln_gb[:, 1, 0:768].rearrange("p (a b) -> p a b", b=384)
        d_db = ln_gb[:, 1, 768:1536].rearrange("p (a b) -> p a b", b=384)
        d_vb = ln_gb[:, 0, :].rearrange("p (t n) -> p t n", t=2)
        d_t = xT[:, 0:8, :].rearrange("p a (c i) -> p (a c) i", c=2)
        d_tt = xT[:, 8:16, :].rearrange("p a (c i) -> p (a c) i", c=2)
        d_vn = area(8192, 2, 1024)
        d_sq, d_rn = xT[:, 0:8, :], xT[:, 8:16, :]
        hid = area(0, D_FF3 // P, S)
        f_sg = area(16384, 2, 4, S)
        t_ba = tokc[:, 0:32].rearrange("p (t c) -> p t c", t=2)
        t_beta = tokc[:, 32:48].rearrange("p (t c) -> p t c", t=2)
        t_x = tokc[:, 48:64].rearrange("p (t c) -> p t c", t=2)
        t_e = tokc[:, 64:80].rearrange("p (t c) -> p t c", t=2)
        t_A = tokc[:, 80:88]
        t_g = tokc[:, 88:104].rearrange("p (t c) -> p t c", t=2)
        t_gc = tokc[:, 104:120].rearrange("p (t c) -> p t c", t=2)
        scw = small[:, 288:384].rearrange("p (k c) -> p k c", k=SHORT_W)
        y3 = area(0, KT, S)
        e_qk, e_v, e_gate = area(4096, 12, S), area(7168, 2, 768), area(8704, 6, S)
        AT3 = 10240
        i_q, i_k = area(14080, 4, S), area(15104, S)
        i_sel, i_work, i_tmp = area(15360, 384), area(15744, 384), area(16128, 384)
        e_raw = area(14080, 2, 4, RP + S)
        e_bbc = area(16896, 6, S)
        e_cut, e_fits = area(16896, 4, S), area(17920, 4, S)
        e_sq, e_rn = area(AT3, 6, S), area(AT3 + 1536, 6, S)
        lam_rows = area(18944, 4, 64)
        lam_prod = area(19200, 2, 64)
        t_w = tokc[:, 0:16].rearrange("p (t c) -> p t c", t=2)
        top8 = tokc[:, 16:32].rearrange("p (t c) -> p t c", t=2)
        t_if = tokc[:, 32:56].rearrange("p (t c) -> p t c", t=2)
        t_lf = tokc[:, 56:68].rearrange("p (t c) -> p t c", t=2)
        t_ef = tokc[:, 68:80].rearrange("p (t c) -> p t c", t=2)
        t_na = tokc[:, 80:92].rearrange("p (t c) -> p t c", t=2)
        mcw = small[:, 384:432].rearrange("p (k c) -> p k c", k=SHORT_W)
        nar_ba, nar_kwi, nar_if = area(16624, S), area(15360, S), area(16384, S)
        table = area(0, 1024)
        row = "(k p) c -> p k c"

        block = ctx.enter_context(nc.Block())

        class Heads:

            def __init__(self, kind, pairs, dv, at, q, k, v):
                self.kind, self.pairs, self.dv = kind, pairs, dv
                self.outs = 1 if kind == "diff" else 2
                self.halves = kind in ("swa", "diff")
                self.q, self.k, self.v = q, k, v
                self.sm = [area(at + 2304 * e, 2, 384) for e in range(2)]
                self.p = [area(at + 2304 * e + 768, 2, 384) for e in range(2)]
                self.pT = [area(at + 2304 * e + 1536, 2, 384) for e in range(2)]

            def logits(self, i, u):
                return (4, 0)[i % 2] + u

        half = lambda v, u: v[64 * u:64 * u + 64]
        col = lambda v, h: v[:, :, h * P:(h + 1) * P]
        swa = Heads("swa", 8, 64, AT1, lambda i, u: half(s_q, u)[:, i], lambda i, u: half(s_kd, u)[:, i // 4],
                    lambda i, u: s_v[:, :, 64 * (i // 4):64 * (i // 4) + 64])
        moba = Heads("moba", 4, P, AT1, lambda i, u: m_qk[:, 2 * i + u], lambda i, u: m_qk[:, 8 + 2 * i + u],
                     lambda i, u: col(m_v, 2 * i + u))
        dsa, mls = (Heads(kind, 3, P, AT3, lambda i, u: e_qk[:, 2 * i + u], lambda i, u: e_qk[:, 6 + 2 * i + u],
                          lambda i, u: col(e_v, 2 * i + u)) for kind in ("dsa", "mlstm"))
        dif = Heads("diff", D_H, P, AT3, lambda i, u: half(e_qk, u)[:, i], lambda i, u: half(e_qk, u)[:, 4 + i],
                    lambda i, u: col(e_v, i))

        @block.sync
        def _(sp):
            n = Count()

            def held(v):
                return v if isinstance(v, int) else sp.snap(v)

            def load(g, more, pieces):
                if g >= RING:
                    sp.wait_ge(lo_ready[g % RING], g // RING + more)
                at = 0
                for src in pieces:
                    sp.dma_start(ring[:, g % RING, :, at:at + src.shape[1]], src.rearrange(row, p=P))\
                      .then_inc(w_landed[g % RING], 16)
                    at += src.shape[1]

            def rows(c):
                return slice(c * CH * P, (c + 1) * CH * P)

            def tile_loads(name, w, col, width=TW, second=None):
                sec = plan[name]
                for t, u, it in tiles_of(sp, sec.n):
                    at = held(col + t * width if second is None else col + u * second + it * width)
                    for c in range(sec.chunks):
                        load(sec.chunk(u, c), sec.more(it), [w[rows(c), ds(at, width)]])

            def piece_loads(name, w, pieces):
                sec = plan[name]
                for c in range(sec.chunks):
                    load(sec.chunk(0, c), 0, [w[rows(c), col:col + width] for col, width in pieces])

            w = I["w_in"]
            tile_loads("aqk", w, C_AQ)
            tile_loads("av", w, C_AV)
            piece_loads("alr", w, [(C_ALR, G_RANK)])
            tile_loads("ag", w, C_AG)
            tile_loads("bq", w, C_BQ)
            piece_loads("bkv", w, [(C_BK, 64), (C_BK, P), (C_BK + 64, 64 + P)])
            tile_loads("bg", w, C_BG)
            tile_loads("cqk", w, C_CQ)
            tile_loads("cv", w, C_CV)
            tile_loads("cg", w, C_CG)
            sec = plan["merge"]
            with sp.Fori(0, 4) as j:
                for b in range(3):
                    gate_at = held(C_MG + b * D + j * TW)
                    branch_at = held(j * TW)
                    for c in range(MERGE):
                        g, more = sec.first + b * MERGE + c, j * (3 * MERGE // RING)
                        if c < sec.chunks:
                            load(g, more, [w[rows(c), ds(gate_at, TW)]])
                        elif c > sec.chunks:
                            load(g, more, [I["w_branch"][rows(b * (BW // P // CH) + c - sec.chunks), ds(branch_at, TW)]])
            tile_loads("wo", I["w_o"], 0)
            w = I["w_in_2"]
            tile_loads("cval", w, 0)
            tile_loads("cgate", w, 1024)
            tile_loads("qkv", w, C_QKV2)
            tile_loads("z", w, C_Z2)
            piece_loads("ba", w, [(C_BA2, 16)])
            tile_loads("wout2", I["w_out_2"], 0)
            tile_loads("gu", I["w_gate_up_2"], 0, second=D_FF2)
            tile_loads("down2", I["w_down_2"], 0)
            w = I["w_in_3"]
            tile_loads("qka", w, 0)
            tile_loads("va", w, C_VA, 384)
            tile_loads("qi", w, C_QI)
            piece_loads("kwi", w, [(C_KI, 64), (C_KI, 64 + 8)])
            tile_loads("qkm", w, C_QM)
            tile_loads("vm", w, C_VM, 384)
            tile_loads("om", w, C_OM, 384)
            piece_loads("if", w, [(C_IF, 12)])
            tile_loads("qkc", w, C_QC)
            tile_loads("vc", w, C_VC)
            tile_loads("wout3", I["w_out_3"], 0)
            tile_loads("up3", I["w_up_3"], 0)
            tile_loads("down3", I["w_down_3"], 0)
            for c in range(4):
                sp.wait_ge((x_even, x_odd)[c % 2], 2 * 5 - 1 + c // 2)
                sp.dma_start(out.rearrange("(t p) c -> p t c", p=P)[:, :, c * TW:(c + 1) * TW],
                             xtok[:, :, c * TW:(c + 1) * TW]).then_inc(out_written, 16)
            sp.wait_ge(out_written, 4 * 16)

        posi = area(2048, P)
        posj = area(2048 + P, P)
        posx = area(2048 + 2 * P, P)
        posy = area(2048 + 3 * P, P)

        @block.gpsimd
        def _(pool):
            n = Count()
            pool.iota(posi.bitcast(I32), [[1, P]], base=0, channel_multiplier=0).then_inc(iotas, 1)
            pool.iota(posj.bitcast(I32), [[0, P]], base=0, channel_multiplier=1).then_inc(iotas, 1)

            def add_shift():
                for c in (0, 2):
                    pool.wait_ge(xg_ready, n.next(xg_ready))
                    xv = xtok[:, :, c * TW:(c + 1) * TW]
                    pool.tensor_tensor(xv, xv, ln_gb[:, 1:2, c * TW:(c + 1) * TW].to_broadcast([P, 2, TW]), ALU.add)\
                        .then_inc(x_even, 1)

            add_shift()
            for name in ("qkv", "z", "ba"):
                sec = plan[name]
                for t, u, it in tiles_of(pool, sec.n):
                    for c in range(AHEAD, AHEAD + sec.chunks):
                        g, more = sec.chunk(u, c), sec.more(it)
                        s = g % RING
                        pool.wait_ge(hi_ready[s], g // RING + 1 + more)
                        pool.tensor_tensor(w_lo[:, s, :, 0:widths[g]], ring[:, s, :, 0:widths[g]],
                                           w_hi[:, s, :, 0:widths[g]].bitcast(F32), ALU.subtract).then_inc(lo_ready[s], 1)
            add_shift()
            add_shift()
            add_shift()
            add_shift()

        @block.tensor
        def _(pe):
            n = Count()

            def products(out, left, right, start, stop):
                first = pe.matmul(out, left[0], right[0], start=start, stop=False)
                pe.matmul(out, left[0], right[1], start=False, stop=False)
                return first, pe.matmul(out, left[1], right[0], start=False, stop=stop)

            def chunk(g, more):
                pe.wait_ge(lo_ready[g % RING], g // RING + 1 + more)

            def tile(kind, u, g, more, chunks, src, width):
                for c in range(chunks):
                    s = (g + c) % RING
                    chunk(g + c, more)
                    x = src(c, s)
                    for k in range(CH):
                        for e in range(width // P if kind == "F" else 2):
                            go, end = c == 0 and k == 0, c == chunks - 1 and k == CH - 1
                            if kind == "F":
                                out, go = ps[:, 2 * u + e // 2, (e % 2) * S:(e % 2) * S + S], go and e % 2 == 0
                                end = end and (e % 2 == 1 or e == width // P - 1)
                                wv = [v[:, s, k, e * P:(e + 1) * P] for v in (w_hi, w_lo)]
                                first, last = products(out, wv, [v[:, k, :] for v in x], go, end)
                            else:
                                out = ps[:, 2 * u + e, 0:width]
                                wv = [v[:, s, k, 0:width] for v in (w_hi, w_lo)]
                                first, last = products(out, [v[:, k, e * P:(e + 1) * P] for v in x], wv, go, end)
                            if k == 0 and e == 0 and g + c > 0:
                                first.then_inc(w_used[(g + c - 1) % RING], 1)
                return last

            def stationary(hi, lo, at=0):
                return lambda c, s: [v[:, at + c * CH:at + (c + 1) * CH, :] for v in (hi, lo)]

            def project(name, kind, src=stationary(x_hi, x_lo), width=TW):
                sec = plan[name]
                for t, u, it in tiles_of(pe, sec.n):
                    pe.wait_ge(tile_free[u], sec.tiles[u] + it)
                    tile(kind, u, sec.chunk(u, 0), sec.more(it), sec.chunks, src, width).then_inc(tile_done[u], 1)

            def in_parts(parts):
                def src(c, s):
                    pe.wait_ge(y_part, parts(c))
                    return stationary(y_hi, y_lo)(c, s)
                return src

            def project_pieces(name, ops):
                sec = plan[name]
                closes = {bank: (kind, col, int(kind == "T")) for kind, col, m, bank, at in ops}
                pe.wait_ge(tile_free[0], sec.tiles[0])
                for c in range(sec.chunks):
                    g = sec.chunk(0, c)
                    chunk(g, 0)
                    for k in range(CH):
                        x = [v[:, c * CH + k, :] for v in (x_hi, x_lo)]
                        banks = set()
                        for kind, col, m, bank, at in ops:
                            w = [v[:, g % RING, k, col:col + m] for v in (w_hi, w_lo)]
                            for e in range(1 if kind == "F" else 2):
                                go = c == 0 and k == 0 and bank not in banks
                                end = c == sec.chunks - 1 and k == CH - 1 and (kind, col, e) == closes[bank]
                                if kind == "F":
                                    first, last = products(ps[0:m, bank, at:at + S], w, x, go, end)
                                else:
                                    first, last = products(ps[:, bank, at + e * m:at + e * m + m],
                                                           [v[:, e * P:(e + 1) * P] for v in x], w, go, end)
                                if not banks and k == 0 and g > 0:
                                    first.then_inc(w_used[(g - 1) % RING], 1)
                                banks.add(bank)
                last.then_inc(tile_done[0], 1)

            def by_token(m, bank, nar):
                pe.wait_ge(narrow_ready, n.next(narrow_ready))
                for t in range(2):
                    last = pe.transpose(ps[:, bank, S + t * m:S + (t + 1) * m], nar[0:m, t * P:(t + 1) * P], ident[0:m, 0:m])
                last.then_inc(narrowT_ready, 1)

            def transpose_x(normed=True):
                for g in range(KT // 2):
                    if normed and g % 2 == 0:
                        ready = (x_even, x_odd)[g // 2 % 2]
                        pe.wait_ge(ready, n.next(ready))
                    pe.wait_ge(xTp_used, max(0, n.now(xTp_used, 1) - 3))
                    for k in range(2):
                        for t in range(2):
                            last = pe.transpose(ps[:, 4 + g % 4, k * S + t * P:k * S + (t + 1) * P],
                                                xtok[:, t, (2 * g + k) * P:(2 * g + k + 1) * P], ident[:])
                    last.then_inc(xTp_ready, 1)

            def attend(A):
                pe.wait_ge(gate_ready, n.next(gate_ready))

                def logits(i):
                    if i >= A.pairs:
                        return
                    if i >= 2:
                        pe.wait_ge(logits_used, n.next(logits_used, 2))
                    for u in range(2):
                        q, k, b = A.q(i, u), A.k(i, u), A.logits(i, u)
                        pe.matmul(ps[:, b, 0:P], q[:, 0:P], k[:, 0:P], start=True, stop=True)
                        pe.matmul(ps[:, b, P:384], q[:, P:S], k[:, 0:S], start=True, stop=True).then_inc(logits_ready, 1)

                logits(0)
                logits(1)
                for i in range(A.pairs):
                    for u in range(A.outs):
                        pe.wait_ge(probs_ready, n.next(probs_ready))
                        for c in range(3):
                            last = pe.transpose(ps[:, 6 + u, c * P:(c + 1) * P], A.p[i % 2][:, u, c * P:(c + 1) * P], ident[:])
                        last.then_inc(probsT_ready, 1)
                    logits(i + 2)
                    if i:
                        pe.wait_ge(o_used, n.next(o_used))
                    for u in range(A.outs):
                        pe.wait_ge(probsT_out, n.next(probsT_out))
                        o = ps[64 * u:64 * u + 64, 2, 0:S] if A.kind == "swa" else ps[:, 2 + u, 0:S]
                        v, pT = A.v(i, u), A.pT[i % 2][:, u]
                        pe.matmul(o, v[:, 0, :], pT[:, 0:S], start=True, stop=False)
                        last = pe.matmul(o[:, P:S], v[:, 1, :], pT[:, S:384], start=False, stop=True)
                    last.then_inc(o_ready, 1)
                n.now(logits_used, 4)
                pe.wait_ge(o_used, n.next(o_used))

            def square_sums(src, heads, tiles):
                pe.wait_ge(sq_ready, n.next(sq_ready))
                for g in range(heads // 2):
                    if g >= 4:
                        pe.wait_ge(root_ready, n.next(root_ready))
                    for e in range(tiles):
                        v = src[:, 2 * g * tiles:(2 * g + 2) * tiles, :].rearrange("p (h e) s -> p h e s", e=tiles)
                        last = pe.matmul(ps[:, 4 + g % 4, :].rearrange("p (h s) -> p h s", h=2), ones[:], v[:, :, e, :],
                                         start=(e == 0), stop=(e == tiles - 1))
                    last.then_inc(ss_ready, 1)
                pe.wait_ge(root_ready, n.next(root_ready, min(4, heads // 2)))

            hidden = lambda c, s: (h_hi[:, s], h_lo[:, s])

            pe.wait_ge(consts, 1)
            pe.wait_ge(par_landed, 16 * 18)
            for t in range(8):
                last = pe.transpose(ps[:, 0, t * R_ALL:(t + 1) * R_ALL], table[0:R_ALL, t * P:(t + 1) * P],
                                    ident[0:R_ALL, 0:R_ALL])
            last.then_inc(tableT_ready, 1)
            pe.wait_ge(x_landed, 16)
            transpose_x(False)
            pe.wait_ge(xTp_used, n.now(xTp_used))
            pe.wait_ge(table_ready, 1)

            project("aqk", "F")
            project("av", "T")
            project_pieces("alr", [("F", 0, G_RANK, 0, 0)])
            project("ag", "F")
            pe.wait_ge(vec_ready, n.next(vec_ready))
            for h in range(G_H):
                last = pe.matmul(ps[:, 4 + h // 2, (h % 2) * S:(h % 2 + 1) * S], gwu[:, h * P:(h + 1) * P], alrT,
                                 start=True, stop=True)
            last.then_inc(mm_ready, 1)
            for lv in range(8):
                pe.wait_ge(fac_ready, n.next(fac_ready))
                b = 4 + 2 * (lv % 2)
                if lv < 7:
                    pe.wait_ge(mm_used, max(0, n.now(mm_used, 1) - 1))
                    for h in range(G_H):
                        for c in range(2):
                            last = pe.matmul(ps[:, b + h // 2, (h % 2) * S + c * P:(h % 2) * S + (c + 1) * P],
                                             a_ke[:, lv % 2, h, c * P:(c + 1) * P], a_qe[:, lv % 2, h, c * P:(c + 1) * P],
                                             start=True, stop=True)
                else:
                    pe.wait_ge(mm_used, max(0, n.now(mm_used, 1) - 1))
                    for h in range(G_H):
                        last = pe.matmul(ps[:, b, h * P:(h + 1) * P], a_ke[:, 1, h, 0:P], a_qe[:, 1, h, P:S],
                                         start=True, stop=True)
                last.then_inc(mm_ready, 1)
            pe.wait_ge(fac_ready, n.next(fac_ready))
            pe.wait_ge(mm_used, max(0, n.now(mm_used, 1) - 1))
            for h in range(G_H):
                for c in range(2):
                    last = pe.matmul(ps[:, 4 + h // 2, (h % 2) * S + c * P:(h % 2) * S + (c + 1) * P],
                                     a_qk[:, 4 + h, c * P:(c + 1) * P], a_qe[:, 0, h, c * P:(c + 1) * P],
                                     start=True, stop=True)
            last.then_inc(mm_ready, 1)
            pe.wait_ge(mm_used, n.now(mm_used))
            for h in range(G_H):
                for e in range(2):
                    o = ps[:, 4 + h, e * S:(e + 1) * S]
                    v = a_v[:, :, h * S + e * P:h * S + (e + 1) * P]
                    pe.matmul(o, v[:, 0, :], a_at[:, h, 0:S], start=True, stop=False)
                    last = pe.matmul(o[:, P:S], v[:, 1, :], a_at[:, h, S:384], start=False, stop=True)
            last.then_inc(mm_ready, 1)
            square_sums(a_sq, G_H, 2)

            pe.wait_ge(stage_over, 1)
            project("bq", "F")
            project_pieces("bkv", [("F", 0, P, 0, 0), ("F", P, P, 0, S), ("T", 2 * P, P, 1, 0)])
            project("bg", "F")
            attend(swa)

            project("cqk", "F")
            project("cv", "T")
            project("cg", "F")
            attend(moba)

            sec = plan["merge"]
            with pe.Fori(0, 4) as j:
                for b in range(3):
                    it, g, more = 3 * j + b, sec.first + b * MERGE, j * (3 * MERGE // RING)
                    pe.wait_ge(tile_free[0], sec.tiles[0] + it)
                    tile("F", 0, g, more, sec.chunks, stationary(x_hi, x_lo), TW).then_inc(tile_done[0], 1)
                    pe.wait_ge(tile_free[1], sec.tiles[1] + it)
                    if b == 0:
                        pe.wait_ge(y_split, 3)
                    tile("F", 1, g + sec.chunks, more, MERGE - sec.chunks, stationary(y1_hi, y1_lo, 8 * b), TW)\
                        .then_inc(tile_done[1], 1)
            pe.wait_ge(stage_over, 4)
            project("wo", "T", stationary(m_hi, m_lo))
            transpose_x()
            pe.wait_ge(xTp_used, n.now(xTp_used))
            project("cval", "F")
            project("cgate", "F")
            project("qkv", "F")
            project("z", "F")
            def channel_sums(b, src):
                pe.wait_ge(conv_ready, n.next(conv_ready))
                for t in range(8):
                    last = pe.matmul(ps[:, b, 0:S], ones[:], src[:, t, :], start=(t == 0), stop=(t == 7))
                last.then_inc(mm_ready, 1)
            project_pieces("ba", [("F", 0, 16, 0, 0)])
            channel_sums(4, c_acc)
            by_token(16, 0, nar_ba)
            channel_sums(5, c_sq)
            square_sums(l2_sq, 16, 1)
            pe.wait_ge(fac_ready, n.next(fac_ready))
            pe.matmul(ps[:, 0, 0:8], upper[:, 0:P], t_g[:, 0], start=True, stop=True)
            pe.matmul(ps[:, 0, 8:16], ones[:], t_g[:, 0], start=True, stop=False)
            pe.matmul(ps[:, 0, 8:16], upper[:, 0:P], t_g[:, 1], start=False, stop=True)
            for t in range(2):
                for h in range(GD_H):
                    last = pe.transpose(ps[:, 4 + 2 * t + h // 4, (h % 4) * P:(h % 4 + 1) * P],
                                        c_qkv[:, 16 + h, t * P:(t + 1) * P], ident[:])
            last.then_inc(mm_ready, 1)
            pe.wait_ge(fac_ready, n.next(fac_ready))
            for h in range(GD_H):
                b = 2 + 3 * (h % 2)
                if h >= 2:
                    pe.wait_ge(fac_ready, n.next(fac_ready))
                g = [t_g[:, t, h:h + 1].to_broadcast([P, P]) for t in range(2)]
                beta = [t_beta[:, t, h:h + 1].to_broadcast([P, P]) for t in range(2)]
                pe.matmul(ps[:, b, 0:S], g[0], upper[:], start=True, stop=False)
                pe.matmul(ps[:, b, P:S], g[1], upper[:, 0:P], start=False, stop=True)
                for t in range(2):
                    pe.matmul(ps[:, b, S + t * P:S + (t + 1) * P], beta[t], ident[:], start=True, stop=True)
                q, k = c_qkv[:, h], c_qkv[:, 8 + h]
                for c, r in ((1, k), (2, q)):
                    pe.matmul(ps[:, b + c, 0:S], k[:, 0:P], r, start=True, stop=True)
                    last = pe.matmul(ps[:, b + c, S:384], k[:, P:S], r[:, P:S], start=True, stop=True)
                last.then_inc(mm_ready, 1)
            pe.wait_ge(fac_ready, n.next(fac_ready, 2))
            pe.wait_ge(inv_ready, n.next(inv_ready, 4))
            with n.loop(pe, 7, {lm_ready: 4, xs_ready: 4, inv_ready: 4}):
                for g in range(4):
                    pe.wait_ge(lm_ready, n.next(lm_ready))
                    for e in range(4):
                        last = pe.matmul(ps[:, g, e * P:(e + 1) * P], d_lm[:, 4 * g + e], d_t[:, 4 * g + e],
                                         start=True, stop=True)
                    last.then_inc(xp_ready, 1)
                for g in range(4):
                    pe.wait_ge(xs_ready, n.next(xs_ready))
                    if g >= 2:
                        pe.wait_ge(inv_ready, n.next(inv_ready))
                    for e in range(4):
                        pe.matmul(ps[:, 4 + g % 2, e * P:(e + 1) * P], d_tt[:, 4 * g + e], d_xs[:, 4 * g + e],
                                  start=True, stop=True)
                    for e in range(4):
                        last = pe.matmul(ps[:, 6 + g % 2, e * P:(e + 1) * P], d_xs[:, 4 * g + e], d_tt[:, 4 * g + e],
                                         start=True, stop=True)
                    last.then_inc(yp_ready, 1)
                pe.wait_ge(inv_ready, n.next(inv_ready, 2))
            def by_head(b, left, right):
                for h in range(GD_H):
                    last = pe.matmul(ps[:, b + h // 4, (h % 4) * P:(h % 4 + 1) * P], left(h), right(h),
                                     start=True, stop=True)
                last.then_inc(mm_ready, 1)
            head = lambda v, t: lambda h: v[:, t, h * P:(h + 1) * P]
            by_head(0, lambda h: d_tt[:, 2 * h], head(d_vb, 0))
            pe.wait_ge(fac_ready, n.next(fac_ready))
            by_head(2, lambda h: d_l21[:, h], head(d_vn, 0))
            pe.wait_ge(fac_ready, n.next(fac_ready))
            by_head(0, lambda h: d_tt[:, 2 * h + 1], head(d_vb, 1))
            pe.wait_ge(fac_ready, n.next(fac_ready))
            for h in range(GD_H):
                o = ps[:, 4 + h // 2, (h % 2) * S:(h % 2 + 1) * S]
                pe.matmul(o, d_vn[:, 0, h * P:(h + 1) * P], d_at[:, h, 0:S], start=True, stop=False)
                last = pe.matmul(o[:, P:S], d_vn[:, 1, h * P:(h + 1) * P], d_at[:, h, S:384], start=False, stop=True)
            last.then_inc(mm_ready, 1)
            square_sums(d_sq, GD_H, 1)
            project("wout2", "T", in_parts(lambda c: 1 if c < 4 else c - 2))
            transpose_x()
            pe.wait_ge(xTp_used, n.now(xTp_used))
            project("gu", "F")
            pe.wait_ge(h_primed, AHEAD)
            project("down2", "T", hidden)
            transpose_x()
            pe.wait_ge(xTp_used, n.now(xTp_used))
            project("qka", "F")
            project("va", "T", width=384)
            project("qi", "F")
            project_pieces("kwi", [("F", 0, P, 0, 0), ("F", P, 8, 1, 0)])
            by_token(8, 1, nar_kwi)
            pe.wait_ge(fac_ready, 23)
            for h in range(8):
                b = 4 + h % 4
                if h >= 4:
                    pe.wait_ge(mm_used, n.next(mm_used))
                q, k = i_q[64 * (h % 2):64 * (h % 2) + 64, h // 2], i_k[64 * (h % 2):64 * (h % 2) + 64]
                pe.matmul(ps[:, b, 0:P], q[:, 0:P], k[:, 0:P], start=True, stop=True)
                pe.matmul(ps[:, b, P:384], q[:, P:S], k, start=True, stop=True).then_inc(mm_ready, 1)
            pe.wait_ge(mm_used, n.next(mm_used, 4))
            attend(dsa)
            project("qkm", "F")
            project("vm", "T", width=384)
            project("om", "F", width=384)
            project_pieces("if", [("F", 0, 12, 0, 0)])
            by_token(12, 0, nar_if)
            pe.wait_ge(fac_ready, 24)
            pe.matmul(ps[:, 0, 0:6], upper[:, 0:P], t_lf[:, 0], start=True, stop=True)
            pe.matmul(ps[:, 0, 6:12], ones[:], t_lf[:, 0], start=True, stop=False)
            pe.matmul(ps[:, 0, 6:12], upper[:, 0:P], t_lf[:, 1], start=False, stop=True).then_inc(mm_ready, 1)
            for h in range(M_H):
                o = ps[:, 4 + h // 2, (h % 2) * S:(h % 2 + 1) * S]
                lf = [t_ef[:, t, h:h + 1].to_broadcast([P, P]) for t in range(2)]
                li = [t_if[:, t, h:h + 1].to_broadcast([P, P]) for t in range(2)]
                pe.matmul(o, lf[0], upper[:], start=True, stop=False)
                pe.matmul(o[:, P:S], lf[1], upper[:, 0:P], start=False, stop=False)
                pe.matmul(o[:, 0:P], li[0], ident[:], start=False, stop=False)
                last = pe.matmul(o[:, P:S], li[1], ident[:], start=False, stop=True)
            last.then_inc(mm_ready, 1)
            pe.wait_ge(mm_used, n.next(mm_used))
            attend(mls)
            square_sums(e_sq, M_H, 1)
            project("qkc", "F")
            project("vc", "T")
            attend(dif)
            square_sums(e_sq, D_H, 1)
            project("wout3", "T", in_parts(lambda c: 6 if c < (A_H + M_H) // CH else 7))
            transpose_x()
            pe.wait_ge(xTp_used, n.now(xTp_used))
            project("up3", "F")
            pe.wait_ge(h_primed, 2 * AHEAD)
            project("down3", "T", hidden)

        @block.scalar
        def _(act):
            n = Count()

            def link(ins):
                ins.then_inc(act_order, 1)
                act.wait_ge(act_order, n.next(act_order))

            act.dma_start(xtok[:], I["x"].rearrange("(t p) c -> p t c", p=P)).then_inc(x_landed, 16)
            act.wait_ge(table_zeroed, 1)
            for dst, src in [
                (table[R_DWW:R_DWW + CONV_W, :], I["conv_dw_w_2"]),
                (table[R_DWB:R_DWB + 1, :], I["conv_dw_b_2"]),
                (table[R_CLG:R_CLG + 1, :], I["conv_ln_g_2"]),
                (table[R_CLB:R_CLB + 1, :], I["conv_ln_b_2"]),
                (table[R_SCW:R_SCW + 12, :], I["gdn_conv_w_2"].rearrange("k (a c) -> (k a) c", c=1024)),
                (table[R_BM:R_BM + 6, :], I["b_merge"].rearrange("b (a c) -> (b a) c", c=1024)),
                (table[R_GLAB:R_GLAB + 1, 0:512], I["gla_b"]),
                (table[R_MNG:R_MNG + 1, 0:768], I["m_norm_g_3"]),
                (table[R_CNG:R_CNG + 1, 0:512], I["c_norm_g_3"]),
                (table[R_GLAG:R_GLAG + 1, 0:256], I["gla_norm_g"]),
                (table[R_GLAG:R_GLAG + 1, T_GDNW * P:(T_GDNW + 1) * P], I["gdn_norm_w_2"]),
                (table[R_CM:R_CM + 8, 0:768], I["conv_m_3"].rearrange("k (a c) -> (k a) c", c=768)),
                (gwu, I["gla_w_up"]),
                (sinks, I["swa_sinks"].to_broadcast([P, 16])),
                (gdnA, I["gdn_A_log_2"].to_broadcast([P, 8])),
                (gdndt, I["gdn_dt_bias_2"].to_broadcast([P, 8])),
                (bib, I["b_i_3"].to_broadcast([P, 6])),
                (bfb, I["b_f_3"].to_broadcast([P, 6])),
            ]:
                act.dma_start(dst, src).then_inc(par_landed, 16)

            def split(g, more=0, rows=None):
                s, width = g % RING, TW
                if isinstance(more, int):
                    g, more = g + more * RING, 0
                    if g >= len(widths):
                        return
                    width = widths[g]
                act.wait_ge(w_landed[s], landed[g] + more * 16)
                if g >= RING:
                    act.wait_ge(w_used[s], g // RING + more)
                last = act.activation(w_hi[:, s, :, 0:width], ring[:, s, :, 0:width], ACT.Copy)
                if rows is not None:
                    last = act.activation(h_hi[:, s], hid[:, rows:rows + CH, :], ACT.Copy)
                last.then_inc(hi_ready[s], 1)

            def splits(sec, u, it, hidden=False):
                for c in range(AHEAD, AHEAD + sec.chunks):
                    split(sec.chunk(u, c), sec.more(it), c % sec.chunks * CH if hidden else None)

            def pass_by(*names, hidden=False):
                for name in names:
                    for t, u, it in tiles_of(act, plan[name].n, plan[name].last):
                        splits(plan[name], u, it, hidden)

            def prime_hidden(name):
                for c in range(AHEAD):
                    s = plan[name].chunk(0, c) % RING
                    act.activation(h_hi[:, s], hid[:, c * CH:(c + 1) * CH, :], ACT.Copy).then_inc(h_primed_hi, 1)

            def take_x():
                for g in range(KT // 2):
                    act.wait_ge(xTp_ready, n.next(xTp_ready))
                    act.activation(x_hi[:, 2 * g:2 * g + 2, :].rearrange("p a s -> p (a s)"), ps[:, 4 + g % 4, :], ACT.Copy)\
                       .then_inc(xh_ready, 1)

            def load_ln(g, b):
                act.dma_start(ln_gb[:, 0, :], g.to_broadcast([P, D])).then_inc(ln_landed, 16)
                act.dma_start(ln_gb[:, 1, :], b.to_broadcast([P, D])).then_inc(ln_landed, 16)

            def gates(name, dst, func, width=TW):
                sec = plan[name]
                per = width // P
                for t, u, it in tiles_of(act, sec.n):
                    splits(sec, u, it)
                    act.wait_ge(tile_done[u], sec.tiles[u] + it + 1)
                    act.activation(dst[:, ds(t * per, per), :].rearrange("p a s -> p (a s)"),
                                   ps[:, 2 * u:2 * u + 2, :].rearrange("p a s -> p (a s)")[:, 0:per * S],
                                   func).then_inc(tile_free[u], 1)

            def softmax_exp(A, sink=None):
                def exps(i):
                    e = i % 2
                    for u in range(2):
                        act.wait_ge(max_ready, n.next(max_ready))
                        if sink is not None:
                            for t in range(2):
                                k = 2 * u + t
                                act.activation(esink[e][:, k:k + 1], sink(i, u, t), ACT.Exp, bias=nmax[e][:, k:k + 1])
                        for t, (c0, c1) in enumerate(((0, P), (P, 384))):
                            k = 2 * u + t
                            sums = {} if A.kind == "mlstm" else {"accum_out": rsum[e][:, k:k + 1]}
                            last = act.activation(A.p[e][:, u, c0:c1], A.sm[e][:, u, c0:c1], ACT.Exp,
                                                  bias=nmax[e][:, k:k + 1], **sums)
                        last.then_inc(exp_done, 1)

                exps(0)
                for i in range(A.pairs):
                    if i + 1 < A.pairs:
                        exps(i + 1)
                    for u in range(A.outs):
                        act.wait_ge(probsT_ready, n.next(probsT_ready))
                        act.activation(A.pT[i % 2][:, u], ps[:, 6 + u, 0:384], ACT.Copy).then_inc(probsT_out, 1)

            def roots(dst, heads, scale, eps):
                for g in range(heads // 2):
                    act.wait_ge(ss_ready, n.next(ss_ready))
                    last = act.activation(dst[:, 2 * g:2 * g + 2, :].rearrange("p a s -> p (a s)"), ps[:, 4 + g % 4, :],
                                          ACT.Sqrt, bias=eps, scale=scale)
                    last.then_inc(root_ready, 1)

            def ln_roots():
                act.wait_ge(var_ready, n.next(var_ready))
                act.activation(stat[:, 28:30], stat[:, 26:28], ACT.Sqrt, bias=eps_ln).then_inc(std_ready, 1)
                act.wait_ge(norm_ready, n.next(norm_ready))
                for c in range(4):
                    for t in range(2):
                        xv = xtok[:, t, c * TW:(c + 1) * TW]
                        last = act.activation(xv, xv, ACT.Identity, scale=stat[:, 28 + t:29 + t], bias=stat[:, 30 + t:31 + t])
                    last.then_inc(xn_ready, 1)

            for g in range(AHEAD):
                split(g)
            take_x()
            pass_by("aqk", "av", "alr")
            gates("ag", a_gate, ACT.Silu)
            act.wait_ge(vec_ready, n.next(vec_ready, 2))
            link(act.activation(a_e[:, 0], a_e[:, 0], ACT.Exp))
            act.activation(a_e[:, 0], a_e[:, 0], ACT.Ln, bias=one).then_inc(act_ready, 1)
            for lv in range(8):
                act.wait_ge(vec_ready, n.next(vec_ready))
                act.activation(a_e[:, lv % 2], a_e[:, lv % 2], ACT.Exp).then_inc(act_ready, 1)
            act.wait_ge(vec_ready, n.next(vec_ready))
            act.activation(a_sq, y1[:, 0:8, :], ACT.Square).then_inc(sq_ready, 1)
            roots(a_rn, G_H, 1.0 / S, eps_rms)
            pass_by("bq", "bkv")
            act.wait_ge(stage_over, 1)
            gates("bg", s_gate, ACT.Silu)
            softmax_exp(swa, lambda i, u, t: sinks[:, 2 * i + u:2 * i + u + 1])
            pass_by("cqk", "cv")
            act.wait_ge(stage_over, 2)
            gates("cg", m_gate, ACT.Silu)
            softmax_exp(moba)
            act.wait_ge(stage_over, 3)
            for b in range(3):
                act.activation(y1_hi[:, 8 * b:8 * b + 8, :], y1[:, 8 * b:8 * b + 8, :], ACT.Copy).then_inc(y_hi_ready, 1)
            sec = plan["merge"]
            with act.Fori(0, 4) as j:
                for b in range(3):
                    g, more = sec.first + b * MERGE + AHEAD, j * (3 * MERGE // RING)
                    for c in range(sec.chunks):
                        if c + AHEAD == sec.chunks - 1:
                            new = g - AHEAD + sec.chunks
                            act.wait_ge(lo_ready[new % RING], new // RING + more)
                            act.dma_start(ring[:, new % RING],
                                          I["w_branch"][b * BW:b * BW + CH * P, ds(j * TW, TW)].rearrange(row, p=P))                               .then_inc(w_landed[new % RING], 16)
                        split(g + c, more)
                    act.wait_ge(tile_done[0], sec.tiles[0] + 3 * j + b + 1)
                    act.wait_ge(tile_free[1], sec.tiles[1] + 3 * j + b)
                    for cb in range(4):
                        last = act.activation(sig[:, cb], ps[:, cb // 2, (cb % 2) * S:(cb % 2 + 1) * S], ACT.Sigmoid,
                                              bias=bmc[:, b, ds(4 * j + cb, 1)])
                        if cb == 3:
                            last.then_inc(tile_free[0], 1)
                    for c in range(sec.chunks, MERGE):
                        split(g + c, more)
            act.wait_ge(stage_over, 4)
            load_ln(I["ln_g"], I["ln_b"])
            pass_by("wo")
            ln_roots()

            def hidden_gate(name):
                sec = plan[name]
                for t, u, it in tiles_of(act, sec.n):
                    splits(sec, u, it)
                    if u == 0:
                        act.wait_ge(tile_done[0], sec.tiles[0] + it + 1)
                        act.wait_ge(tile_free[1], sec.tiles[1] + it)
                        act.activation(f_sg[:, 0].rearrange("p a s -> p (a s)"),
                                       ps[:, 0:2, :].rearrange("p a s -> p (a s)"), ACT.Silu).then_inc(tile_free[0], 1)

            take_x()
            pass_by("cval")
            gates("cgate", c_acc, ACT.Sigmoid)
            sec = plan["qkv"]
            before = n.now(vec_ready)
            for t, u, it in tiles_of(act, sec.n):
                splits(sec, u, it)
                act.wait_ge(tile_done[u], sec.tiles[u] + it + 1)
                act.wait_ge(vec_ready, before - 1 + t)
                act.activation(c_raw[:, u, :, RP:RP + S], ps[:, 2 * u:2 * u + 2, :].rearrange("p a (c s) -> p (a c) s", c=2),
                               ACT.Copy).then_inc(tile_free[u], 1)
            sec = plan["z"]
            for u in range(2):
                splits(sec, u, 0)
                act.wait_ge(vec_ready, n.next(vec_ready, 3))
                v = c_qkv[:, 12 * u:12 * u + 12]
                act.activation(v, v, ACT.Silu).then_inc(silu_done, 1)
                act.wait_ge(tile_done[u], sec.tiles[u] + 1)
                act.activation(c_z[:, 4 * u:4 * u + 4, :].rearrange("p a s -> p (a s)"),
                               ps[:, 2 * u:2 * u + 2, :].rearrange("p a s -> p (a s)"), ACT.Silu).then_inc(tile_free[u], 1)
            pass_by("ba")
            act.wait_ge(vec_ready, n.next(vec_ready))
            act.activation(c_sq, c_acc, ACT.Square).then_inc(conv_ready, 1)
            act.wait_ge(vec_ready, n.next(vec_ready))
            act.activation(t_beta, t_ba[:, :, 0:8], ACT.Sigmoid)
            act.activation(t_A, gdnA, ACT.Exp)
            link(act.activation(t_e, t_e, ACT.Exp))
            act.activation(t_e, t_e, ACT.Ln, bias=one).then_inc(act_ready, 1)
            act.wait_ge(mm_ready, n.next(mm_ready, 13))
            act.activation(c_rs, ps[:, 5, 0:S], ACT.Sqrt, bias=eps_ln, scale=1.0 / 1024).then_inc(act_ready, 1)
            act.wait_ge(vec_ready, n.next(vec_ready))
            for t in range(8):
                last = act.activation(y2[:, t], c_acc[:, t], ACT.Silu, bias=colp[:, t, R_CLB:R_CLB + 1],
                                      scale=colp[:, t, R_CLG:R_CLG + 1])
            last.then_inc(act_ready, 1)
            act.wait_ge(act_ready, 12)
            act.activation(l2_sq, c_qkv[:, 0:16], ACT.Square).then_inc(sq_ready, 1)
            roots(l2_rn, 16, 1.0, eps_rms)
            for h in range(GD_H):
                act.wait_ge(vec_ready, n.next(vec_ready))
                act.activation(d_dt[:, h % 2], d_dt[:, h % 2], ACT.Exp).then_inc(act_ready, 1)
            with n.loop(act, 7, {xp_ready: 4}):
                for g in range(4):
                    act.wait_ge(xp_ready, n.next(xp_ready))
                    act.activation(d_xs[:, 4 * g:4 * g + 4].rearrange("p a b -> p (a b)"), ps[:, g, :],
                                   ACT.Copy).then_inc(xs_ready, 1)
            act.wait_ge(vec_ready, n.next(vec_ready))
            act.activation(d_sq, y2[:, 8:16], ACT.Square).then_inc(sq_ready, 1)
            roots(d_rn, GD_H, 1.0 / P, eps_rms)
            load_ln(I["ln1_g_2"], I["ln1_b_2"])
            pass_by("wout2")
            ln_roots()
            take_x()
            load_ln(I["ln2_g_2"], I["ln2_b_2"])
            hidden_gate("gu")
            act.wait_ge(tile_free[1], plan["gu"].tiles[1] + plan["gu"].n // 2)
            prime_hidden("down2")
            pass_by("down2", hidden=True)
            ln_roots()
            take_x()
            load_ln(I["ln1_g_3"], I["ln1_b_3"])
            for r, name in enumerate(("lam_q1_3", "lam_k1_3", "lam_q2_3", "lam_k2_3")):
                act.dma_start(lam_rows[:, r], I[name].to_broadcast([P, 64])).then_inc(lam_landed, 16)
            pass_by("qka", "va", "qi", "kwi")
            softmax_exp(dsa)
            act.wait_ge(stage_over, 6)
            for t, u, it in tiles_of(act, 3):
                splits(plan["qkm"], u, it)
                act.wait_ge(vec_ready, n.next(vec_ready))
                v = e_qk[:, 4 * t:4 * t + 4]
                act.activation(v, v, ACT.Silu).then_inc(silu_done, 1)
            pass_by("vm")
            gates("om", e_gate, ACT.Sigmoid, 384)
            pass_by("if")
            act.wait_ge(vec_ready, n.next(vec_ready))
            link(act.activation(t_ef, t_ef, ACT.Exp))
            act.activation(t_ef, t_ef, ACT.Ln, bias=one).then_inc(act_ready, 1)
            act.wait_ge(vec_ready, n.next(vec_ready))
            softmax_exp(mls, lambda i, u, t: t_na[:, t, 2 * i + u:2 * i + u + 1])
            act.wait_ge(vec_ready, n.next(vec_ready))
            act.activation(e_sq, y3[:, 6:12], ACT.Square).then_inc(sq_ready, 1)
            roots(e_rn, M_H, 1.0 / P, eps_ln)
            act.wait_ge(vec_ready, n.next(vec_ready))
            act.activation(lam[:, 2:4], lam[:, 0:2], ACT.Exp).then_inc(act_ready, 1)
            pass_by("qkc", "vc")
            softmax_exp(dif)
            act.wait_ge(vec_ready, n.next(vec_ready))
            act.activation(e_sq[:, 0:4], e_cut, ACT.Square, scale=SHRINK).then_inc(sq_ready, 1)
            roots(e_rn, D_H, 1.0 / P, eps_diff)
            pass_by("wout3")
            ln_roots()
            take_x()
            load_ln(I["ln2_g_3"], I["ln2_b_3"])
            sec = plan["up3"]
            for t, u, it in tiles_of(act, sec.n):
                splits(sec, u, it)
                act.wait_ge(tile_done[u], sec.tiles[u] + it + 1)
                v = f_sg[:, u].rearrange("p a s -> p (a s)")
                act.activation(v, ps[:, 2 * u:2 * u + 2, :].rearrange("p a s -> p (a s)"), ACT.Relu)\
                   .then_inc(tile_free[u], 1)
                act.wait_ge(tile_free[u], sec.tiles[u] + it + 1)
                act.activation(hid[:, ds(4 * t, 4), :].rearrange("p a s -> p (a s)"), v, ACT.Square)\
                   .then_inc(hid_ready, 1)
            act.wait_ge(hid_ready, sec.n)
            prime_hidden("down3")
            pass_by("down3", hidden=True)
            ln_roots()

        @block.vector
        def _(dve):
            n = Count()

            def link(ins):
                ins.then_inc(dve_order, 1)
                dve.wait_ge(dve_order, n.next(dve_order))

            def tt(o, a, b, op):
                return dve.tensor_tensor(o, a, b, op)

            def tsc(o, a, s1, op0, s2=None, op1=ALU.bypass):
                return dve.tensor_scalar(o, a, s1, s2, op0, op1)

            def stt(o, a, s, b, op0, op1, **kw):
                return dve.scalar_tensor_tensor(o, a, s, b, op0, op1, **kw)

            dve.memset(table[:], 0.0).then_inc(table_zeroed, 1)
            dve.memset(eps_ln, LN_EPS)
            dve.memset(eps_rms, RMS_EPS)
            dve.memset(one, 1.0)
            dve.memset(eps_diff, LN_EPS * SHRINK ** 2)
            for h in range(A_H):
                dve.memset(slopes_a[:, h:h + 1], 2.0 ** (-8.0 * (h + 1) / A_H))
            for h in range(D_H):
                dve.memset(slopes_c[:, h:h + 1], 2.0 ** (-8.0 * (h + 1) / D_H))
            dve.memset(ones[:], 1.0)
            dve.memset(upper[:, P:S], 1.0)
            for m in (causal, causalT):
                dve.memset(m[:, P:S], 0.0)
            dve.wait_ge(iotas, 2)
            pi, pj, px, py = (v.bitcast(I32) for v in (posi, posj, posx, posy))
            tt(ident[:], pi, pj, ALU.is_equal)
            link(tt(upper[:, 0:P], pi, pj, ALU.is_ge))
            for dst, cmp in [(causal[:, 0:P], ALU.is_gt), (causal[:, S:384], ALU.is_gt), (causalT[:, 0:P], ALU.is_lt),
                             (causalT[:, S:384], ALU.is_lt), (band[:, 0:P], ALU.is_gt), (band[:, P:S], ALU.is_le),
                             (band[:, S:384], ALU.is_gt)]:
                link(tt(dst, pi, pj, cmp))
                dve.tensor_scalar(dst, dst, NEG, None, ALU.mult)
            for c in (0, 2):
                tt(ndist[:, c * P:(c + 1) * P], pi, pj, ALU.subtract)
            link(tt(ndist[:, P:S], pi, pj, ALU.subtract))
            link(tsc(ndist[:, P:S], ndist[:, P:S], -float(P), ALU.add))
            link(tt(px, pi, pj, ALU.bitwise_xor))
            for lv in range(7):
                link(tsc(py, px, lv, ALU.logical_shift_right))
                link(tsc(levels[:, lv], py, 1, ALU.is_equal))
                link(tt(levels[:, lv], levels[:, lv], upper[:, 0:P], ALU.mult))
            dve.wait_ge(x_landed, 16)
            dve.sem_inc(consts, 1)

            dve.wait_ge(tableT_ready, 1)
            link(dve.tensor_copy(colp[:].rearrange("p t r -> p (t r)"), ps[:, 0, :]))
            for b in range(3):
                last = dve.tensor_copy(bmc[:, b, :].rearrange("p (a t) -> p a t", a=2),
                                       colp[:, :, R_BM + 2 * b:R_BM + 2 * b + 2].rearrange("p t a -> p a t"))
            last.then_inc(table_ready, 1)

            def split(g, more=0, rows=None):
                s, width = g % RING, TW
                if isinstance(more, int):
                    g, more = g + more * RING, 0
                    if g >= len(widths):
                        return
                    width = widths[g]
                dve.wait_ge(hi_ready[s], g // RING + 1 + more)
                last = tt(w_lo[:, s, :, 0:width], ring[:, s, :, 0:width], w_hi[:, s, :, 0:width].bitcast(F32), ALU.subtract)
                if rows is not None:
                    last = tt(h_lo[:, s], hid[:, rows:rows + CH, :], h_hi[:, s].bitcast(F32), ALU.subtract)
                last.then_inc(lo_ready[s], 1)

            def splits(sec, u, it, hidden=False):
                for c in range(AHEAD, AHEAD + sec.chunks):
                    split(sec.chunk(u, c), sec.more(it), c % sec.chunks * CH if hidden else None)

            def pass_by(*names):
                for name in names:
                    for t, u, it in tiles_of(dve, plan[name].n):
                        splits(plan[name], u, it)

            def prime_hidden(name, times):
                for c in range(AHEAD):
                    s = plan[name].chunk(0, c) % RING
                    dve.wait_ge(h_primed_hi, AHEAD * times + c + 1)
                    tt(h_lo[:, s], hid[:, c * CH:(c + 1) * CH, :], h_hi[:, s].bitcast(F32), ALU.subtract)\
                        .then_inc(h_primed, 1)

            def take_x():
                for g in range(KT // 2):
                    dve.wait_ge(xh_ready, n.next(xh_ready))
                    lo, hi = (v[:, 2 * g:2 * g + 2, :].rearrange("p a s -> p (a s)") for v in (x_lo, x_hi))
                    tt(lo, ps[:, 4 + g % 4, :], hi.bitcast(F32), ALU.subtract).then_inc(xTp_used, 1)

            def split_y(y, a, b):
                link(dve.tensor_copy(y_hi[:, a:b], y[:, a:b]))
                tt(y_lo[:, a:b], y[:, a:b], y_hi[:, a:b].bitcast(F32), ALU.subtract).then_inc(y_part, 1)
                dve.wait_ge(y_part, n.next(y_part))

            def take(name, dst, kind, width=TW):
                sec = plan[name]
                for t, u, it in tiles_of(dve, sec.n):
                    splits(sec, u, it)
                    dve.wait_ge(tile_done[u], sec.tiles[u] + it + 1)
                    if kind == "F":
                        per = width // P
                        dve.tensor_copy(dst[:, ds(t * per, per), :].rearrange("p a s -> p (a s)"),
                                        ps[:, 2 * u:2 * u + 2, :].rearrange("p a s -> p (a s)")[:, 0:per * S])\
                           .then_inc(tile_free[u], 1)
                    else:
                        dve.tensor_copy(dst[:, :, ds(t * width, width)], ps[:, 2 * u:2 * u + 2, 0:width])\
                           .then_inc(tile_free[u], 1)

            def take_narrow(name, m, bank, nar, dst):
                dve.wait_ge(tile_done[0], plan[name].tiles[0] + 1)
                dve.tensor_copy(nar[0:m], ps[0:m, bank, 0:S]).then_inc(narrow_ready, 1)
                dve.wait_ge(narrowT_ready, n.next(narrowT_ready))
                dve.tensor_copy(dst, ps[:, bank, S:S + 2 * m]).then_inc(tile_free[0], 1)
                dve.wait_ge(tile_free[0], plan[name].tiles[0] + 1)

            def wait_gates(name):
                sec = plan[name]
                for u in range(2):
                    dve.wait_ge(tile_free[u], sec.tiles[u] + (sec.n + 1 - u) // 2)

            def over():
                dve.sem_inc(stage_over, 1)

            def attention(A, scale, mask, y, gate=None, slopes=None):
                kind = A.kind

                def lowered(i):
                    e = i % 2
                    for u in range(2):
                        m, sm, lg = nmax[e][:, 2 * u:2 * u + 2], A.sm[e][:, u], ps[:, A.logits(i, u), 0:384]
                        if kind == "mlstm":
                            for c0, w in ((0, P), (P, S)):
                                last = tt(sm[:, c0:c0 + w], e_bbc[:, 2 * i + u, 0:w], causal[:, c0:c0 + w], ALU.add)
                            link(last)
                        else:
                            if slopes is not None:
                                h = 2 * i + u if A.outs == 2 else i
                                link(stt(sm, ndist[:], slopes[:, h:h + 1], mask, ALU.mult, ALU.add))
                            dve.wait_ge(logits_ready, n.next(logits_ready))
                            stt(sm, lg, scale, mask if slopes is None else sm, ALU.mult, ALU.add).then_inc(logits_used, 1)
                            dve.wait_ge(logits_used, n.next(logits_used))
                        dve.tensor_reduce(m[:, 0:1], sm[:, 0:P], AX, ALU.max, negate=True)
                        last = dve.tensor_reduce(m[:, 1:2], sm[:, P:384], AX, ALU.max, negate=True)
                        if kind == "mlstm":
                            link(last)
                            tsc(m, m, 0.0, ALU.min).then_inc(max_ready, 1)
                        elif kind == "swa":
                            link(last)
                            k = esink[e][:, 2 * u:2 * u + 1]
                            link(tsc(k, sinks[:, 2 * i + u:2 * i + u + 1], -1.0, ALU.mult))
                            tsc(m, m, k, ALU.min).then_inc(max_ready, 1)
                        else:
                            last.then_inc(max_ready, 1)

                def weights(i):
                    e = i % 2
                    if kind == "diff":
                        p0, p1, r = A.p[e][:, 0], A.p[e][:, 1], rinv[e]
                        dve.wait_ge(exp_done, n.next(exp_done, 2))
                        link(dve.reciprocal(r, rsum[e]))
                        link(tsc(r[:, 2:4], r[:, 2:4], lam[:, 4:5], ALU.mult))
                        tsc(p0[:, 0:P], p0[:, 0:P], r[:, 0:1], ALU.mult)
                        link(tsc(p0[:, P:384], p0[:, P:384], r[:, 1:2], ALU.mult))
                        stt(p0[:, 0:P], p1[:, 0:P], r[:, 2:3], p0[:, 0:P], ALU.mult, ALU.add)
                        stt(p0[:, P:384], p1[:, P:384], r[:, 3:4], p0[:, P:384], ALU.mult, ALU.add)\
                            .then_inc(probs_ready, 1)
                        return
                    for u in range(2):
                        l, r, p, lg = rsum[e][:, 2 * u:2 * u + 2], rinv[e][:, 2 * u:2 * u + 2], A.p[e][:, u], A.logits(i, u)
                        dve.wait_ge(exp_done, n.next(exp_done))
                        if kind == "swa":
                            link(tt(l, l, esink[e][:, 2 * u:2 * u + 2], ALU.add))
                        if kind == "mlstm":
                            dve.wait_ge(logits_ready, n.next(logits_ready))
                            stt(p[:, 0:P], ps[:, lg, 0:P], scale, p[:, 0:P], ALU.mult, ALU.mult, accum_out=l[:, 0:1])
                            stt(p[:, P:384], ps[:, lg, P:384], scale, p[:, P:384], ALU.mult, ALU.mult,
                                accum_out=l[:, 1:2]).then_inc(logits_used, 1)
                            dve.wait_ge(logits_used, n.next(logits_used))
                            link(stt(l, l, -1.0, l, ALU.mult, ALU.max))
                            link(tt(l, l, esink[e][:, 2 * u:2 * u + 2], ALU.max))
                        link(dve.reciprocal(r, l))
                        tsc(p[:, 0:P], p[:, 0:P], r[:, 0:1], ALU.mult)
                        tsc(p[:, P:384], p[:, P:384], r[:, 1:2], ALU.mult).then_inc(probs_ready, 1)

                def results(i):
                    dve.wait_ge(o_ready, n.next(o_ready))
                    if kind == "swa":
                        last = tt(y[:, i], ps[:, 2, 0:S], gate[:, i], ALU.mult)
                    elif kind == "diff":
                        last = dve.tensor_copy(y[:, i], ps[:, 2, 0:S])
                    elif gate is None:
                        last = dve.tensor_copy(y[:, 2 * i:2 * i + 2, :], ps[:, 2:4, 0:S])
                    else:
                        last = tt(y[:, 2 * i:2 * i + 2, :], ps[:, 2:4, 0:S], gate[:, 2 * i:2 * i + 2, :], ALU.mult)
                    last.then_inc(o_used, 1)

                lowered(0)
                for i in range(A.pairs):
                    if i + 1 < A.pairs:
                        lowered(i + 1)
                    weights(i)
                    if i:
                        results(i - 1)
                results(A.pairs - 1)
                dve.wait_ge(o_used, n.next(o_used, A.pairs))

            def inverse_roots(dst, heads):
                dve.wait_ge(root_ready, n.next(root_ready, heads // 2))
                link(dve.reciprocal(dst, dst))

            def layer_norm(name, hidden=False):
                sec = plan[name]
                for t, u, it in tiles_of(dve, sec.n, True):
                    splits(sec, u, it, hidden)
                    dve.wait_ge(tile_done[u], sec.tiles[u] + it + 1)
                    xv = xtok[:, :, t * TW:(t + 1) * TW]
                    stt(xv, xv, ALPHA, ps[:, 2 * u:2 * u + 2, :], ALU.mult, ALU.add).then_inc(tile_free[u], 1)
                    dve.wait_ge(tile_free[u], sec.tiles[u] + it + 1)
                    dve.bn_stats(stat[:, 32 + 6 * t:38 + 6 * t], xtok[:, 0, t * TW:(t + 1) * TW])
                    last = dve.bn_stats(tokc[:, 6 * t:6 * t + 6], xtok[:, 1, t * TW:(t + 1) * TW])
                link(last)
                dve.bn_aggr(stat[:, 2:4], stat[:, 32:56])
                link(dve.bn_aggr(stat[:, 4:6], tokc[:, 0:24]))
                dve.tensor_copy(stat[:, 26:28], stat[:, 3:6:2]).then_inc(var_ready, 1)
                dve.wait_ge(std_ready, n.next(std_ready))
                link(dve.reciprocal(stat[:, 28:30], stat[:, 28:30]))
                stt(stat[:, 30:32], stat[:, 2:6:2], -1.0, stat[:, 28:30], ALU.mult, ALU.mult).then_inc(norm_ready, 1)
                dve.wait_ge(ln_landed, n.next(ln_landed, 32))
                gb = lambda e, c: ln_gb[:, e:e + 1, c * TW:(c + 1) * TW].to_broadcast([P, 2, TW])
                for c in range(4):
                    xv = xtok[:, :, c * TW:(c + 1) * TW]
                    dve.wait_ge(xn_ready, n.next(xn_ready))
                    if c % 2 == 0:
                        tt(xv, xv, gb(0, c), ALU.mult).then_inc(xg_ready, 1)
                    else:
                        link(tt(xv, xv, gb(0, c), ALU.mult))
                        tt(xv, xv, gb(1, c), ALU.add).then_inc(x_odd, 1)

            for g in range(AHEAD):
                split(g)
            take_x()
            take("aqk", a_qk, "F")
            take("av", a_v, "T")
            pass_by("alr")
            dve.wait_ge(tile_done[0], plan["alr"].tiles[0] + 1)
            link(dve.tensor_copy(alrT, ps[0:G_RANK, 0, 0:S]))
            dve.sem_inc(tile_free[0], 1)
            dve.sem_inc(vec_ready, 1)
            pass_by("ag")
            dve.wait_ge(mm_ready, n.next(mm_ready))
            for h in range(G_H):
                tsc(a_b[:, h], ps[:, 4 + h // 2, (h % 2) * S:(h % 2 + 1) * S], colp[:, h, R_GLAB:R_GLAB + 1], ALU.add)\
                    .then_inc(dve_order, 1)
            dve.wait_ge(dve_order, n.next(dve_order, G_H))
            stt(a_e[:, 0], a_b, -1.0, a_b, ALU.mult, ALU.min).then_inc(vec_ready, 1)
            link(tsc(a_b, a_b, 0.0, ALU.min))
            dve.wait_ge(act_ready, n.next(act_ready))
            link(tt(a_b, a_b, a_e[:, 0], ALU.subtract))
            link(tsc(a_e[:, 1], a_b, 1.0 / G_TAU, ALU.mult))
            for h in range(G_H):
                last = dve.tensor_tensor_scan(a_b[:, h], ones[:, 0:1].to_broadcast([P, S]), a_e[:, 1, h], 0.0, ALU.mult, ALU.add)
            link(last)
            link(dve.memset(a_at, 0.0))
            QS = float(P) ** -0.5
            q4, k4 = a_qk[:, 0:4], a_qk[:, 4:8]

            def level_factors(lv):
                half = 1 << lv
                bv = a_b.rearrange("p h (c w) -> p (h c) w", w=2 * half)
                mid = bv[:, :, half - 1:half].to_broadcast([P, 4 * S // (2 * half), 2 * half])
                e = a_e[:, lv % 2]
                link(tt(e.rearrange("p h (c w) -> p (h c) w", w=2 * half), bv, mid, ALU.subtract))
                stt(e, e, -1.0, e, ALU.mult, ALU.min).then_inc(vec_ready, 1)

            def merge_level(lv):
                dve.wait_ge(mm_ready, n.next(mm_ready))
                b = 4 + 2 * (lv % 2)
                if lv == 7:
                    dve.tensor_copy(a_at[:, :, P:S], ps[:, b, :].rearrange("p (h s) -> p h s", h=4)).then_inc(mm_used, 1)
                    return
                m = ident[:] if lv == 8 else levels[:, lv]
                b = 4 if lv == 8 else b
                for g in range(2):
                    for c in range(2):
                        o = a_at[:, 2 * g:2 * g + 2, c * S:c * S + P]
                        d = ps[:, b + g, :].rearrange("p (h s) -> p h s", h=2)[:, :, c * P:(c + 1) * P]
                        mk = m.unsqueeze(1).to_broadcast([P, 2, P]).bitcast(I32)
                        last = dve.copy_predicated(o, mk, d)
                last.then_inc(mm_used, 1)

            level_factors(0)
            for lv in range(8):
                if lv < 7:
                    level_factors(lv + 1)
                dve.wait_ge(act_ready, n.next(act_ready))
                stt(a_qe[:, lv % 2], q4, QS, a_e[:, lv % 2], ALU.mult, ALU.mult)
                link(tt(a_ke[:, lv % 2], k4, a_e[:, lv % 2], ALU.mult))
                dve.sem_inc(fac_ready, 1)
                if lv >= 1:
                    merge_level(lv - 1)
            merge_level(7)
            link(tsc(a_qe[:, 0], q4, QS, ALU.mult))
            dve.sem_inc(fac_ready, 1)
            merge_level(8)
            dve.wait_ge(mm_ready, n.next(mm_ready))
            link(dve.tensor_copy(y1[:, 0:8, :].rearrange("p a s -> p (a s)"), ps[:, 4:8, :].rearrange("p a s -> p (a s)")))
            dve.sem_inc(vec_ready, 1)
            wait_gates("ag")
            dve.wait_ge(sq_ready, n.next(sq_ready))
            for e in range(2):
                ya = y1[:, 0:8].rearrange("p (h e) s -> p h e s", e=2)[:, :, e, :]
                ga = a_gate.rearrange("p (h e) s -> p h e s", e=2)[:, :, e, :]
                stt(ya, ya, colp[:, e, R_GLAG:R_GLAG + 1], ga, ALU.mult, ALU.mult).then_inc(dve_order, 1)
            dve.wait_ge(dve_order, n.next(dve_order, 2))
            inverse_roots(a_rn, G_H)
            for e in range(2):
                ya = y1[:, 0:8].rearrange("p (h e) s -> p h e s", e=2)[:, :, e, :]
                last = tt(ya, ya, a_rn, ALU.mult)
            link(last)
            over()
            take("bq", s_q, "F")
            pass_by("bkv")
            dve.wait_ge(tile_done[0], plan["bkv"].tiles[0] + 1)
            dve.tensor_copy(s_kd[:].rearrange("p a s -> p (a s)"), ps[:, 0, :])
            dve.tensor_copy(s_v[:].rearrange("p a s -> p (a s)"), ps[:, 1, 0:S]).then_inc(tile_free[0], 1)
            pass_by("bg")
            wait_gates("bg")
            dve.sem_inc(gate_ready, 1)
            attention(swa, 64.0 ** -0.5, band[:], y1[:, 8:16], s_gate)
            over()
            take("cqk", m_qk, "F")
            take("cv", m_v, "T")
            pass_by("cg")
            wait_gates("cg")
            dve.sem_inc(gate_ready, 1)
            attention(moba, float(P) ** -0.5, causal[:], y1[:, 16:24], m_gate)
            over()
            for b in range(3):
                dve.wait_ge(y_hi_ready, b + 1)
                y = y1[:, 8 * b:8 * b + 8, :]
                tt(y1_lo[:, 8 * b:8 * b + 8, :], y, y1_hi[:, 8 * b:8 * b + 8, :].bitcast(F32), ALU.subtract)\
                    .then_inc(y_split, 1)
            sec = plan["merge"]
            with n.loop(dve, 4, {dve_order: 4}) as j:
                for b in range(3):
                    for c in range(MERGE):
                        split(sec.first + b * MERGE + c + AHEAD, j * (3 * MERGE // RING))
                    dve.wait_ge(tile_done[1], sec.tiles[1] + 3 * j + b + 1)
                    dve.wait_ge(tile_free[0], sec.tiles[0] + 3 * j + b + 1)
                    up = ps[:, 2:4, :].rearrange("p a s -> p (a s)")
                    sg = sig.rearrange("p a s -> p (a s)")
                    mt = mtmp.rearrange("p a s -> p (a s)")
                    md = mergedT[:, ds(4 * j, 4), :].rearrange("p a s -> p (a s)")
                    tt(md if b == 0 else mt, sg, up, ALU.mult).then_inc(tile_free[1], 1)
                    dve.wait_ge(tile_free[1], sec.tiles[1] + 3 * j + b + 1)
                    if b:
                        link(tt(md, md, mt, ALU.add))
                hi, lo = (v[:, ds(4 * j, 4), :].rearrange("p a s -> p (a s)") for v in (m_hi, m_lo))
                link(dve.tensor_copy(hi, md))
                link(tt(lo, md, hi.bitcast(F32), ALU.subtract))
            over()
            layer_norm("wo")

            def hidden_up(name):
                sec = plan[name]
                for t, u, it in tiles_of(dve, sec.n):
                    splits(sec, u, it)
                    if u == 1:
                        dve.wait_ge(tile_done[1], sec.tiles[1] + it + 1)
                        dve.wait_ge(tile_free[0], sec.tiles[0] + it + 1)
                        tt(hid[:, ds(4 * it, 4), :].rearrange("p a s -> p (a s)"), f_sg[:, 0].rearrange("p a s -> p (a s)"),
                           ps[:, 2:4, :].rearrange("p a s -> p (a s)"), ALU.mult).then_inc(tile_free[1], 1)

            take_x()
            for k in range(SHORT_W):
                link(dve.tensor_copy(scw[:, k, :].rearrange("p (a t) -> p a t", a=3),
                                     colp[:, :, R_SCW + 3 * k:R_SCW + 3 * k + 3].rearrange("p t a -> p a t")))
            dve.memset(c_h[:, :, 0:HP], 0.0)
            dve.memset(c_raw[:, :, :, 0:RP], 0.0)
            sec = plan["cval"]
            for t, u, it in tiles_of(dve, sec.n):
                splits(sec, u, it)
                dve.wait_ge(tile_done[u], sec.tiles[u] + it + 1)
                dve.tensor_copy(c_h[:, 4 * t:4 * t + 4, HP:HP + S],
                                ps[:, 2 * u:2 * u + 2, :].rearrange("p a (c s) -> p (a c) s", c=2))\
                   .then_inc(tile_free[u], 1)
            pass_by("cgate")
            wait_gates("cgate")
            link(tt(c_h[:, :, HP:HP + S], c_h[:, :, HP:HP + S], c_acc, ALU.mult))

            def wide_conv(t):
                before = n.now(dve_order, 2 * CONV_W)
                for k in range(CONV_W):
                    for e in range(2):
                        acc = c_acc[:, ds(t + e, 1), :].rearrange("p a s -> p (a s)")
                        win = c_h[:, ds(t + e, 1), k:k + S].rearrange("p a s -> p (a s)")
                        tap, bias = (colp[:, ds(t + e, 1), r:r + 1].rearrange("p a s -> p (a s)")
                                     for r in (R_DWW + k, R_DWB))
                        if k == 0:
                            last = tsc(acc, win, tap, ALU.mult, bias, ALU.add)
                        else:
                            dve.wait_ge(dve_order, before + 2 * (k - 1) + e + 1)
                            last = stt(acc, win, tap, acc, ALU.mult, ALU.add)
                        last.then_inc(dve_order, 1)
                dve.wait_ge(dve_order, before + 2 * CONV_W)

            sec = plan["qkv"]
            with n.loop(dve, sec.n // 2, {dve_order: 2 * (CONV_W + 3)}) as i:
                for u in range(2):
                    t = 2 * i + u
                    dve.wait_ge(tile_free[u], sec.tiles[u] + i + 1)
                    for k in range(SHORT_W):
                        for c in range(4):
                            o = c_qkv[:, ds(4 * t + c, 1), :].rearrange("p a s -> p (a s)")
                            r = c_raw[:, u, c, k:k + S]
                            wk = scw[:, k, ds(4 * t + c, 1)]
                            last = tsc(o, r, wk, ALU.mult) if k == 0 else stt(o, r, wk, o, ALU.mult, ALU.add)
                        if k < SHORT_W - 1:
                            link(last)
                        else:
                            last.then_inc(vec_ready, 1)
                wide_conv(2 * i)
            wide_conv(6)
            dve.sem_inc(conv_ready, 1)
            dve.wait_ge(mm_ready, n.next(mm_ready))
            link(tsc(c_mu, ps[:, 4, 0:S], 1.0 / 1024, ALU.mult))
            tt(c_acc, c_acc, c_mu.unsqueeze(1).to_broadcast([P, 8, S]), ALU.subtract).then_inc(vec_ready, 1)
            take_narrow("ba", 16, 0, nar_ba, t_ba.rearrange("p t c -> p (t c)"))
            link(tt(t_x, t_ba[:, :, 8:16], gdndt.unsqueeze(1).to_broadcast([P, 2, 8]), ALU.add))
            stt(t_e, t_x, -1.0, t_x, ALU.mult, ALU.min).then_inc(vec_ready, 1)
            dve.wait_ge(act_ready, n.next(act_ready))
            link(stt(t_x, t_x, 0.0, t_e, ALU.max, ALU.add))
            link(stt(t_g, t_x, -1.0, t_A.unsqueeze(1).to_broadcast([P, 2, 8]), ALU.mult, ALU.mult))
            dve.wait_ge(act_ready, n.next(act_ready))
            link(dve.reciprocal(c_rs, c_rs))
            dve.wait_ge(mm_ready, n.next(mm_ready))
            tt(c_acc, c_acc, c_rs.unsqueeze(1).to_broadcast([P, 8, S]), ALU.mult).then_inc(vec_ready, 1)
            dve.wait_ge(act_ready, n.next(act_ready))
            for g in range(8):
                dve.wait_ge(root_ready, n.next(root_ready))
                rn, v = l2_rn[:, 2 * g:2 * g + 2], c_qkv[:, 2 * g:2 * g + 2]
                link(dve.reciprocal(rn, rn))
                last = stt(v, v, float(P) ** -0.5 if g < 4 else 1.0, rn, ALU.mult, ALU.mult)
            link(last)
            dve.sem_inc(fac_ready, 1)
            dve.wait_ge(mm_ready, n.next(mm_ready))
            dve.tensor_copy(t_gc.rearrange("p t c -> p (t c)"), ps[:, 0, 0:16])
            for t in range(2):
                last = tt(d_vb[:, t].rearrange("p (h c) -> p h c", h=8),
                          ps[:, 4 + 2 * t:6 + 2 * t, :].rearrange("p a (h c) -> p (a h) c", h=4),
                          t_beta[:, t].unsqueeze(2).to_broadcast([P, 8, P]), ALU.mult)
            link(last)
            dve.sem_inc(fac_ready, 1)
            for h in range(GD_H):
                b, dt, db = 2 + 3 * (h % 2), d_dt[:, h % 2], d_db[:, h % 2]
                dve.wait_ge(mm_ready, n.next(mm_ready))
                stt(dt[:, 0:S], ps[:, b, 0:S], t_gc[:, 0, h:h + 1], causalT[:, 0:S], ALU.subtract, ALU.add)
                stt(dt[:, S:384], ps[:, b, P:S], t_gc[:, 1, h:h + 1], causalT[:, S:384], ALU.subtract, ALU.add)\
                    .then_inc(vec_ready, 1)
                dve.wait_ge(act_ready, n.next(act_ready))
                tt(d_at[:, h], ps[:, b + 2, 0:384], dt, ALU.mult)
                tt(db[:, 0:S], dt[:, 0:S], ps[:, b, S:512], ALU.mult)
                link(tt(db[:, S:384], dt[:, S:384], ps[:, b, S + P:512], ALU.mult))
                tt(d_lt[:, 2 * h:2 * h + 2], ps[:, b + 1, 0:384].rearrange("p (a c) -> p a c", a=3)[:, 0:3:2],
                   db.rearrange("p (a c) -> p a c", a=3)[:, 0:3:2], ALU.mult)
                tt(d_l21[:, h], ps[:, b + 1, P:S], db[:, P:S], ALU.mult).then_inc(fac_ready, 1)
                dve.wait_ge(fac_ready, n.next(fac_ready, 12 if h == 0 else 1))
            for g in range(4):
                for m in (d_t, d_tt):
                    last = dve.tensor_copy(m[:, 4 * g:4 * g + 4], ident[:].unsqueeze(1).to_broadcast([P, 4, P]))
                last.then_inc(inv_ready, 1)
            dve.wait_ge(inv_ready, n.next(inv_ready, 4))
            with n.loop(dve, 7, {yp_ready: 4, inv_ready: 4}) as lv:
                for g in range(4):
                    mk = levels[:, ds(lv, 1), :].to_broadcast([P, 4, P])
                    tt(d_lm[:, 4 * g:4 * g + 4], d_lt[:, 4 * g:4 * g + 4], mk, ALU.mult).then_inc(lm_ready, 1)
                for g in range(4):
                    dve.wait_ge(yp_ready, n.next(yp_ready))
                    for m, b in ((d_t, 4), (d_tt, 6)):
                        v = m[:, 4 * g:4 * g + 4].rearrange("p a b -> p (a b)")
                        last = tt(v, v, ps[:, b + g % 2, :], ALU.subtract)
                    last.then_inc(inv_ready, 1)
                    dve.wait_ge(inv_ready, n.next(inv_ready))
            flat = lambda b: ps[:, b:b + 2, :].rearrange("p a s -> p (a s)")
            dve.wait_ge(mm_ready, n.next(mm_ready))
            dve.tensor_copy(d_vn[:, 0], flat(0)).then_inc(fac_ready, 1)
            dve.wait_ge(mm_ready, n.next(mm_ready))
            tt(d_vb[:, 1], d_vb[:, 1], flat(2), ALU.subtract).then_inc(fac_ready, 1)
            dve.wait_ge(mm_ready, n.next(mm_ready))
            dve.tensor_copy(d_vn[:, 1], flat(0)).then_inc(fac_ready, 1)
            dve.wait_ge(mm_ready, n.next(mm_ready))
            dve.tensor_copy(y2[:, 8:16].rearrange("p a s -> p (a s)"), ps[:, 4:8, :].rearrange("p a s -> p (a s)"))\
               .then_inc(vec_ready, 1)
            split_y(y2, 0, 8)
            wait_gates("z")
            dve.wait_ge(sq_ready, 3)
            link(stt(y2[:, 8:16], y2[:, 8:16], colp[:, T_GDNW, R_GLAG:R_GLAG + 1], c_z, ALU.mult, ALU.mult))
            for g in range(GD_H // 2):
                dve.wait_ge(root_ready, n.next(root_ready))
                rn, v = d_rn[:, 2 * g:2 * g + 2], y2[:, 8 + 2 * g:10 + 2 * g]
                link(dve.reciprocal(rn, rn))
                link(tt(v, v, rn, ALU.mult))
                split_y(y2, 8 + 2 * g, 10 + 2 * g)
            over()
            layer_norm("wout2")
            take_x()
            hidden_up("gu")
            prime_hidden("down2", 0)
            layer_norm("down2", hidden=True)
            take_x()
            for k in range(SHORT_W):
                last = dve.tensor_copy(mcw[:, k, :].rearrange("p (a t) -> p a t", a=2),
                                       colp[:, 0:6, R_CM + 2 * k:R_CM + 2 * k + 2].rearrange("p t a -> p a t"))
            link(last)
            take("qka", e_qk, "F")
            take("va", e_v, "T", 384)
            take("qi", i_q, "F")
            pass_by("kwi")
            dve.wait_ge(tile_done[0], plan["kwi"].tiles[0] + 1)
            dve.tensor_copy(i_k, ps[:, 0, 0:S])
            take_narrow("kwi", 8, 1, nar_kwi, t_w.rearrange("p t c -> p (t c)"))
            dve.sem_inc(fac_ready, 1)
            dve.sem_inc(gate_ready, 1)
            for h in range(8):
                dve.wait_ge(mm_ready, n.next(mm_ready))
                o = i_work if h == 0 else i_tmp
                tsc(o[:, 0:P], ps[:, 4 + h % 4, 0:P], 0.0, ALU.max, t_w[:, 0, h:h + 1], ALU.mult)
                tsc(o[:, P:384], ps[:, 4 + h % 4, P:384], 0.0, ALU.max, t_w[:, 1, h:h + 1], ALU.mult)\
                    .then_inc(mm_used, 1)
                dve.wait_ge(mm_used, n.next(mm_used, 10 if h == 0 else 1))
                if h:
                    link(tt(i_work, i_work, i_tmp, ALU.add))
            link(tt(i_work, i_work, causal[:], ALU.add))
            for _ in range(TOPK // 8):
                dve.max(top8[:, 0], i_work[:, 0:P])
                link(dve.max(top8[:, 1], i_work[:, P:384]))
                dve.match_replace(i_work[:, 0:P], top8[:, 0], i_work[:, 0:P], TAKEN)
                link(dve.match_replace(i_work[:, P:384], top8[:, 1], i_work[:, P:384], TAKEN))
            link(tsc(i_sel, i_work, TAKEN / 2, ALU.is_gt, NEG, ALU.mult))
            link(tt(i_sel, i_sel, causal[:], ALU.add))
            attention(dsa, float(P) ** -0.5, i_sel, y3[:, 0:6], slopes=slopes_a)
            over()
            dve.memset(e_raw[:, :, :, 0:RP], 0.0)
            sec = plan["qkm"]
            for t, u, it in tiles_of(dve, 3):
                splits(sec, u, it)
                dve.wait_ge(tile_done[u], sec.tiles[u] + t // 2 + 1)
                dve.tensor_copy(e_raw[:, u, :, RP:RP + S],
                                ps[:, 2 * u:2 * u + 2, :].rearrange("p a (c s) -> p (a c) s", c=2))\
                   .then_inc(tile_free[u], 1)
                dve.wait_ge(tile_free[u], sec.tiles[u] + t // 2 + 1)
                for k in range(SHORT_W):
                    for c in range(4):
                        o, r, wk = e_qk[:, 4 * t + c], e_raw[:, u, c, k:k + S], mcw[:, k, 4 * t + c:4 * t + c + 1]
                        last = tsc(o, r, wk, ALU.mult) if k == 0 else stt(o, r, wk, o, ALU.mult, ALU.add)
                    if k < SHORT_W - 1:
                        link(last)
                    else:
                        last.then_inc(vec_ready, 1)
            take("vm", e_v, "T", 384)
            pass_by("om", "if")
            take_narrow("if", 12, 0, nar_if, t_if.rearrange("p t c -> p (t c)"))
            tt(t_if[:, :, 0:6], t_if[:, :, 0:6], bib.unsqueeze(1).to_broadcast([P, 2, 6]), ALU.add)
            link(tt(t_lf, t_if[:, :, 6:12], bfb.unsqueeze(1).to_broadcast([P, 2, 6]), ALU.add))
            stt(t_ef, t_lf, -1.0, t_lf, ALU.mult, ALU.min).then_inc(vec_ready, 1)
            dve.wait_ge(act_ready, 21)
            link(stt(t_lf, t_lf, 0.0, t_ef, ALU.min, ALU.subtract))
            link(tsc(t_ef, t_lf, -1.0, ALU.mult))
            dve.sem_inc(fac_ready, 1)
            dve.wait_ge(mm_ready, n.next(mm_ready))
            tsc(t_na.rearrange("p t c -> p (t c)"), ps[:, 0, 0:12], -1.0, ALU.mult).then_inc(vec_ready, 1)
            dve.wait_ge(mm_ready, n.next(mm_ready))
            dve.tensor_copy(e_bbc.rearrange("p a s -> p (a s)"),
                            ps[:, 4:7, :].rearrange("p a s -> p (a s)")).then_inc(mm_used, 1)
            dve.wait_ge(mm_used, n.next(mm_used))
            dve.wait_ge(silu_done, 5)
            dve.sem_inc(gate_ready, 1)
            attention(mls, float(P) ** -0.5, None, y3[:, 6:12])
            dve.sem_inc(vec_ready, 1)
            wait_gates("om")
            dve.wait_ge(sq_ready, 4)
            for h in range(M_H):
                last = stt(y3[:, 6 + h], y3[:, 6 + h], colp[:, h, R_MNG:R_MNG + 1], e_gate[:, h], ALU.mult, ALU.mult)
            link(last)
            inverse_roots(e_rn, M_H)
            link(tt(y3[:, 6:12], y3[:, 6:12], e_rn, ALU.mult))
            over()
            dve.wait_ge(lam_landed, 64)
            tt(lam_prod[:, 0], lam_rows[:, 0], lam_rows[:, 1], ALU.mult)
            link(tt(lam_prod[:, 1], lam_rows[:, 2], lam_rows[:, 3], ALU.mult))
            dve.tensor_reduce(lam[:, 0:2], lam_prod, AX, ALU.add).then_inc(vec_ready, 1)
            take("qkc", e_qk, "F")
            take("vc", e_v[:, :, 0:512], "T")
            LAM0 = 0.8 - 0.6 * math.exp(0.0)
            dve.wait_ge(act_ready, 22)
            link(tt(lam[:, 4:5], lam[:, 3:4], lam[:, 2:3], ALU.subtract))
            link(tsc(lam[:, 4:5], lam[:, 4:5], -LAM0, ALU.add))
            dve.sem_inc(gate_ready, 1)
            attention(dif, 64.0 ** -0.5, causal[:], y3[:, 12:16], slopes=slopes_c)
            tsc(e_cut, y3[:, 12:16], LARGE, ALU.min, -LARGE, ALU.max).then_inc(vec_ready, 1)
            split_y(y3, 0, A_H + M_H)
            dve.wait_ge(root_ready, n.next(root_ready, D_H // 2))
            rn = e_rn[:, 0:4]
            link(tsc(e_fits, rn, ROOT_MAX, ALU.is_lt, SHRINK, ALU.mult))
            link(dve.reciprocal(rn, rn))
            link(tt(rn, rn, e_fits, ALU.mult))
            link(tt(y3[:, 12:16], y3[:, 12:16], rn, ALU.mult))
            for h in range(D_H):
                last = tsc(y3[:, 12 + h], y3[:, 12 + h], colp[:, h, R_CNG:R_CNG + 1], ALU.mult, 1.0 - LAM0, ALU.mult)
            link(last)
            split_y(y3, A_H + M_H, KT)
            over()
            layer_norm("wout3")
            take_x()
            pass_by("up3")
            prime_hidden("down3", 1)
            layer_norm("down3", hidden=True)


_INS = [
    "x", "w_in", "gla_w_up", "gla_b", "gla_norm_g", "swa_sinks", "b_merge", "w_branch", "w_o", "ln_g", "ln_b", "w_in_2",
    "conv_dw_w_2", "conv_dw_b_2", "conv_ln_g_2", "conv_ln_b_2", "gdn_conv_w_2", "gdn_A_log_2",
    "gdn_dt_bias_2", "gdn_norm_w_2", "w_out_2", "ln1_g_2", "ln1_b_2", "w_gate_up_2", "w_down_2", "ln2_g_2",
    "ln2_b_2", "w_in_3", "conv_m_3", "b_i_3", "b_f_3", "m_norm_g_3", "lam_q1_3", "lam_k1_3", "lam_q2_3", "lam_k2_3",
    "c_norm_g_3", "w_out_3", "ln1_g_3", "ln1_b_3", "w_up_3", "w_down_3", "ln2_g_3", "ln2_b_3",
]


def _flat(name, a):
    if name == "w_branch":
        return a.reshape(-1, a.shape[-1])
    if name == "x":
        return a.reshape(a.shape[1:])
    return a.reshape(-1, a.shape[-1])


def kernel(**inputs):
    import concourse.bacc as _bacc
    from concourse.bass_utils import run_bass_kernel_spmd as _run

    nc = _bacc.Bacc("TRN2", target_bir_lowering=False, num_devices=1)
    arrays, aps = {}, {}
    for name in _INS:
        a = np.ascontiguousarray(_flat(name, np.asarray(inputs[name])))
        arrays[f"in_{name}"] = a
        aps[name] = nc.dram_tensor(f"in_{name}", a.shape, mybir.dt.from_np(a.dtype), kind="ExternalInput").ap()
    out = nc.dram_tensor("out", (S, D), F32, kind="ExternalOutput").ap()
    build(nc, aps, out)
    r = _run(nc, [arrays], core_ids=[0])
    return r.results[0]["out"].reshape(1, S, D)
```
